# Optimizing a Trainium2 kernel written in Bass

```python
import jax
import jax.numpy as jnp
from jax import lax
import numpy as np

D_MODEL = 1024
BATCH = 1
SEQ = 128
DEPTH = 2
DEC_BATCH = 1
DEC_SEQ = 512
PAST_LEN = 128

GRID_W = 64
HEAD_DIM = 64
NA_HEADS = 6
NA_KH_MAX = 8
NA_KW = 16
NA_QB = 16
NA_KB = 32
RW_HEADS = 4
RW_DECAY_LORA = 64
RW_A_LORA = 64
RW_GATE_LORA = 128
SWA_HEADS = 6
SWA_KV_HEADS = 2
SWA_WINDOW = 128
SWA_BLOCK = 128
N_EXPERTS = 16
EC_CAPACITY = 2
D_FF = 1024
ROPE_THETA = 10000.0
NORM_EPS = 1e-6
GN_EPS = 64e-5
NEG_INF = -1e30

NA_W = NA_HEADS * HEAD_DIM
RW_W = RW_HEADS * HEAD_DIM
SWA_W = SWA_HEADS * HEAD_DIM
SWA_KV_W = SWA_KV_HEADS * HEAD_DIM
MIX_W = NA_W + RW_W + SWA_W
RW_IN_W = 3 * RW_W + 2 * RW_DECAY_LORA + 2 * RW_A_LORA + RW_GATE_LORA
IN_W = 3 * NA_W + RW_IN_W + SWA_W + 2 * SWA_KV_W
IN_SPLITS = [NA_W, 2 * NA_W, 3 * NA_W, 3 * NA_W + RW_IN_W, 3 * NA_W + RW_IN_W + SWA_W, 3 * NA_W + RW_IN_W + SWA_W + SWA_KV_W]
RW_SPLITS = [RW_W, 2 * RW_W, 3 * RW_W, 3 * RW_W + 2 * RW_DECAY_LORA, 3 * RW_W + 2 * RW_DECAY_LORA + 2 * RW_A_LORA]
F32 = jnp.float32

kernel_name = 'hybrid_na_rwkv7_swa_ec_diffusion_step'

def rms_norm(x, g):
    xf = x.astype(F32)
    y = xf * lax.rsqrt(jnp.mean(xf * xf, axis=-1, keepdims=True) + NORM_EPS)
    return (y * g).astype(x.dtype)

def adaln(cond, w, b):
    m = jax.nn.silu(cond) @ w + b
    return [z[:, None, :] for z in jnp.split(m, 6, axis=-1)]

def split_heads(z, n_heads):
    b, l, _ = z.shape
    return z.reshape(b, l, n_heads, HEAD_DIM).transpose(0, 2, 1, 3)

def merge_heads(z):
    b, h, l, d = z.shape
    return z.transpose(0, 2, 1, 3).reshape(b, l, h * d)

def axial_rope(x):
    n = x.shape[2]
    t = jnp.arange(n)
    n_freq = HEAD_DIM // 4
    inv = ROPE_THETA ** (-jnp.arange(n_freq, dtype=F32) / n_freq)
    ang = jnp.concatenate([(t // GRID_W).astype(F32)[:, None] * inv, (t % GRID_W).astype(F32)[:, None] * inv], axis=-1)
    cos, sin = jnp.cos(ang), jnp.sin(ang)
    xf = x.astype(F32)
    x1, x2 = xf[..., :HEAD_DIM // 2], xf[..., HEAD_DIM // 2:]
    return jnp.concatenate([x1 * cos - x2 * sin, x1 * sin + x2 * cos], axis=-1).astype(x.dtype)

def project(h, p):
    u = h @ p['w_in']
    qa, ka, va, u_rw, qc, kc, vc = jnp.split(u, IN_SPLITS, axis=-1)
    qa = rms_norm(split_heads(qa, NA_HEADS), p['na_q_norm'])
    ka = rms_norm(split_heads(ka, NA_HEADS), p['na_k_norm'])
    va = split_heads(va, NA_HEADS)
    qc = rms_norm(split_heads(qc, SWA_HEADS), p['swa_q_norm'])
    kc = rms_norm(split_heads(kc, SWA_KV_HEADS), p['swa_k_norm'])
    vc = split_heads(vc, SWA_KV_HEADS)
    return qa, ka, va, u_rw, qc, kc, vc

def dense_attention(q, k, v, sink):
    b, hq, l, d = q.shape
    hkv = k.shape[1]
    g = hq // hkv
    qg = q.reshape(b, hkv, g, l, d)
    s = jnp.einsum('bhgqd,bhkd->bhgqk', qg, k).astype(F32) * HEAD_DIM ** -0.5
    if sink is None:
        pr = jax.nn.softmax(s, axis=-1)
    else:
        sk = jnp.broadcast_to(sink.astype(F32).reshape(1, hkv, g, 1, 1), s.shape[:-1] + (1,))
        pr = jax.nn.softmax(jnp.concatenate([s, sk], axis=-1), axis=-1)[..., :-1]
    o = jnp.einsum('bhgqk,bhkd->bhgqd', pr.astype(v.dtype), v)
    return o.reshape(b, hq, l, d)

def neighbourhood_attention(q, k, v, k_ctx, v_ctx, rpb):
    b, h, n, d = q.shape
    rows = n // GRID_W
    kh = min(NA_KH_MAX, rows)
    nqb = GRID_W // NA_QB
    scale = HEAD_DIM ** -0.5
    r = jnp.arange(rows)
    row_idx = jnp.clip(r - kh // 2, 0, rows - kh)[:, None] + jnp.arange(kh)
    j = jnp.arange(nqb)
    col_idx = jnp.clip(j * NA_QB - NA_KW // 2, 0, GRID_W - NA_KB)[:, None] + jnp.arange(NA_KB)
    q_col = j[:, None] * NA_QB + jnp.arange(NA_QB)
    c_start = jnp.clip(q_col - NA_KW // 2, 0, GRID_W - NA_KW)
    col_ok = (col_idx[:, None, :] >= c_start[..., None]) & (col_idx[:, None, :] < c_start[..., None] + NA_KW)
    flat = row_idx[:, None, :, None] * GRID_W + col_idx[None, :, None, :]
    kg = k[:, :, flat]
    vg = v[:, :, flat]
    qb = q.reshape(b, h, rows, nqb, NA_QB, d)
    s_win = jnp.einsum('bhrjqd,bhrjkcd->bhrjqkc', qb, kg).astype(F32) * scale
    d_row = row_idx - r[:, None] + NA_KH_MAX - 1
    d_col = jnp.clip(col_idx[:, None, :] - q_col[..., None], 1 - NA_KW, NA_KW - 1) + NA_KW - 1
    bias = rpb[:, d_row[:, None, None, :, None], d_col[None, :, :, None, :]].astype(F32)
    s_win = jnp.where(col_ok[:, :, None, :], s_win + bias, NEG_INF)
    s_win = s_win.reshape(b, h, rows, nqb, NA_QB, kh * NA_KB)
    s_ctx = jnp.einsum('bhnd,bhld->bhnl', q, k_ctx).astype(F32) * scale
    s_ctx = s_ctx.reshape(b, h, rows, nqb, NA_QB, -1)
    pr = jax.nn.softmax(jnp.concatenate([s_win, s_ctx], axis=-1), axis=-1).astype(v.dtype)
    p_win = pr[..., :kh * NA_KB].reshape(b, h, rows, nqb, NA_QB, kh, NA_KB)
    p_ctx = pr[..., kh * NA_KB:]
    o = jnp.einsum('bhrjqkc,bhrjkcd->bhrjqd', p_win, vg) + jnp.einsum('bhrjql,bhld->bhrjqd', p_ctx, v_ctx)
    return o.reshape(b, h, n, d)

def window_attention(q, k, v, k_ctx, v_ctx, sink):
    b, hq, n, d = q.shape
    hkv = k.shape[1]
    g = hq // hkv
    nb = n // SWA_BLOCK
    scale = HEAD_DIM ** -0.5
    qb = q.reshape(b, hkv, g, nb, SWA_BLOCK, d)
    pad = ((0, 0), (0, 0), (SWA_BLOCK, SWA_BLOCK), (0, 0))
    idx = jnp.arange(nb)[:, None] * SWA_BLOCK + jnp.arange(3 * SWA_BLOCK)
    kg = jnp.pad(k, pad)[:, :, idx]
    vg = jnp.pad(v, pad)[:, :, idx]
    q_pos = jnp.arange(nb)[:, None] * SWA_BLOCK + jnp.arange(SWA_BLOCK)
    k_pos = idx - SWA_BLOCK
    ok = (jnp.abs(q_pos[:, :, None] - k_pos[:, None, :]) <= SWA_WINDOW) & (k_pos >= 0)[:, None, :] & (k_pos < n)[:, None, :]
    s_win = jnp.einsum('bhgnqd,bhnkd->bhgnqk', qb, kg).astype(F32) * scale
    s_win = jnp.where(ok, s_win, NEG_INF)
    s_ctx = jnp.einsum('bhgnqd,bhld->bhgnql', qb, k_ctx).astype(F32) * scale
    sk = jnp.broadcast_to(sink.astype(F32).reshape(1, hkv, g, 1, 1, 1), s_win.shape[:-1] + (1,))
    pr = jax.nn.softmax(jnp.concatenate([s_win, s_ctx, sk], axis=-1), axis=-1).astype(v.dtype)
    w = 3 * SWA_BLOCK
    o = jnp.einsum('bhgnqk,bhnkd->bhgnqd', pr[..., :w], vg) + jnp.einsum('bhgnql,bhld->bhgnqd', pr[..., w:-1], v_ctx)
    return o.reshape(b, hq, n, d)

def token_shift(u, mu):
    prev = jnp.pad(u, ((0, 0), (1, 0), (0, 0)))[:, :-1]
    nxt = jnp.pad(u, ((0, 0), (0, 1), (0, 0)))[:, 1:]
    return u + mu[0] * (prev - u) + mu[1] * (nxt - u)

def orient(z):
    z = jnp.transpose(z, (1, 2, 0, 3, 4))
    return jnp.stack([z[:, 0], z[::-1, 1]], axis=1)

def rwkv_step(s, inp):
    decay, kk, kka, k, v, r = inp
    sa = jnp.einsum('dbhvk,dbhk->dbhv', s, -kk)
    s = s * decay[..., None, :] + sa[..., None] * kka[..., None, :] + v[..., None] * k[..., None, :]
    return s, jnp.einsum('dbhvk,dbhk->dbhv', s, r)

def rwkv_mix(u, s0, p):
    b, l, _ = u.shape
    out_dtype = u.dtype
    hd = (RW_HEADS, HEAD_DIM)
    u = token_shift(u.astype(F32), p['rw_mu'].astype(F32))
    r, k, v, wl, al, gl = jnp.split(u, RW_SPLITS, axis=-1)
    wl = wl.reshape(b, l, 2, RW_DECAY_LORA)
    al = al.reshape(b, l, 2, RW_A_LORA)
    w = -jax.nn.softplus(-(p['rw_w0'] + jnp.einsum('bldr,drc->bldc', jnp.tanh(wl), p['rw_w2']))) - 0.5
    decay = jnp.exp(-jnp.exp(w))
    a = jax.nn.sigmoid(p['rw_a0'] + jnp.einsum('bldr,drc->bldc', al, p['rw_a2']))
    g = jax.nn.sigmoid(gl) @ p['rw_g2']
    kk = (k * p['rw_k_k']).reshape(b, l, *hd)
    kk = kk * lax.rsqrt(jnp.maximum(jnp.sum(kk * kk, axis=-1, keepdims=True), 1e-24))
    kd = (k[:, :, None] * (1.0 + (a - 1.0) * p['rw_k_a'])).reshape(b, l, 2, *hd)
    r = r.reshape(b, l, *hd)
    v = v.reshape(b, l, *hd)
    both = lambda z: jnp.broadcast_to(z[:, :, None], (b, l, 2) + hd)
    xs = (orient(decay.reshape(b, l, 2, *hd)), orient(both(kk)), orient(both(kk) * a.reshape(b, l, 2, *hd)),
          orient(kd), orient(both(v)), orient(both(r)))
    s_fin, o = lax.scan(rwkv_step, s0.astype(F32), xs)
    y = jnp.transpose(o[:, 0] + o[::-1, 1], (1, 0, 2, 3))
    mu = jnp.mean(y, axis=-1, keepdims=True)
    var = jnp.mean(jnp.square(y - mu), axis=-1, keepdims=True)
    y = (y - mu) * lax.rsqrt(var + GN_EPS) * p['rw_ln_g'].reshape(hd) + p['rw_ln_b'].reshape(hd)
    bonus = jnp.einsum('blhn,bldhn,hn->blh', r, kd, p['rw_r_k'])[..., None] * v
    out = (y + bonus).reshape(b, l, RW_W) * g
    return out.astype(out_dtype), s_fin

def expert_choice(h, w_router, w_gate, w_up, w_down):
    b, l, _ = h.shape
    cap = EC_CAPACITY * l // N_EXPERTS
    aff = jax.nn.softmax((h @ w_router).astype(F32), axis=-1)
    gate, idx = lax.top_k(jnp.swapaxes(aff, 1, 2), cap)
    bi = jnp.arange(b)[:, None, None]
    xe = h[bi, idx]
    he = jax.nn.silu(jnp.einsum('becd,edf->becf', xe, w_gate)) * jnp.einsum('becd,edf->becf', xe, w_up)
    ye = jnp.einsum('becf,efd->becd', he, w_down) * gate[..., None].astype(h.dtype)
    return jnp.zeros_like(h).at[bi, idx].add(ye)

def finish(x, oa, ob, oc, g1, sh2, sc2, g2, p):
    mix = jnp.concatenate([merge_heads(oa), ob, merge_heads(oc)], axis=-1) @ p['w_out']
    x = x + g1 * mix
    h = rms_norm(x, p['norm2_g']) * (1.0 + sc2) + sh2
    return x + g2 * expert_choice(h, p['w_router'], p['w_gate'], p['w_up'], p['w_down'])

def context_layer(x, c_ctx, p):
    sh1, sc1, g1, sh2, sc2, g2 = adaln(c_ctx[None], p['ada_w'], p['ada_b'])
    h = rms_norm(x, p['norm1_g']) * (1.0 + sc1) + sh1
    qa, ka, va, u_rw, qc, kc, vc = project(h, p)
    oa = dense_attention(qa, ka, va, None)
    s0 = jnp.zeros((2, x.shape[0], RW_HEADS, HEAD_DIM, HEAD_DIM), F32)
    ob, s_fin = rwkv_mix(u_rw, s0, p)
    oc = dense_attention(qc, kc, vc, p['swa_sink'])
    x = finish(x, oa, ob, oc, g1, sh2, sc2, g2, p)
    return x, ka, va, kc, vc, jnp.transpose(s_fin, (1, 0, 2, 3, 4))

def latent_layer(x, c, k_na, v_na, k_swa, v_swa, s_rw, p):
    sh1, sc1, g1, sh2, sc2, g2 = adaln(c, p['ada_w'], p['ada_b'])
    h = rms_norm(x, p['norm1_g']) * (1.0 + sc1) + sh1
    qa, ka, va, u_rw, qc, kc, vc = project(h, p)
    oa = neighbourhood_attention(qa, ka, va, k_na, v_na, p['na_rpb'])
    ob, _ = rwkv_mix(u_rw, jnp.transpose(s_rw, (1, 0, 2, 3, 4)), p)
    oc = window_attention(axial_rope(qc), axial_rope(kc), vc, k_swa, v_swa, p['swa_sink'])
    return finish(x, oa, ob, oc, g1, sh2, sc2, g2, p)

def setup_inputs(seed: int = 0) -> dict:
    key = jax.random.key(seed)
    ks = iter(jax.random.split(key, 64))

    def nrm(shape, scale):
        return scale * jax.random.normal(next(ks), shape, F32)

    def gain(shape):
        return 1.0 + nrm(shape, 0.02)

    def unif(shape, lo, hi):
        return jax.random.uniform(next(ks), shape, F32, lo, hi)

    L, D = DEPTH, D_MODEL
    return {
        'x_prompt': nrm((BATCH, SEQ, D), 1.0),
        'x_sample': nrm((DEC_BATCH, DEC_SEQ, D), 1.0),
        'cache_na_k': nrm((DEC_BATCH, L, NA_HEADS, PAST_LEN, HEAD_DIM), 1.0),
        'cache_na_v': nrm((DEC_BATCH, L, NA_HEADS, PAST_LEN, HEAD_DIM), 1.0),
        'cache_swa_k': nrm((DEC_BATCH, L, SWA_KV_HEADS, PAST_LEN, HEAD_DIM), 1.0),
        'cache_swa_v': nrm((DEC_BATCH, L, SWA_KV_HEADS, PAST_LEN, HEAD_DIM), 1.0),
        'state_rwkv': nrm((DEC_BATCH, L, 2, RW_HEADS, HEAD_DIM, HEAD_DIM), 0.3),
        'c': nrm((DEC_BATCH, D), 1.0),
        'c_ctx': nrm((D,), 1.0),
        'ada_w': nrm((L, D, 6 * D), 0.5 * D ** -0.5),
        'ada_b': nrm((L, 6 * D), 0.02),
        'norm1_g': gain((L, D)),
        'norm2_g': gain((L, D)),
        'w_in': nrm((L, D, IN_W), D ** -0.5),
        'na_q_norm': gain((L, HEAD_DIM)),
        'na_k_norm': gain((L, HEAD_DIM)),
        'na_rpb': nrm((L, NA_HEADS, 2 * NA_KH_MAX - 1, 2 * NA_KW - 1), 0.1),
        'rw_mu': unif((L, 2, RW_IN_W), 0.0, 0.4),
        'rw_w0': unif((L, 2, RW_W), -6.0, 1.0),
        'rw_w2': nrm((L, 2, RW_DECAY_LORA, RW_W), 0.5 * RW_DECAY_LORA ** -0.5),
        'rw_a0': nrm((L, 2, RW_W), 0.3),
        'rw_a2': nrm((L, 2, RW_A_LORA, RW_W), 0.5 * RW_A_LORA ** -0.5),
        'rw_g2': nrm((L, RW_GATE_LORA, RW_W), RW_GATE_LORA ** -0.5),
        'rw_k_k': 0.85 + nrm((L, RW_W), 0.05),
        'rw_k_a': gain((L, RW_W)),
        'rw_r_k': nrm((L, RW_HEADS, HEAD_DIM), 0.1),
        'rw_ln_g': gain((L, RW_W)),
        'rw_ln_b': nrm((L, RW_W), 0.02),
        'swa_q_norm': gain((L, HEAD_DIM)),
        'swa_k_norm': gain((L, HEAD_DIM)),
        'swa_sink': nrm((L, SWA_HEADS), 1.0),
        'w_out': nrm((L, MIX_W, D), MIX_W ** -0.5),
        'w_router': nrm((L, D, N_EXPERTS), D ** -0.5),
        'w_gate': nrm((L, N_EXPERTS, D, D_FF), D ** -0.5),
        'w_up': nrm((L, N_EXPERTS, D, D_FF), D ** -0.5),
        'w_down': nrm((L, N_EXPERTS, D_FF, D), D_FF ** -0.5),
    }

def reference(x_prompt, x_sample, cache_na_k, cache_na_v, cache_swa_k, cache_swa_v, state_rwkv, c, c_ctx,
              ada_w, ada_b, norm1_g, norm2_g, w_in, na_q_norm, na_k_norm, na_rpb,
              rw_mu, rw_w0, rw_w2, rw_a0, rw_a2, rw_g2, rw_k_k, rw_k_a, rw_r_k, rw_ln_g, rw_ln_b,
              swa_q_norm, swa_k_norm, swa_sink, w_out, w_router, w_gate, w_up, w_down):
    xp = x_prompt
    xs = x_sample
    new_ka, new_va, new_kc, new_vc, new_s = [], [], [], [], []
    for l in range(DEPTH):
        p = {
            'ada_w': ada_w[l], 'ada_b': ada_b[l], 'norm1_g': norm1_g[l], 'norm2_g': norm2_g[l],
            'w_in': w_in[l], 'na_q_norm': na_q_norm[l], 'na_k_norm': na_k_norm[l], 'na_rpb': na_rpb[l],
            'rw_mu': rw_mu[l], 'rw_w0': rw_w0[l], 'rw_w2': rw_w2[l], 'rw_a0': rw_a0[l], 'rw_a2': rw_a2[l],
            'rw_g2': rw_g2[l], 'rw_k_k': rw_k_k[l], 'rw_k_a': rw_k_a[l], 'rw_r_k': rw_r_k[l],
            'rw_ln_g': rw_ln_g[l], 'rw_ln_b': rw_ln_b[l], 'swa_q_norm': swa_q_norm[l],
            'swa_k_norm': swa_k_norm[l], 'swa_sink': swa_sink[l], 'w_out': w_out[l],
            'w_router': w_router[l], 'w_gate': w_gate[l], 'w_up': w_up[l], 'w_down': w_down[l],
        }
        xp, ka, va, kc, vc, s = context_layer(xp, c_ctx, p)
        new_ka.append(ka)
        new_va.append(va)
        new_kc.append(kc)
        new_vc.append(vc)
        new_s.append(s)
        xs = latent_layer(xs, c, cache_na_k[:, l], cache_na_v[:, l], cache_swa_k[:, l], cache_swa_v[:, l],
                          state_rwkv[:, l], p)
    return (xp, xs, jnp.stack(new_ka, axis=1), jnp.stack(new_va, axis=1), jnp.stack(new_kc, axis=1),
            jnp.stack(new_vc, axis=1), jnp.stack(new_s, axis=1))


_drawn_inputs = setup_inputs


def setup_inputs(seed=0):
    import zlib

    import numpy as np

    out = dict(_drawn_inputs(seed))
    spreads = {}
    factors = {'cache_na_k': 3.606,
     'cache_na_v': 2.952,
     'cache_swa_k': 4.551,
     'cache_swa_v': 3.731,
     'state_rwkv': 8.0,
     'norm2_g': 7.165,
     'na_q_norm': 8.0,
     'na_k_norm': 2.803,
     'na_rpb': 8.0,
     'rw_ln_g': 8.0,
     'rw_ln_b': 8.0,
     'swa_q_norm': 8.0,
     'swa_k_norm': 2.893,
     'swa_sink': 8.0}
    for name, (base, spread) in spreads.items():
        noise = np.random.default_rng([zlib.crc32(name.encode()), seed]).standard_normal(out[name].shape)
        drawn = base * np.exp(spread * noise) if base else spread * noise
        out[name] = jnp.asarray(drawn.astype(out[name].dtype))
    for name, factor in factors.items():
        out[name] = (out[name] * factor).astype(out[name].dtype)
    return out
```

```python
from contextlib import ExitStack

import numpy as np

import concourse.bass as bass
from concourse import mybir

F32 = mybir.dt.float32
U32 = mybir.dt.uint32
ALU = mybir.AluOpType
ACT = mybir.ActivationFunctionType
AX = mybir.AxisListType.X

P = 128
LAYERS = 2
D = 1024
KD = D // P
LAT, CTX = 512, 128
TOK = LAT + CTX
SEGMENTS = ((0, LAT), (LAT, TOK))
HD = 64
PAIRS_A = 3
RWC = 9
NT = TOK // P
EXPERTS = 16
LCAP, CCAP = 2 * LAT // EXPERTS, 2 * CTX // EXPERTS
CAP = LCAP + CCAP
FF = 1024
PAIRS = EXPERTS // 2
NEG = -1e30
DECAY = float(-np.exp(np.float32(-0.5)))

PIECE = 256
STREAM = 2
ADA_PIECES = 6 * D // PIECE
W_IN_PIECES = 12
OUT_PIECES = D // PIECE
PIECES = W_IN_PIECES + OUT_PIECES
RING = 6
EXPERT_PIECES = 12
MULTIPLIED = RING + 8

def _columns(sizes):
    at, out = 0, {}
    for name, n in sizes:
        out[name] = (at, at + n)
        at += n
    return out, at

PAR, PAR_N = _columns([("ada_b", 48), ("g1", 8), ("g2", 8), ("na_q", 1), ("na_k", 1), ("sw_q", 1), ("sw_k", 1),
                       ("mu0", 9), ("mu1", 9), ("w0", 4), ("a0", 4), ("k_k", 2), ("k_a", 2), ("r_k", 2),
                       ("ln_g", 2), ("ln_b", 2), ("sink", 6), ("w2", 256), ("a2", 256), ("lg2", 256), ("router", 128)])
CST, CST_N = _columns([("ident", 128), ("ones", 128), ("bones", 128), ("rot", 128), ("scmask", 1024),
                       ("lv", 2 * 7 * 128), ("namask", 768), ("swmask", 512), ("iota", 640), ("tokid", 5),
                       ("cos", 512), ("sin", 512), ("eps", 2)])


def _constants():
    c = np.zeros((P, CST_N), np.float32)

    def put(name, a):
        lo, hi = CST[name]
        c[:, lo:hi] = np.asarray(a, np.float32).reshape(P, hi - lo)

    p, q = np.arange(P)[:, None], np.arange(P)[None]
    put("ident", p == q)
    put("ones", np.ones((P, P)))
    put("bones", p // HD == q // HD)
    put("rot", np.where((q % HD < 32) & (p == q + 32), -1.0, 0.0) + np.where((q % HD >= 32) & (p == q - 32), 1.0, 0.0))
    sc, lv = [], []
    for d in range(2):
        strict, incl = ((p < q), (p <= q)) if d == 0 else ((p > q), (p >= q))
        sc += [strict, incl, strict, incl]
        for i in range(7):
            s = 1 << i
            a, b = (p, q) if d == 0 else (q, p)
            lv.append((b // s == a // s + 1) & (a // s % 2 == 0))
    put("scmask", np.stack(sc, 1))
    put("lv", np.stack(lv, 1))
    na = []
    for j in (0, 1, 3):
        start = min(max(j * 16 - 8, 0), 32)
        qc = 16 * j + np.arange(P)[:, None] % 16
        kc = start + np.arange(256)[None] % 32
        cs = np.clip(qc - 8, 0, 48)
        na.append(np.where((kc >= cs) & (kc < cs + 16), 0.0, NEG))
    put("namask", np.stack(na, 1))
    z = np.zeros((P, P))
    put("swmask", np.concatenate([np.where(q >= p, 0.0, NEG), z, z, np.where(q <= p, 0.0, NEG)], 1))
    put("iota", np.broadcast_to(np.arange(TOK), (P, TOK)))
    put("tokid", np.arange(P)[:, None] + P * np.arange(NT)[None])
    inv = np.float32(10000.0) ** (-np.arange(16, dtype=np.float32) / np.float32(16))
    t = np.arange(LAT)
    ang = np.concatenate([inv[:, None] * (t // 64).astype(np.float32), inv[:, None] * (t % 64).astype(np.float32)], 0)
    put("cos", np.tile(np.cos(ang), (4, 1)))
    put("sin", np.tile(np.sin(ang), (4, 1)))
    put("eps", np.broadcast_to(np.array([1e-6, 64e-5]), (P, 2)))
    return c


ARENA = 22100
N_RW = 2 * NT
N_ATT = 6 * 4 + 6 * 4 + 6 + 6
VEC_STEPS = 400
LEVELS = 6
INCS = {
    "stream_used": PIECES, "ada_used": ADA_PIECES, **{f"ada{s}": 16 * ADA_PIECES // RING for s in range(RING)}, "par_in": 16, "rpb_in": 16 * 48, "cache_in": 32, "state_in": 16, "vscr": 16,
    "vwin_in": 16 * 32, "out_kv": 48, "out_state": 16, "idx_out": 16, "idx_in": 32, "rw_x": LEVELS * N_RW,
    "sq": 2 * KD, "rst_s": 2, "h_ready": 2 * KD, "shift_a": RWC, "rw_lora": 1, "rw_le": 8, "rw_kk_sq": 2,
    "rw_kk_s": 2, "rw_exp": N_RW, "rw_tpc": N_RW, "rw_yc": LEVELS * N_RW, "rw_wc": N_RW, "rw_uc": N_RW, "rw_fs": 2,
    "rw_fsq": 2, "nsq": 10, "nsr": 10, "att_p": N_ATT, "att_ptc": N_ATT, "r_exp": 1, "act_step": 1,
    "xe_in": PAIRS, "m_silu": EXPERTS, "he_t": EXPERTS, "ye": EXPERTS,
    "ada": 1, "sq_used": 2 * KD, "proj_done": RWC, "lora_mm": 10, "kk_mm": 2, "rw_tp": N_RW, "rw_sc": 4 * N_RW,
    "rw_d0": N_RW, "rw_y": LEVELS * N_RW, "rw_z": LEVELS * N_RW, "rw_w": N_RW, "rw_u": N_RW, "rw_os": N_RW, "rw_fm": 6,
    "qk_done": 10, "qk_norm": 10, "rope_mm": 4, "v_mm": 2 * NT, "att_s": N_ATT, "att_t": N_ATT, "att_o": N_ATT,
    "out_mm": KD, "router_mm": 1, "aff_tp": 1, "h_tp": 2 * NT, "slot_tp": 1, "gather": PAIRS, "ring_free": 2,
    "ring_used": EXPERT_PIECES * EXPERTS + RING, "he_tp": EXPERTS, "scatter": KD * PAIRS,
    "vec_step": VEC_STEPS, "ms": 2, "h_part": 2 * KD, "shifted": RWC, "rw_sig": 1, "rw_kk": 2, "rw_kk_m": 2,
    "rw_prep_done": 1, "rw_sums": N_RW, "rw_in": N_RW, "rw_masked": 4 * N_RW, "rw_dt": N_RW, "rw_dd": (LEVELS + 1) * N_RW,
    "rw_state": N_RW, "rw_y_all": 1, "rw_yc2": 2, "rw_var": 2, "rw_bonus": 1, "rw_final": 1, "qk_ms": 10, "qk_used": 10,
    "k_ctx": 4, "roped": 4, "v_done": 2 * NT, "att_s_used": N_ATT, "att_m": N_ATT, "att_pn": N_ATT, "att_oc": N_ATT,
    "out_done": 2 * KD, "r_sub": 1, "aff_sp": 1, "h_tok": 2 * NT, "idx_top": 2,
    "sel": PAIRS, "selT": PAIRS, "he": EXPERTS, "scattered": KD * PAIRS, "xe_zero": 1,
}
INCS.update({f"stream{s}": 16 * PIECES // STREAM for s in range(STREAM)})
INCS.update({f"ring{s}": 16 * EXPERT_PIECES * EXPERTS // RING for s in range(RING)})
ONCE = ("boot", "cond_e", "silu_step", "silu", "layer_done", "out_y")


def program(nc, io):
    with ExitStack() as ctx:
        def sb(name, shape, dt=F32):
            return ctx.enter_context(nc.sbuf_tensor(name, shape, dt))

        sem = {name: ctx.enter_context(nc.semaphore(name)) for name in (*INCS, *ONCE)}

        cst = sb("cst", [P, CST_N])
        par = sb("par", [P, PAR_N])
        xT = sb("xT", [P, KD, TOK])
        hT = sb("hT", [P, KD, TOK])
        mixT = sb("mixT", [P, KD, TOK])
        stream = sb("stream", [P, STREAM, KD, PIECE])
        condT = sb("condT", [P, KD, 2])
        condE = sb("condE", [P, KD, 2])
        silu = sb("silu", [P, KD, 2])
        mod = sb("mod", [P, 48, 2])
        gain1 = sb("gain1", [P, KD, 2])
        gain2 = sb("gain2", [P, KD, 2])
        small = sb("small", [P, 64])
        dummy = sb("token", [P, 4])
        arena = sb("arena", [P, ARENA])
        psum = ctx.enter_context(nc.psum_tensor("psum", [P, 4096], F32))

        def C(name):
            return cst[:, CST[name][0]:CST[name][1]]

        def PV(name, i=0, n=1):
            return par[:, PAR[name][0] + i:PAR[name][0] + i + n]

        def bank(i, n=1):
            return psum[:, 512 * i:512 * (i + n)]

        def carve(at, *shape):
            n = int(np.prod(shape))
            assert at[0] + n <= ARENA, (at[0], n)
            v = arena[:, at[0]:at[0] + n]
            at[0] += n
            if len(shape) == 2:
                return v.rearrange("p (a b) -> p a b", a=shape[0])
            if len(shape) == 3:
                return v.rearrange("p (a b c) -> p a b c", a=shape[0], b=shape[1])
            if len(shape) == 4:
                return v.rearrange("p (a b c d) -> p a b c d", a=shape[0], b=shape[1], c=shape[2])
            return v

        ident, ones, bones = C("ident"), C("ones"), C("bones")
        scmask = C("scmask").rearrange("p (d n) -> p d n", d=2)
        lv = C("lv").rearrange("p (d s n) -> p d s n", d=2, s=7)
        namask = C("namask").rearrange("p (d n) -> p d n", d=3)

        mu_c = small[:, 8:17]
        one_ka, two_ka = small[:, 17:19], small[:, 19:21]
        naq8, swq8 = small[:, 21:22], small[:, 22:23]

        at = [0]
        rT, kT, vT, kkT, gT, yT = (carve(at, 2, TOK) for _ in range(6))
        ldT, aT = carve(at, 2, 2, TOK), carve(at, 2, 2, TOK)
        rw_common = at[0]
        lora = carve(at, 3, TOK)
        scr = carve(at, 2, TOK)
        at = [rw_common]
        Wc, Wm, Ec = (carve(at, 2, P) for _ in range(3))
        eR, eA, eB = (carve(at, 2, P) for _ in range(3))
        AR = carve(at, 2, 2, P)
        BK = carve(at, 2, 2, P)
        BKt = carve(at, 2, 2 * P)
        Vt = carve(at, 2 * P)
        SC = carve(at, 4, 4 * P)
        X = carve(at, 2, 4, P)
        Ysb = carve(at, 4, P)
        t1, t2 = Ysb[:, 0:2, :], Ysb[:, 2:4, :]
        DD = carve(at, 4, 2, P)
        Wsb, Usb = carve(at, 4 * HD), carve(at, 4 * HD)
        state = carve(at, 4, 2, HD)
        S0c, Stmp = carve(at, 2, HD), carve(at, 2, HD)
        e12 = carve(at, 2, 2)
        rw_end = at[0]

        at = [0]
        qa, ka, qc = (carve(at, 3, TOK) for _ in range(3))
        kc = carve(at, TOK)
        vtok = carve(at, NT, 512)
        vwin = carve(at, 8, 384)
        rpb = carve(at, 6, 512)
        kcache = carve(at, 4, P)
        vcache = carve(at, 512)
        nrm = carve(at, 2, TOK)
        swap = carve(at, LAT)
        Ssb, Pb, PT = (carve(at, 2, 516) for _ in range(3))
        amax = carve(at, 2, 4)
        att_end = at[0]

        at = [0]
        ring = carve(at, RING, 2, FF)
        ada_ring = arena[:, 0:RING * KD * PIECE].rearrange("p (s k c) -> p s k c", s=RING, k=KD)
        moe_common = at[0]
        xe0, xe1 = carve(at, KD, CAP), carve(at, KD, P)
        routing = at[0]
        sg, he = carve(at, FF), carve(at, FF)
        heT = carve(at, KD, P)
        ye_lat, ye_ctx = carve(at, D), carve(at, D)
        selT_lat, selT_ctx = carve(at, LAT), carve(at, CTX)
        sel_lat, sel_ctx = carve(at, 4, P), carve(at, 2 * CCAP)
        idx_lat, idx_ctx = carve(at, PAIRS, P), carve(at, PAIRS, 2 * CCAP)
        id_lat, gate_lat, id_ctx, gate_ctx = (carve(at, PAIRS) for _ in range(4))
        moe_end, at = at[0], [routing]
        aff_sp = carve(at, 4, 32)
        aff = carve(at, NT, EXPERTS)
        amx = carve(at, NT, 2)
        affT = carve(at, 512)
        tops = carve(at, 2, P)
        tops_ctx = carve(at, 2, 48)
        idx_u = carve(at, LCAP)
        vals = carve(at, LCAP)
        at = [ARENA - 3 * TOK]
        assert at[0] >= moe_common
        sq, rst = carve(at, 2, TOK), carve(at, TOK)
        htok = mixT[:, :, :].rearrange("p k t -> p (k t)").rearrange("p (i d) -> p i d", i=NT)

        block = ctx.enter_context(nc.Block())

        UNITS = []
        for i in range(4):
            UNITS += [(0, i, 0), (1, 3 - i, 2)]
        UNITS += [(0, 4, 1), (1, 4, 3)]

        ATT = []
        for h in range(6):
            for j in range(4):
                ATT.append(("na", h, j))
        for i in range(3):
            for g in range(2):
                for b in range(4):
                    ATT.append(("sw", i + 3 * g, b))
        for h in range(6):
            ATT.append(("cna", h, 0))
        for h in range(6):
            ATT.append(("csw", h, 0))

        def width(u):
            kind, h, j = u
            return {"na": 384, "sw": 384 if j in (0, 3) else 512}.get(kind, 128)

        @block.sync
        def _(sp):
            for dst, src in ((cst[:, :], io["cst"]), (xT[:, :, :], io["xT"]), (condT[:, :, :], io["cond"])):
                sp.dma_start(dst, src).then_inc(sem["boot"], 16)
            with sp.Fori(0, LAYERS) as l:
                sp.wait_ge(sem["ring_free"], l * INCS["ring_free"] + 2)
                sp.dma_start(par[:, :], io["par"][l]).then_inc(sem["par_in"], 16)
                for i in range(ADA_PIECES):
                    if i >= RING:
                        sp.wait_ge(sem["ada_used"], l * INCS["ada_used"] + i - RING + 1)
                    sp.dma_start(ada_ring[:, i % RING, :, :], io["ada_w"][l, i]).then_inc(sem[f"ada{i % RING}"], 16)
                n = 0

                def piece():
                    nonlocal n
                    s = n % STREAM
                    if n >= STREAM:
                        sp.wait_ge(sem["stream_used"], l * INCS["stream_used"] + n - STREAM + 1)
                    src = io["w_in"][l, order[n]] if n < W_IN_PIECES else io["w_out"][l, n - W_IN_PIECES]
                    sp.dma_start(stream[:, s, :, :], src).then_inc(sem[f"stream{s}"], 16)
                    n += 1

                order = [7, 8, 9, 10, 11, 0, 1, 2, 3, 4, 5, 6]
                for _ in range(5):
                    piece()
                sp.wait_ge(sem["rw_prep_done"], l * INCS["rw_prep_done"] + 1)
                sp.dma_start(state[:, 0:3:2, :, :], io["state"][l]).then_inc(sem["state_in"], 16)
                for _ in range(STREAM):
                    piece()
                sp.wait_ge(sem["rw_final"], l * INCS["rw_final"] + 1)
                sp.wait_ge(sem["rw_state"], l * INCS["rw_state"] + 10)
                sp.dma_start(kcache[:, :, :], io["kcache"][l]).then_inc(sem["cache_in"], 16)
                sp.dma_start(vcache, io["vcache"][l]).then_inc(sem["cache_in"], 16)
                for h in range(6):
                    for r in range(8):
                        src = bass.AP(tensor=io["rpb"].tensor, offset=l * 6144 + 1024 * h + 64 * r + 49, ap=[[1, 16], [1, 512]])
                        sp.dma_start(rpb[16 * r:16 * r + 16, h, :], src).then_inc(sem["rpb_in"], 16)
                for _ in range(7 - STREAM):
                    piece()
                for i in range(NT):
                    sp.wait_ge(sem["v_done"], l * INCS["v_done"] + 2 * (i + 1))
                sp.dma_start(io["vscr"].rearrange("(i p) c -> p i c", p=P), vtok[:, 0:4, 0:384]).then_inc(sem["vscr"], 16)
                sp.dma_start(io["nv"][l], vtok[:, 4, :]).then_inc(sem["out_kv"], 16)
                sp.wait_ge(sem["k_ctx"], l * INCS["k_ctx"] + 4)
                sp.dma_start(io["nk"][l][:, 0:3, :], ka[:, :, LAT:TOK]).then_inc(sem["out_kv"], 16)
                sp.dma_start(io["nk"][l][:, 3, :], kc[:, LAT:TOK]).then_inc(sem["out_kv"], 16)
                sp.wait_ge(sem["vscr"], l * INCS["vscr"] + 16)
                scr_v = io["vscr"].rearrange("(r c) f -> r c f", c=64)
                for j in range(4):
                    start = min(max(16 * j - 8, 0), 32)
                    for half in range(2):
                        for r in range(4):
                            sp.dma_start(vwin[32 * r:32 * r + 32, 2 * j + half, :],
                                                           scr_v[4 * half + r, start:start + 32, :]).then_inc(sem["vwin_in"], 16)
                for _ in range(OUT_PIECES):
                    piece()
                sp.wait_ge(sem["out_kv"], l * INCS["out_kv"] + 48)
                sp.wait_ge(sem["idx_top"], l * INCS["idx_top"] + 2)
                sp.dma_start(io["tops"], tops[0:32, 0, :]).then_inc(sem["idx_out"], 16)
                sp.wait_ge(sem["idx_out"], l * INCS["idx_out"] + 16)
                src = bass.AP(tensor=io["tops"].tensor, offset=0, ap=[[0, P], [P, EXPERTS], [1, LCAP]])
                sp.dma_start(idx_lat.rearrange("p e (h s) -> p (e h) s", h=2), src).then_inc(sem["idx_in"], 16)
                src = bass.AP(tensor=io["tops"].tensor, offset=EXPERTS * P, ap=[[0, P], [P, EXPERTS], [1, CCAP]])
                sp.dma_start(idx_ctx.rearrange("p e (h s) -> p (e h) s", h=2), src).then_inc(sem["idx_in"], 16)
                with sp.Fori(0, EXPERTS) as e:
                    for j in range(EXPERT_PIECES):
                        sp.wait_ge(sem["ring_used"], l * INCS["ring_used"] + e * EXPERT_PIECES + j + 1)
                        w, r = ("w_gate", j // 2) if j < 8 and j % 2 == 0 else ("w_up", j // 2) if j < 8 else ("w_down", j - 8)
                        sp.dma_start(ring[:, j % RING, :, :], io[w][l, e, 256 * r:256 * r + 256, :].rearrange("(k p) c -> p k c", p=P))\
                            .then_inc(sem[f"ring{j % RING}"], 16)
            sp.wait_ge(sem["layer_done"], 4 * LAYERS)
            sp.dma_start(io["y"], xT[:, :, :]).then_inc(sem["out_y"], 16)
            sp.wait_ge(sem["out_y"], 16)
            sp.wait_ge(sem["out_state"], 16 * LAYERS)
            sp.wait_ge(sem["out_kv"], 48 * LAYERS)
            sp.wait_ge(sem["idx_out"], 16 * LAYERS)
            sp.wait_ge(sem["vscr"], 16 * LAYERS)

        @block.gpsimd
        def _(pool):
            with pool.Fori(0, LAYERS) as l:
                for u, (d, c, s) in enumerate(UNITS):
                    pool.wait_ge(sem["rw_masked"], l * INCS["rw_masked"] + 4 * (u + 1))
                    for i in range(6):
                        if i >= 2:
                            pool.wait_ge(sem["rw_y"], l * INCS["rw_y"] + 6 * u + i - 1)
                        elif u:
                            pool.wait_ge(sem["rw_y"], l * INCS["rw_y"] + 6 * u)
                        nc.gpsimd.tensor_tensor(
                            X[:, i % 2, :, :], SC[:, :, 0:P], lv[:, d, i + 1, :].unsqueeze(1).to_broadcast([P, 4, P]), ALU.mult).then_inc(sem["rw_x"], 1)
                pool.wait_ge(sem["rw_state"], l * INCS["rw_state"] + 10)
                nc.gpsimd.dma_start(io["ns"][l], state[:, 1:4:2, :, :]).then_inc(sem["out_state"], 16)
                pool.wait_ge(sem["out_state"], l * INCS["out_state"] + 16)
                nc.gpsimd.tensor_tensor(dummy[:, 0:1], ident[:, 0:1], ident[:, 0:1], ALU.mult).then_inc(sem["layer_done"], 1)
                pool.wait_ge(sem["layer_done"], 4 * (l + 1))

        @block.scalar
        def _(act):
            A = nc.scalar.activation
            act.wait_ge(sem["boot"], 48)
            A(condE[:, :, :], condT[:, :, :], ACT.Exp, scale=-1.0).then_inc(sem["cond_e"], 1)
            with act.Fori(0, LAYERS) as l:

                def norm(first):
                    for k in range(KD):
                        if k >= 2:
                            act.wait_ge(sem["sq_used"], l * INCS["sq_used"] + first * KD + k - 1)
                        A(sq[:, k % 2, :], xT[:, k, :], ACT.Square).then_inc(sem["sq"], 1)
                    act.wait_ge(sem["sq_used"], l * INCS["sq_used"] + KD * (first + 1))
                    A(rst, bank(0, 2)[:, 0:TOK], ACT.Ln, scale=1.0 / D, bias=C("eps")[:, 0:1]).then_inc(sem["ms"], 1)
                    act.wait_ge(sem["ms"], l * INCS["ms"] + first + 1)
                    A(rst, rst, ACT.Exp, scale=-0.5).then_inc(sem["rst_s"], 1)
                    gain, shift = ((gain1, 0), (gain2, 24))[first]
                    for k in range(KD):
                        act.wait_ge(sem["h_part"], l * INCS["h_part"] + first * KD + k + 1)
                        for cond, (lo, hi) in enumerate(SEGMENTS):
                            i = A(hT[:, k, lo:hi], hT[:, k, lo:hi], ACT.Identity, scale=gain[:, k, cond:cond + 1],
                                  bias=mod[:, shift + k, cond:cond + 1])
                        i.then_inc(sem["h_ready"], 1)

                norm(0)
                for c in range(RWC):
                    act.wait_ge(sem["proj_done"], l * INCS["proj_done"] + c + 1)
                    dst = (rT[:, c % 2, :], kT[:, c % 2, :], vT[:, c % 2, :])[c // 2] if c < 6 else lora[:, c - 6, :]
                    A(dst, bank(2 * (c % 2), 2)[:, 0:TOK], ACT.Identity, scale=mu_c[:, c:c + 1]).then_inc(sem["shift_a"], 1)
                act.wait_ge(sem["shifted"], l * INCS["shifted"] + RWC)
                A(lora[:, 0, :], lora[:, 0, :], ACT.Tanh).then_inc(sem["rw_lora"], 1)
                A(lora[:, 2, :], lora[:, 2, :], ACT.Sigmoid).then_inc(sem["rw_sig"], 1)
                for g in range(8):
                    act.wait_ge(sem["lora_mm"], l * INCS["lora_mm"] + g + 1)
                    dst, bias = ((ldT, "w0"), (aT, "a0"))[g // 4]
                    i = g % 4
                    A(dst[:, i // 2, i % 2, :], bank(2 * (g % 2), 2)[:, 0:TOK], ACT.Sigmoid, bias=PV(bias, i)).then_inc(sem["rw_le"], 1)
                act.wait_ge(sem["rw_kk"], l * INCS["rw_kk"] + 2)
                for p in range(2):
                    A(scr[:, p, :], kkT[:, p, :], ACT.Square).then_inc(sem["rw_kk_sq"], 1)
                act.wait_ge(sem["rw_kk_m"], l * INCS["rw_kk_m"] + 2)
                A(scr[:, :, :], scr[:, :, :], ACT.Ln, scale=2.0 ** 20).then_inc(sem["rw_kk_s"], 1)
                act.wait_ge(sem["rw_kk_s"], l * INCS["rw_kk_s"] + 1)
                A(scr[:, :, :], scr[:, :, :], ACT.Exp, scale=-0.5).then_inc(sem["rw_kk_s"], 1)
                for u, (d, c, s) in enumerate(UNITS):
                    act.wait_ge(sem["rw_sums"], l * INCS["rw_sums"] + u + 1)
                    for dst, src, sign in (((eR, Wm, 1.0), (eA, Ec, 1.0), (eB, Wm, -1.0)) if d == 0 else
                                           ((eR, Ec, -1.0), (eA, Wm, -1.0), (eB, Ec, 1.0))):
                        A(dst[:, :, :], src[:, :, :], ACT.Exp, scale=sign)
                    A(e12[:, 0, :].unsqueeze(2), Wc[:, :, 63:64], ACT.Exp)
                    A(e12[:, 1, :].unsqueeze(2), Wm[:, :, P - 1:P], ACT.Exp).then_inc(sem["rw_exp"], 1)
                    act.wait_ge(sem["rw_tp"], l * INCS["rw_tp"] + u + 1)
                    nc.scalar.copy(BKt[:, :, :].rearrange("p a b -> p (a b)"), bank(0))
                    nc.scalar.copy(Vt, bank(1)[:, 0:2 * P]).then_inc(sem["rw_tpc"], 1)
                    for i in range(6):
                        act.wait_ge(sem["rw_y"], l * INCS["rw_y"] + 6 * u + i + 1)
                        nc.scalar.copy(Ysb[:, :, :].rearrange("p a b -> p (a b)"), bank(4)).then_inc(sem["rw_yc"], 1)
                    act.wait_ge(sem["rw_w"], l * INCS["rw_w"] + u + 1)
                    for h in range(2):
                        i = nc.scalar.copy(Wsb.rearrange("p (a b v) -> p a b v", a=2, b=2)[:, :, h, :],
                                           bank(5 + h)[:, 0:P].rearrange("p (a v) -> p a v", a=2))
                    i.then_inc(sem["rw_wc"], 1)
                    act.wait_ge(sem["rw_u"], l * INCS["rw_u"] + u + 1)
                    nc.scalar.copy(Usb, bank(7)[:, 256:512]).then_inc(sem["rw_uc"], 1)
                for p in range(2):
                    act.wait_ge(sem["rw_yc2"], l * INCS["rw_yc2"] + p + 1)
                    A(scr[:, p, :], yT[:, p, :], ACT.Square).then_inc(sem["rw_fsq"], 1)
                for p in range(2):
                    act.wait_ge(sem["rw_fm"], l * INCS["rw_fm"] + 3 + p)
                    A(scr[:, p, :], bank(4 + 2 * p, 2)[:, 0:TOK], ACT.Ln, scale=1.0 / HD, bias=C("eps")[:, 1:2]).then_inc(sem["rw_var"], 1)
                    act.wait_ge(sem["rw_var"], l * INCS["rw_var"] + p + 1)
                    A(scr[:, p, :], scr[:, p, :], ACT.Exp, scale=-0.5).then_inc(sem["rw_fs"], 1)
                act.wait_ge(sem["out_state"], l * INCS["out_state"] + 16)
                for c in range(10):
                    act.wait_ge(sem["qk_done"], l * INCS["qk_done"] + c + 1)
                    if c >= 2:
                        act.wait_ge(sem["qk_used"], l * INCS["qk_used"] + c - 1)
                    A(nrm[:, c % 2, :], bank(2 * (c % 2), 2)[:, 0:TOK], ACT.Square).then_inc(sem["nsq"], 1)
                    act.wait_ge(sem["qk_norm"], l * INCS["qk_norm"] + c + 1)
                    A(nrm[:, c % 2, :], bank(4, 2)[:, 0:TOK], ACT.Ln, scale=1.0 / HD, bias=C("eps")[:, 0:1]).then_inc(sem["qk_ms"], 1)
                    act.wait_ge(sem["qk_ms"], l * INCS["qk_ms"] + c + 1)
                    A(nrm[:, c % 2, :], nrm[:, c % 2, :], ACT.Exp, scale=-0.5).then_inc(sem["nsr"], 1)
                def exp(n):
                    w = width(ATT[n]) + (ATT[n][0] in ("sw", "csw"))
                    act.wait_ge(sem["att_m"], l * INCS["att_m"] + n + 1)
                    if n >= 2:
                        act.wait_ge(sem["att_t"], l * INCS["att_t"] + n - 1)
                    A(Pb[:, n % 2, 0:w], Ssb[:, n % 2, 0:w], ACT.Exp, bias=amax[:, n % 2, 0:1],
                                      accum_out=amax[:, n % 2, 1:2]).then_inc(sem["att_p"], 1)

                def pt(n):
                    w = width(ATT[n])
                    act.wait_ge(sem["att_t"], l * INCS["att_t"] + n + 1)
                    if n >= 2:
                        act.wait_ge(sem["att_o"], l * INCS["att_o"] + n - 1)
                    nc.scalar.copy(PT[:, n % 2, 0:w], bank(2 + n % 2)[:, 0:w]).then_inc(sem["att_ptc"], 1)

                for n in range(len(ATT) + 1):
                    if n < len(ATT):
                        exp(n)
                    if n >= 1:
                        pt(n - 1)
                act.wait_ge(sem["out_done"], l * INCS["out_done"] + 2 * KD)
                norm(1)
                act.wait_ge(sem["r_sub"], l * INCS["r_sub"] + 1)
                A(aff[:, :, :], aff[:, :, :], ACT.Exp).then_inc(sem["r_exp"], 1)
                for q in range(2 * NT):
                    act.wait_ge(sem["h_tp"], l * INCS["h_tp"] + q + 1)
                    nc.scalar.copy(htok[:, q // 2, 512 * (q % 2):512 * (q % 2) + 512], bank(4 + q % 2)).then_inc(sem["h_tok"], 1)
                gat = bank(6, 2).rearrange("p (k s) -> p k s", k=KD)
                gac = bank(4)[:, 0:256].rearrange("p (k s) -> p k s", k=KD)

                def gathered(n, used):
                    act.wait_ge(sem["gather"], l * INCS["gather"] + n)
                    if used is not None:
                        act.wait_ge(sem["ring_used"], l * INCS["ring_used"] + MULTIPLIED + EXPERT_PIECES * used)
                    nc.scalar.copy(xe0[:, :, 0:LCAP], gat[:, :, 0:LCAP])
                    nc.scalar.copy(xe0[:, :, LCAP:CAP], gac[:, :, 0:CCAP])
                    nc.scalar.copy(xe1[:, :, LCAP:P], gat[:, :, LCAP:P])
                    nc.scalar.copy(xe1[:, :, 0:CCAP], gac[:, :, CCAP:2 * CCAP]).then_inc(sem["xe_in"], 1)

                def expert(e, odd):
                    m = P if odd else CAP
                    act.wait_ge(sem["ring_used"], l * INCS["ring_used"] + MULTIPLIED + EXPERT_PIECES * e)
                    A(sg[0:m, :], bank(0, 2)[0:m, :], ACT.Silu).then_inc(sem["m_silu"], 1)

                def finish(e, odd):
                    m = P if odd else CAP
                    act.wait_ge(sem["he_tp"], l * INCS["he_tp"] + e + 1)
                    nc.scalar.copy(heT[:, :, 0:m], bank(0, 2).rearrange("p (k s) -> p k s", k=KD)[:, :, 0:m]).then_inc(sem["he_t"], 1)
                    act.wait_ge(sem["ring_used"], l * INCS["ring_used"] + RING + EXPERT_PIECES * (e + 1))
                    y = bank(4, 2)
                    if odd:
                        nc.scalar.copy(ye_lat[LCAP:P, :], y[LCAP:P, :])
                        nc.scalar.copy(ye_ctx[32:32 + CCAP, :], y[0:CCAP, :]).then_inc(sem["ye"], 1)
                    else:
                        nc.scalar.copy(ye_lat[0:LCAP, :], y[0:LCAP, :])
                        nc.scalar.copy(ye_ctx[0:CCAP, :], y[LCAP:CAP, :]).then_inc(sem["ye"], 1)

                act.wait_ge(sem["xe_zero"], l * INCS["xe_zero"] + 1)
                gathered(1, None)
                with act.Fori(0, PAIRS - 1) as i:
                    expert(2 * i, False)
                    finish(2 * i, False)
                    expert(2 * i + 1, True)
                    gathered(i + 2, 2 * i + 1)
                    finish(2 * i + 1, True)
                expert(EXPERTS - 2, False)
                finish(EXPERTS - 2, False)
                expert(EXPERTS - 1, True)
                finish(EXPERTS - 1, True)
                nc.scalar.copy(dummy[:, 1:2], C("ones")[:, 0:1]).then_inc(sem["act_step"], 1)
                act.wait_ge(sem["act_step"], l + 1)
                nc.scalar.copy(dummy[:, 1:2], C("ones")[:, 0:1]).then_inc(sem["layer_done"], 1)
                act.wait_ge(sem["layer_done"], 4 * (l + 1))

        @block.tensor
        def _(pe):
            mm = nc.tensor.matmul

            pe.wait_ge(sem["boot"], 48)
            mm(psum[0:1, 3584:3586], ident[:, 0:1], ident[:, 0:2], start=True, stop=True).then_inc(sem["ring_free"], 2)
            with pe.Fori(0, LAYERS) as l:
                pe.wait_ge(sem["par_in"], l * INCS["par_in"] + 16)
                n = 0

                def arrived():
                    nonlocal n
                    pe.wait_ge(sem[f"stream{n % STREAM}"], l * INCS[f"stream{n % STREAM}"] + 16 * (n // STREAM + 1))
                    n += 1
                    return (n - 1) % STREAM

                pe.wait_ge(sem["silu"], 1)
                for i in range(ADA_PIECES):
                    pe.wait_ge(sem[f"ada{i % RING}"], l * INCS[f"ada{i % RING}"] + 16 * (i // RING + 1))
                    for j in range(2):
                        q = 2 * i + j
                        for k in range(KD):
                            last = mm(psum[:, 2048 + 2 * q:2048 + 2 * q + 2], ada_ring[:, i % RING, k, j * P:(j + 1) * P], silu[:, k, :],
                                      start=k == 0, stop=k == KD - 1)
                    last.then_inc(sem["ada_used"], 1)
                mm(psum[0:1, 3072:3074], ident[:, 0:1], ident[:, 0:2], start=True, stop=True).then_inc(sem["ada"], 1)

                def norm(first):
                    for k in range(KD):
                        pe.wait_ge(sem["sq"], l * INCS["sq"] + first * KD + k + 1)
                        for lo, hi in SEGMENTS:
                            last = mm(bank(0, 2)[:, lo:hi], ones, sq[:, k % 2, lo:hi], start=k == 0, stop=k == KD - 1)
                        last.then_inc(sem["sq_used"], 1)

                norm(0)
                pe.wait_ge(sem["h_ready"], l * INCS["h_ready"] + KD)
                c = 0
                for i in range(5):
                    s = arrived()
                    for j in range(2 if i < 4 else 1):
                        if c >= 2:
                            pe.wait_ge(sem["shifted"], l * INCS["shifted"] + c - 1)
                        else:
                            pe.wait_ge(sem["ms"], l * INCS["ms"] + 1)
                        for lo, hi in SEGMENTS:
                            for k in range(KD):
                                last = mm(bank(2 * (c % 2), 2)[:, lo:hi], stream[:, s, k, j * P:(j + 1) * P], hT[:, k, lo:hi],
                                          start=k == 0, stop=k == KD - 1)
                        last.then_inc(sem["proj_done"], 1)
                        c += 1
                    mm(psum[0:1, 3072:3074], ident[:, 0:1], ident[:, 0:2], start=True, stop=True).then_inc(sem["stream_used"], 1)
                pe.wait_ge(sem["rw_lora"], l * INCS["rw_lora"] + 1)
                pe.wait_ge(sem["shifted"], l * INCS["shifted"] + RWC)
                for g in range(8):
                    d, p = g % 4 // 2, g % 2
                    w = PAR["w2" if g < 4 else "a2"][0] + p * P
                    if g >= 2:
                        pe.wait_ge(sem["rw_le"], l * INCS["rw_le"] + g - 1)
                    for lo, hi in SEGMENTS:
                        last = mm(bank(2 * (g % 2), 2)[:, lo:hi], par[HD * d:HD * d + HD, w:w + P],
                                  lora[HD * d:HD * d + HD, g // 4, lo:hi], start=True, stop=True)
                    last.then_inc(sem["lora_mm"], 1)
                pe.wait_ge(sem["rw_sig"], l * INCS["rw_sig"] + 1)
                for p in range(2):
                    w = PAR["lg2"][0] + p * P
                    pe.wait_ge(sem["rw_le"], l * INCS["rw_le"] + 7 + p)
                    for lo, hi in SEGMENTS:
                        last = mm(bank(2 * p, 2)[:, lo:hi], par[:, w:w + P], lora[:, 2, lo:hi], start=True, stop=True)
                    last.then_inc(sem["lora_mm"], 1)
                for p in range(2):
                    pe.wait_ge(sem["rw_kk_sq"], l * INCS["rw_kk_sq"] + p + 1)
                    for lo, hi in SEGMENTS:
                        last = mm(bank(4 + 2 * p, 2)[:, lo:hi], bones, scr[:, p, lo:hi], start=True, stop=True)
                    last.then_inc(sem["kk_mm"], 1)
                for u, (d, c, s) in enumerate(UNITS):
                    pe.wait_ge(sem["rw_in"], l * INCS["rw_in"] + u + 1)
                    T = slice(c * P, (c + 1) * P)
                    for i in range(4):
                        nc.tensor.transpose(bank(0)[:, P * i:P * i + P], BK[:, i // 2, i % 2, :], ident)
                    for p in range(2):
                        last = nc.tensor.transpose(bank(1)[:, P * p:P * p + P], vT[:, p, T], ident)
                    last.then_inc(sem["rw_tp"], 1)
                    for h in range(4):
                        hb, p = HD * (h % 2), h // 2
                        if h >= 2:
                            pe.wait_ge(sem["rw_masked"], l * INCS["rw_masked"] + 4 * u + h - 1)
                        rhs = AR[hb:hb + HD, p, :, :].rearrange("p a t -> p (a t)")
                        mm(bank(2 + h % 2)[:, 0:256], BK[hb:hb + HD, 0, p, :], rhs, start=True, stop=True)
                        mm(bank(2 + h % 2)[:, 256:512], BK[hb:hb + HD, 1, p, :], rhs, start=True, stop=True).then_inc(sem["rw_sc"], 1)
                    pe.wait_ge(sem["rw_dt"], l * INCS["rw_dt"] + u + 1)
                    for h in range(4):
                        last = nc.tensor.transpose(bank(4)[:, P * h:P * h + P], DD[:, h, 1, :], ident)
                    last.then_inc(sem["rw_d0"], 1)
                    for i in range(6):
                        pe.wait_ge(sem["rw_dd"], l * INCS["rw_dd"] + 7 * u + i + 1)
                        pe.wait_ge(sem["rw_x"], l * INCS["rw_x"] + 6 * u + i + 1)
                        for h in range(4):
                            last = mm(bank(4)[:, P * h:P * h + P], X[:, i % 2, h, :], DD[:, h, 0, :], start=True, stop=True)
                        last.then_inc(sem["rw_y"], 1)
                        pe.wait_ge(sem["rw_yc"], l * INCS["rw_yc"] + 6 * u + i + 1)
                        for h in range(4):
                            z = bank(5, 2)[:, 256 * h:256 * h + 256]
                            mm(z[:, 0:P], DD[:, h, 1, :], Ysb[:, h, :], start=True, stop=True)
                            last = mm(z[:, P:2 * P], Ysb[:, h, :], DD[:, h, 1, :], start=True, stop=True)
                        last.then_inc(sem["rw_z"], 1)
                    pe.wait_ge(sem["rw_dd"], l * INCS["rw_dd"] + 7 * u + 7)
                    pe.wait_ge(sem["rw_tpc"], l * INCS["rw_tpc"] + u + 1)
                    for h in range(4):
                        hb, p = HD * (h % 2), h // 2
                        o = bank(5 + h % 2)[:, HD * p:HD * p + HD]
                        mm(o, AR[hb:hb + HD, p, 0, :], S0c[hb:hb + HD, p, :], start=True, stop=False)
                        last = mm(o, SC[:, h, 2 * P:3 * P], Vt[:, HD * h:HD * h + HD], start=False, stop=True)
                    last.then_inc(sem["rw_w"], 1)
                    pe.wait_ge(sem["rw_wc"], l * INCS["rw_wc"] + u + 1)
                    for h in range(4):
                        last = mm(bank(7)[:, 256 + HD * h:256 + HD * h + HD], DD[:, h, 1, :], Wsb[:, HD * h:HD * h + HD], start=True, stop=True)
                    last.then_inc(sem["rw_u"], 1)
                    pe.wait_ge(sem["rw_uc"], l * INCS["rw_uc"] + u + 1)
                    for h in range(4):
                        hb, p = HD * (h % 2), h // 2
                        o = bank(1)[hb:hb + HD, HD * p:HD * p + HD]
                        mm(o, BKt[:, 0, HD * h:HD * h + HD], Usb[:, HD * h:HD * h + HD], start=True, stop=False)
                        mm(o, BKt[:, 1, HD * h:HD * h + HD], Vt[:, HD * h:HD * h + HD], start=False, stop=True)
                        o = bank(0)[hb:hb + HD, P * p:P * p + P]
                        mm(o, S0c[hb:hb + HD, p, :], AR[hb:hb + HD, p, 1, :], start=True, stop=False)
                        mm(o, Usb[:, HD * h:HD * h + HD], SC[:, h, P:2 * P], start=False, stop=False)
                        last = mm(o, Vt[:, HD * h:HD * h + HD], SC[:, h, 3 * P:4 * P], start=False, stop=True)
                    last.then_inc(sem["rw_os"], 1)
                def head_sums(src, b, name, v):
                    pe.wait_ge(sem[name], l * INCS[name] + v)
                    for lo, hi in SEGMENTS:
                        last = mm(bank(b, 2)[:, lo:hi], bones, src[:, lo:hi], start=True, stop=True)
                    last.then_inc(sem["rw_fm"], 1)

                for p in range(2):
                    head_sums(yT[:, p, :], 4 + 2 * p, "rw_y_all", 1)
                for p in range(2):
                    head_sums(scr[:, p, :], 4 + 2 * p, "rw_fsq", p + 1)
                for p in range(2):
                    head_sums(kT[:, p, :], 2 * p, "rw_bonus", 1)
                pe.wait_ge(sem["rw_final"], l * INCS["rw_final"] + 1)
                c = 0

                def qk_norm(c):
                    pe.wait_ge(sem["nsq"], l * INCS["nsq"] + c + 1)
                    for lo, hi in SEGMENTS:
                        last = mm(bank(4, 2)[:, lo:hi], bones, nrm[:, c % 2, lo:hi], start=True, stop=True)
                    last.then_inc(sem["qk_norm"], 1)
                    if c >= 6:
                        pe.wait_ge(sem["qk_used"], l * INCS["qk_used"] + c + 1)
                        if c > 6:
                            pe.wait_ge(sem["roped"], l * INCS["roped"] + c - 6)
                        dst = kc if c == 9 else qc[:, c - 6, :]
                        mm(bank(6), C("rot"), dst[:, 0:LAT], start=True, stop=True).then_inc(sem["rope_mm"], 1)

                for i in range(5):
                    s = arrived()
                    for j in range(2):
                        if c >= 2:
                            pe.wait_ge(sem["qk_used"], l * INCS["qk_used"] + c - 1)
                        for lo, hi in SEGMENTS:
                            for k in range(KD):
                                last = mm(bank(2 * (c % 2), 2)[:, lo:hi], stream[:, s, k, j * P:(j + 1) * P], hT[:, k, lo:hi],
                                          start=k == 0, stop=k == KD - 1)
                        last.then_inc(sem["qk_done"], 1)
                        if c >= 1:
                            if c >= 2:
                                pe.wait_ge(sem["qk_ms"], l * INCS["qk_ms"] + c - 1)
                            qk_norm(c - 1)
                        c += 1
                    mm(psum[0:1, 3584:3586], ident[:, 0:1], ident[:, 0:2], start=True, stop=True).then_inc(sem["stream_used"], 1)
                pe.wait_ge(sem["qk_ms"], l * INCS["qk_ms"] + 9)
                qk_norm(9)
                pe.wait_ge(sem["qk_used"], l * INCS["qk_used"] + 10)
                slots_v = [arrived(), arrived()]
                v = 0
                for i in range(NT):
                    for j in range(2):
                        if v >= 2:
                            pe.wait_ge(sem["v_done"], l * INCS["v_done"] + v - 1)
                        for k in range(KD):
                            last = mm(bank(v % 2)[:, 0:PIECE], hT[:, k, i * P:(i + 1) * P], stream[:, slots_v[j], k, :],
                                      start=k == 0, stop=k == KD - 1)
                        last.then_inc(sem["v_mm"], 1)
                        v += 1
                for _ in range(2):
                    mm(psum[0:1, 3584:3586], ident[:, 0:1], ident[:, 0:2], start=True, stop=True).then_inc(sem["stream_used"], 1)
                pe.wait_ge(sem["roped"], l * INCS["roped"] + 4)
                pe.wait_ge(sem["v_done"], l * INCS["v_done"] + 10)
                pe.wait_ge(sem["cache_in"], l * INCS["cache_in"] + 32)

                def scores(n):
                    kind, h, j = ATT[n]
                    o = bank(n % 2)
                    if n >= 2:
                        pe.wait_ge(sem["att_s_used"], l * INCS["att_s_used"] + n - 1)
                    if kind == "na":
                        hb, p = HD * (h % 2), h // 2
                        start = min(max(16 * j - 8, 0), 32)
                        q = qa[hb:hb + HD, p, P * j:P * j + P]
                        keys = ka[hb:hb + HD, p, 0:LAT].rearrange("p (r c) -> p r c", c=64)[:, :, start:start + 32]
                        mm(o[:, 0:256].rearrange("p (r c) -> p r c", c=32), q, keys, start=True, stop=True)
                        last = mm(o[:, 256:384], q, kcache[hb:hb + HD, p, :], start=True, stop=True)
                    elif kind == "cna":
                        hb, p = HD * (h % 2), h // 2
                        last = mm(o[:, 0:P], qa[hb:hb + HD, p, LAT:TOK], ka[hb:hb + HD, p, LAT:TOK], start=True, stop=True)
                    else:
                        g, i = h // 3, h % 3
                        hb = HD * g
                        if kind == "csw":
                            last = mm(o[:, 0:P], qc[hb:hb + HD, i, LAT:TOK], kc[hb:hb + HD, LAT:TOK], start=True, stop=True)
                        else:
                            q = qc[hb:hb + HD, i, P * j:P * j + P]
                            lo = max(j - 1, 0)
                            own = (j + 1 - lo) * P
                            mm(o[:, 0:own], q, kc[hb:hb + HD, lo * P:(j + 1) * P], start=True, stop=True)
                            last = mm(o[:, own:own + P], q, kcache[hb:hb + HD, 3, :], start=True, stop=True)
                            if j < 3:
                                last = mm(o[:, own + P:own + 2 * P], q, kc[hb:hb + HD, (j + 1) * P:(j + 2) * P], start=True, stop=True)
                    last.then_inc(sem["att_s"], 1)

                def values(n):
                    kind, h, j = ATT[n]
                    f = HD * h if kind in ("na", "cna") else 384 + HD * (h // 3)
                    if kind == "na":
                        return [vwin[:, 2 * j, f:f + HD], vwin[:, 2 * j + 1, f:f + HD], vcache[:, f:f + HD]]
                    if kind == "sw":
                        lo = max(j - 1, 0)
                        out = [vtok[:, b, f:f + HD] for b in range(lo, j + 1)] + [vcache[:, f:f + HD]]
                        return out + ([vtok[:, j + 1, f:f + HD]] if j < 3 else [])
                    return [vtok[:, 4, f:f + HD]]

                def probs_T(n):
                    pe.wait_ge(sem["att_pn"], l * INCS["att_pn"] + n + 1)
                    if n >= 2:
                        pe.wait_ge(sem["att_ptc"], l * INCS["att_ptc"] + n - 1)
                    for i in range(width(ATT[n]) // P):
                        last = nc.tensor.transpose(bank(2 + n % 2)[:, P * i:P * i + P], Pb[:, n % 2, P * i:P * i + P], ident)
                    last.then_inc(sem["att_t"], 1)

                def outputs(n):
                    kind, h, j = ATT[n]
                    hb = HD * (h % 2)
                    pe.wait_ge(sem["att_ptc"], l * INCS["att_ptc"] + n + 1)
                    if n >= 2:
                        pe.wait_ge(sem["att_oc"], l * INCS["att_oc"] + n - 1)
                    vs = values(n)
                    for i, v in enumerate(vs):
                        last = mm(bank(4 + n % 2)[hb:hb + HD, 0:P], v, PT[:, n % 2, P * i:P * i + P], start=i == 0, stop=i == len(vs) - 1)
                    last.then_inc(sem["att_o"], 1)

                pe.wait_ge(sem["vwin_in"], l * INCS["vwin_in"] + 16 * 32)
                for n_ in range(len(ATT) + 2):
                    if n_ < len(ATT):
                        scores(n_)
                    if 1 <= n_ <= len(ATT):
                        probs_T(n_ - 1)
                    if n_ >= 2:
                        outputs(n_ - 2)
                pe.wait_ge(sem["att_oc"], l * INCS["att_oc"] + len(ATT))
                mm(psum[0:1, 3584:3586], ident[:, 0:1], ident[:, 0:2], start=True, stop=True).then_inc(sem["ring_used"], RING)
                c = 0
                for i in range(OUT_PIECES):
                    s = arrived()
                    for j in range(2):
                        if c >= 2:
                            pe.wait_ge(sem["out_done"], l * INCS["out_done"] + 2 * (c - 1))
                        for lo, hi in SEGMENTS:
                            for k in range(KD):
                                last = mm(bank(2 * (c % 2), 2)[:, lo:hi], stream[:, s, k, j * P:(j + 1) * P], mixT[:, k, lo:hi],
                                          start=k == 0, stop=k == KD - 1)
                        last.then_inc(sem["out_mm"], 1)
                        c += 1
                    mm(psum[0:1, 3584:3586], ident[:, 0:1], ident[:, 0:2], start=True, stop=True).then_inc(sem["stream_used"], 1)
                pe.wait_ge(sem["out_done"], l * INCS["out_done"] + 2 * KD)
                norm(1)
                pe.wait_ge(sem["h_ready"], l * INCS["h_ready"] + 2 * KD)
                router = par[:, PAR["router"][0]:PAR["router"][1]].rearrange("p (k e) -> p k e", k=KD)
                for i in range(NT):
                    for k in range(KD):
                        last = mm(bank(2)[:, EXPERTS * i:EXPERTS * (i + 1)], hT[:, k, i * P:(i + 1) * P], router[:, k, :],
                                  start=k == 0, stop=k == KD - 1)
                last.then_inc(sem["router_mm"], 1)
                for i in range(NT):
                    for j in range(2):
                        q = 2 * i + j
                        if q >= 2:
                            pe.wait_ge(sem["h_tok"], l * INCS["h_tok"] + q - 1)
                        for k in range(4):
                            last = nc.tensor.transpose(bank(4 + q % 2)[:, P * k:P * k + P], hT[:, 4 * j + k, i * P:(i + 1) * P], ident)
                        last.then_inc(sem["h_tp"], 1)
                pe.wait_ge(sem["aff_sp"], l * INCS["aff_sp"] + 1)
                for i in range(4):
                    last = nc.tensor.transpose(bank(3)[0:32, P * i:P * i + P], aff_sp[:, i, :], ident)
                last.then_inc(sem["aff_tp"], 1)
                pe.wait_ge(sem["idx_top"], l * INCS["idx_top"] + 2)
                mm(bank(2)[0:1, 0:2], ident[:, 0:1], ident[:, 0:2], start=True, stop=True)
                for i in range(2):
                    nc.tensor.transpose(bank(3)[:, 32 * i:32 * i + 32], tops[0:32, i, :], ident[0:32, 0:32])
                    last = nc.tensor.transpose(bank(3)[0:48, 64 + 32 * i:96 + 32 * i], tops_ctx[0:32, i, :], ident[0:32, 0:32])
                last.then_inc(sem["slot_tp"], 1)
                pe.wait_ge(sem["h_tok"], l * INCS["h_tok"] + 10)
                gat = bank(6, 2).rearrange("p (k s) -> p k s", k=KD)
                gac = bank(4)[:, 0:256].rearrange("p (k s) -> p k s", k=KD)
                heT_ps = bank(0, 2).rearrange("p (k s) -> p k s", k=KD)

                def gather(n):
                    pe.wait_ge(sem["sel"], l * INCS["sel"] + n)
                    for k in range(KD):
                        for i in range(4):
                            mm(gat[:, k, :], htok[:, i, k * P:(k + 1) * P], sel_lat[:, i, :], start=i == 0, stop=i == 3)
                        last = mm(gac[:, k, :], htok[:, 4, k * P:(k + 1) * P], sel_ctx, start=True, stop=True)
                    last.then_inc(sem["gather"], 1)

                def gate_up(e, odd):
                    m, x = (P, xe1) if odd else (CAP, xe0)
                    for j in range(8):
                        pe.wait_ge(sem[f"ring{j % RING}"], l * INCS[f"ring{j % RING}"] + 32 * e + 16 * (j // RING + 1))
                        for kk in range(2):
                            k = 2 * (j // 2) + kk
                            for f in range(2):
                                last = mm(bank(2 * (j % 2) + f)[0:m, :], x[:, k, 0:m], ring[:, j % RING, kk, 512 * f:512 * f + 512],
                                          start=k == 0, stop=k == KD - 1)
                        last.then_inc(sem["ring_used"], 1)

                def down(e, odd):
                    m = P if odd else CAP
                    pe.wait_ge(sem["he"], l * INCS["he"] + e + 1)
                    for k in range(KD):
                        last = nc.tensor.transpose(heT_ps[:, k, 0:m], he[0:m, k * P:(k + 1) * P], ident[0:m, 0:m])
                    last.then_inc(sem["he_tp"], 1)
                    pe.wait_ge(sem["he_t"], l * INCS["he_t"] + e + 1)
                    for j in range(8, EXPERT_PIECES):
                        pe.wait_ge(sem[f"ring{j % RING}"], l * INCS[f"ring{j % RING}"] + 32 * e + 16 * (j // RING + 1))
                        for kk in range(2):
                            k = 2 * (j - 8) + kk
                            for f in range(2):
                                last = mm(bank(4 + f)[0:m, :], heT[:, k, 0:m], ring[:, j % RING, kk, 512 * f:512 * f + 512],
                                          start=k == 0, stop=k == KD - 1)
                        last.then_inc(sem["ring_used"], 1)

                def scatter(n):
                    pe.wait_ge(sem["ye"], l * INCS["ye"] + 2 * n)
                    pe.wait_ge(sem["selT"], l * INCS["selT"] + n)
                    for k in range(KD):
                        b = (6, 4)[k % 2]
                        if k >= 2:
                            pe.wait_ge(sem["scattered"], l * INCS["scattered"] + KD * n - KD + k - 1)
                        mm(bank(b), ye_lat[:, k * P:(k + 1) * P], selT_lat, start=True, stop=True)
                        mm(bank(b + 1)[:, 0:CTX], ye_ctx[0:48, k * P:(k + 1) * P], selT_ctx[0:48, :], start=True, stop=True)\
                            .then_inc(sem["scatter"], 1)

                gather(1)
                pe.wait_ge(sem["xe_in"], l * INCS["xe_in"] + 1)
                gate_up(0, False)
                down(0, False)
                gate_up(1, True)
                pe.wait_ge(sem["ye"], l * INCS["ye"] + 1)
                gather(2)
                pe.wait_ge(sem["xe_in"], l * INCS["xe_in"] + 2)
                down(1, True)
                with pe.Fori(1, PAIRS - 1) as i:
                    gate_up(2 * i, False)
                    scatter(i)
                    pe.wait_ge(sem["scattered"], l * INCS["scattered"] + KD * i)
                    down(2 * i, False)
                    gate_up(2 * i + 1, True)
                    pe.wait_ge(sem["ye"], l * INCS["ye"] + 2 * i + 1)
                    gather(i + 2)
                    pe.wait_ge(sem["xe_in"], l * INCS["xe_in"] + i + 2)
                    down(2 * i + 1, True)
                gate_up(EXPERTS - 2, False)
                scatter(PAIRS - 1)
                pe.wait_ge(sem["scattered"], l * INCS["scattered"] + KD * (PAIRS - 1))
                down(EXPERTS - 2, False)
                gate_up(EXPERTS - 1, True)
                down(EXPERTS - 1, True)
                mm(psum[0:1, 3584:3586], ident[:, 0:1], ident[:, 0:2], start=True, stop=True).then_inc(sem["ring_free"], 2)
                scatter(PAIRS)
                pe.wait_ge(sem["scattered"], l * INCS["scattered"] + KD * PAIRS)
                mm(psum[0:1, 3584:3586], ident[:, 0:1], ident[:, 0:2], start=True, stop=True).then_inc(sem["layer_done"], 1)
                pe.wait_ge(sem["layer_done"], 4 * (l + 1))

        @block.vector
        def _(dve):
            V = nc.vector
            dve.wait_ge(sem["boot"], 48)
            dve.wait_ge(sem["cond_e"], 1)
            V.tensor_scalar(condE[:, :, :], condE[:, :, :], 1.0, None, ALU.add).then_inc(sem["silu_step"], 1)
            dve.wait_ge(sem["silu_step"], 1)
            V.reciprocal(condE[:, :, :], condE[:, :, :]).then_inc(sem["silu_step"], 1)
            dve.wait_ge(sem["silu_step"], 2)
            V.tensor_tensor(silu[:, :, :], condT[:, :, :], condE[:, :, :], ALU.mult).then_inc(sem["silu"], 1)
            with dve.Fori(0, LAYERS) as l:

                count = dict.fromkeys(INCS, 0)

                def v(ins):
                    count["vec_step"] += 1
                    ins.then_inc(sem["vec_step"], 1)
                    dve.wait_ge(sem["vec_step"], l * INCS["vec_step"] + count["vec_step"])

                def out(name, ins):
                    count[name] += 1
                    ins.then_inc(sem[name], 1)
                    dve.wait_ge(sem[name], l * INCS[name] + count[name])

                dve.wait_ge(sem["par_in"], l * INCS["par_in"] + 16)
                v(V.tensor_tensor(mu_c, PV("mu0", 0, 9), PV("mu1", 0, 9), ALU.add))
                v(V.tensor_scalar(mu_c, mu_c, -1.0, 1.0, ALU.mult, ALU.add))
                v(V.tensor_scalar(one_ka, PV("k_a", 0, 2), -1.0, 1.0, ALU.mult, ALU.add))
                v(V.tensor_scalar(two_ka, one_ka, 2.0, None, ALU.mult))
                v(V.tensor_scalar(naq8, PV("na_q"), 0.125, None, ALU.mult))
                v(V.tensor_scalar(swq8, PV("sw_q"), 0.125, None, ALU.mult))
                dve.wait_ge(sem["ada"], l * INCS["ada"] + 1)
                v(V.tensor_tensor(mod[:, :, :], psum[:, 2048:2144].rearrange("p (q c) -> p q c", c=2),
                                  PV("ada_b", 0, 48).unsqueeze(2).to_broadcast([P, 48, 2]), ALU.add))
                for g, name, q in ((gain1, "g1", 8), (gain2, "g2", 32)):
                    v(V.scalar_tensor_tensor(g[:, :, :], mod[:, q:q + 8, :], 1.0, PV(name, 0, 8).unsqueeze(2).to_broadcast([P, 8, 2]),
                                             ALU.add, ALU.mult))

                def norm(first):
                    dve.wait_ge(sem["rst_s"], l * INCS["rst_s"] + first + 1)
                    for k in range(KD):
                        V.tensor_tensor(hT[:, k, :], xT[:, k, :], rst, ALU.mult).then_inc(sem["h_part"], 1)

                norm(0)
                for c in range(RWC):
                    dve.wait_ge(sem["shift_a"], l * INCS["shift_a"] + c + 1)
                    dst = (rT[:, c % 2, :], kT[:, c % 2, :], vT[:, c % 2, :])[c // 2] if c < 6 else lora[:, c - 6, :]
                    u = bank(2 * (c % 2), 2)
                    for n, (lo, hi) in enumerate(SEGMENTS):
                        v(V.scalar_tensor_tensor(dst[:, lo + 1:hi], u[:, lo:hi - 1], PV("mu0", c), dst[:, lo + 1:hi], ALU.mult, ALU.add))
                        ins = V.scalar_tensor_tensor(dst[:, lo:hi - 1], u[:, lo + 1:hi], PV("mu1", c), dst[:, lo:hi - 1], ALU.mult, ALU.add)
                        (out if n else lambda _, i: v(i))("shifted", ins)
                for p in range(2):
                    out("rw_kk", V.tensor_scalar(kkT[:, p, :], kT[:, p, :], PV("k_k", p), None, ALU.mult))
                dve.wait_ge(sem["rw_le"], l * INCS["rw_le"] + 8)
                v(V.tensor_scalar(ldT[:, :, :, :], ldT[:, :, :, :], DECAY, None, ALU.mult))
                dve.wait_ge(sem["lora_mm"], l * INCS["lora_mm"] + 10)
                for p in range(2):
                    v(V.tensor_copy(gT[:, p, :], bank(2 * p, 2)[:, 0:TOK]))
                dve.wait_ge(sem["kk_mm"], l * INCS["kk_mm"] + 2)
                for p in range(2):
                    out("rw_kk_m", V.tensor_scalar(scr[:, p, :], bank(4 + 2 * p, 2)[:, 0:TOK], 1e-24, None, ALU.max))
                dve.wait_ge(sem["rw_kk_s"], l * INCS["rw_kk_s"] + 2)
                out("rw_prep_done", V.scalar_tensor_tensor(kkT[:, :, :], kkT[:, :, :], 2.0 ** 10, scr[:, :, :], ALU.mult, ALU.mult))
                v(V.memset(state[:, 1:4:2, :, :], 0.0))
                v(V.memset(yT[:, :, :], 0.0))
                dve.wait_ge(sem["state_in"], l * INCS["state_in"] + 16)
                for u, (d, c, s) in enumerate(UNITS):
                    T = slice(c * P, (c + 1) * P)
                    for p in range(2):
                        v(V.tensor_tensor_scan(Wc[:, p, :], ones, ldT[:, d, p, T], 0.0, ALU.mult, ALU.add))
                    v(V.tensor_tensor(Wm[:, :, :], Wc[:, :, :], Wc[:, :, 63:64].to_broadcast([P, 2, P]), ALU.subtract))
                    out("rw_sums", V.tensor_tensor(Ec[:, :, :], Wm[:, :, :], ldT[:, d, :, T], ALU.subtract))
                    for p in range(2):
                        v(V.tensor_scalar(t2[:, p, :], aT[:, d, p, T], PV("k_a", p), one_ka[:, p:p + 1], ALU.mult, ALU.add))
                    v(V.tensor_tensor(t2[:, :, :], t2[:, :, :], kT[:, :, T], ALU.mult))
                    v(V.tensor_tensor(t1[:, :, :], kkT[:, :, T], aT[:, d, :, T], ALU.mult))
                    dve.wait_ge(sem["rw_exp"], l * INCS["rw_exp"] + u + 1)
                    v(V.scalar_tensor_tensor(AR[:, :, 0, :], kkT[:, :, T], -1.0, eA[:, :, :], ALU.mult, ALU.mult))
                    v(V.tensor_tensor(AR[:, :, 1, :], rT[:, :, T], eR[:, :, :], ALU.mult))
                    v(V.tensor_tensor(BK[:, 0, :, :], t1[:, :, :], eB[:, :, :], ALU.mult))
                    v(V.tensor_tensor(BK[:, 1, :, :], t2[:, :, :], eB[:, :, :], ALU.mult))
                    ein, eout = (e12[:, 0, :], e12[:, 1, :]) if d == 0 else (e12[:, 1, :], e12[:, 0, :])
                    out("rw_in", V.tensor_tensor(S0c[:, :, :], state[:, s, :, :], ein.unsqueeze(2).to_broadcast([P, 2, HD]), ALU.mult))
                    for h in range(4):
                        dve.wait_ge(sem["rw_sc"], l * INCS["rw_sc"] + 4 * u + h + 1)
                        out("rw_masked", V.tensor_tensor(SC[:, h, :], bank(2 + h % 2), scmask[:, d, :], ALU.mult))
                    v(V.tensor_tensor(DD[:, :, 1, :], SC[:, :, 0:P], lv[:, d, 0, :].unsqueeze(1).to_broadcast([P, 4, P]), ALU.mult))
                    out("rw_dt", V.tensor_tensor(DD[:, :, 1, :], DD[:, :, 1, :], ident.unsqueeze(1).to_broadcast([P, 4, P]), ALU.add))
                    dve.wait_ge(sem["rw_d0"], l * INCS["rw_d0"] + u + 1)
                    out("rw_dd", V.tensor_copy(DD[:, :, 0, :], bank(4).rearrange("p (h t) -> p h t", h=4)))
                    for i in range(6):
                        dve.wait_ge(sem["rw_z"], l * INCS["rw_z"] + 6 * u + i + 1)
                        z = bank(5, 2).rearrange("p (h n) -> p h n", h=4)
                        flat = DD[:, :, :, :].rearrange("p h a t -> p h (a t)")
                        out("rw_dd", V.tensor_tensor(flat, flat, z, ALU.add))
                    dve.wait_ge(sem["rw_os"], l * INCS["rw_os"] + u + 1)
                    v(V.tensor_tensor(yT[:, :, T], yT[:, :, T], bank(0)[:, 0:256].rearrange("p (a t) -> p a t", a=2), ALU.add))
                    v(V.tensor_tensor(Stmp[:, :, :], S0c[:, :, :], bank(1)[:, 0:P].rearrange("p (a t) -> p a t", a=2), ALU.add))
                    out("rw_state", V.tensor_tensor(state[:, s, :, :], Stmp[:, :, :], eout.unsqueeze(2).to_broadcast([P, 2, HD]), ALU.mult))
                V.tensor_copy(small[:, 60:61], ident[:, 0:1]).then_inc(sem["rw_y_all"], 1)
                for p in range(2):
                    dve.wait_ge(sem["rw_fm"], l * INCS["rw_fm"] + p + 1)
                    out("rw_yc2", V.scalar_tensor_tensor(yT[:, p, :], bank(4 + 2 * p, 2)[:, 0:TOK], -1.0 / HD, yT[:, p, :], ALU.mult, ALU.add))
                v(V.tensor_tensor(aT[:, 0, :, :], aT[:, 0, :, :], aT[:, 1, :, :], ALU.add))
                for p in range(2):
                    v(V.tensor_scalar(aT[:, 0, p, :], aT[:, 0, p, :], PV("k_a", p), two_ka[:, p:p + 1], ALU.mult, ALU.add))
                v(V.tensor_tensor(kT[:, :, :], kT[:, :, :], aT[:, 0, :, :], ALU.mult))
                v(V.tensor_tensor(kT[:, :, :], kT[:, :, :], rT[:, :, :], ALU.mult))
                v(V.tensor_scalar(kT[:, 0, :], kT[:, 0, :], PV("r_k", 0), None, ALU.mult))
                out("rw_bonus", V.tensor_scalar(kT[:, 1, :], kT[:, 1, :], PV("r_k", 1), None, ALU.mult))
                dve.wait_ge(sem["rw_fs"], l * INCS["rw_fs"] + 2)
                v(V.tensor_tensor(yT[:, :, :], yT[:, :, :], scr[:, :, :], ALU.mult))
                for p in range(2):
                    v(V.tensor_scalar(yT[:, p, :], yT[:, p, :], PV("ln_g", p), PV("ln_b", p), ALU.mult, ALU.add))
                for p in range(2):
                    dve.wait_ge(sem["rw_fm"], l * INCS["rw_fm"] + 5 + p)
                    v(V.tensor_tensor(vT[:, p, :], vT[:, p, :], bank(2 * p, 2)[:, 0:TOK], ALU.mult))
                v(V.tensor_tensor(yT[:, :, :], yT[:, :, :], vT[:, :, :], ALU.add))
                out("rw_final", V.tensor_tensor(mixT[:, 3:5, :], yT[:, :, :], gT[:, :, :], ALU.mult))
                for c in range(10):
                    x = bank(2 * (c % 2), 2)
                    r = nrm[:, c % 2, :]
                    dve.wait_ge(sem["nsr"], l * INCS["nsr"] + c + 1)
                    g = naq8 if c < 3 else PV("na_k") if c < 6 else swq8 if c < 9 else PV("sw_k")
                    if c < 3:
                        v(V.tensor_scalar(r, r, g, None, ALU.mult))
                        for j in range(4):
                            view = lambda t: t[:, 0:LAT].rearrange("p (r j c) -> p r j c", r=8, j=4)[:, :, j, :]
                            v(V.tensor_tensor(qa[:, c, P * j:P * j + P].rearrange("p (r c) -> p r c", r=8)[:, :, :],
                                              view(x), view(r), ALU.mult))
                        out("qk_used", V.tensor_tensor(qa[:, c, LAT:TOK], x[:, LAT:TOK], r[:, LAT:TOK], ALU.mult))
                    else:
                        dst = ka[:, c - 3, :] if c < 6 else qc[:, c - 6, :] if c < 9 else kc
                        out("qk_used", V.scalar_tensor_tensor(dst, x[:, 0:TOK], g, r, ALU.mult, ALU.mult))
                        if c < 6 or c == 9:
                            out("k_ctx", V.tensor_copy(small[:, 61:62], ident[:, 0:1]))
                        if c >= 6:
                            dve.wait_ge(sem["rope_mm"], l * INCS["rope_mm"] + c - 5)
                            v(V.tensor_tensor(swap, bank(6), C("sin"), ALU.mult))
                            v(V.tensor_tensor(dst[:, 0:LAT], dst[:, 0:LAT], C("cos"), ALU.mult))
                            out("roped", V.tensor_tensor(dst[:, 0:LAT], dst[:, 0:LAT], swap, ALU.add))
                for i in range(NT):
                    for j in range(2):
                        q = 2 * i + j
                        dve.wait_ge(sem["v_mm"], l * INCS["v_mm"] + q + 1)
                        V.tensor_copy(vtok[:, i, PIECE * j:PIECE * (j + 1)], bank(q % 2)[:, 0:PIECE]).then_inc(sem["v_done"], 1)
                dve.wait_ge(sem["v_done"], l * INCS["v_done"] + 10)
                dve.wait_ge(sem["rpb_in"], l * INCS["rpb_in"] + 16 * 48)

                def stage1(n):
                    kind, h, j = ATT[n]
                    b, S, w = bank(n % 2), Ssb[:, n % 2, :], width(ATT[n])
                    dve.wait_ge(sem["att_s"], l * INCS["att_s"] + n + 1)
                    if kind == "na":
                        x0 = min(max(16 * j - 8, 0), 32) - 16 * j + 16
                        bias = rpb[:, h, :].rearrange("p (r x) -> p r x", x=64)[:, ::-1, ::-1][:, :, x0:x0 + 32]
                        v(V.tensor_tensor(S[:, 0:256].rearrange("p (r c) -> p r c", c=32), b[:, 0:256].rearrange("p (r c) -> p r c", c=32),
                                          bias, ALU.add))
                        out("att_s_used", V.tensor_copy(S[:, 256:384], b[:, 256:384]))
                        v(V.tensor_tensor(S[:, 0:256], S[:, 0:256], namask[:, (0, 1, 1, 2)[j], :], ALU.add))
                    elif kind == "sw":
                        m = C("swmask")[:, P:] if j == 0 else C("swmask")
                        out("att_s_used", V.tensor_tensor(S[:, 0:w], b[:, 0:w], m[:, 0:w], ALU.add))
                    else:
                        out("att_s_used", V.tensor_copy(S[:, 0:w], b[:, 0:w]))
                    if kind in ("sw", "csw"):
                        v(V.tensor_copy(S[:, w:w + 1], PV("sink", h)))
                        w += 1
                    out("att_m", V.tensor_reduce(amax[:, n % 2, 0:1], S[:, 0:w], AX, ALU.max, negate=True))

                def stage2(n):
                    w = width(ATT[n])
                    dve.wait_ge(sem["att_p"], l * INCS["att_p"] + n + 1)
                    v(V.reciprocal(amax[:, n % 2, 2:3], amax[:, n % 2, 1:2]))
                    out("att_pn", V.tensor_scalar(Pb[:, n % 2, 0:w], Pb[:, n % 2, 0:w], amax[:, n % 2, 2:3], None, ALU.mult))

                def stage3(n):
                    kind, h, j = ATT[n]
                    hb = HD * (h % 2)
                    dve.wait_ge(sem["att_o"], l * INCS["att_o"] + n + 1)
                    src = bank(4 + n % 2)[hb:hb + HD, 0:P]
                    chunk = h // 2 + (0 if kind in ("na", "cna") else 5)
                    if kind == "na":
                        dst = mixT[hb:hb + HD, chunk, 0:LAT].rearrange("p (r j c) -> p r j c", r=8, j=4)[:, :, j, :]
                        src = src.rearrange("p (r c) -> p r c", r=8)
                    elif kind == "sw":
                        dst = mixT[hb:hb + HD, chunk, P * j:P * j + P]
                    else:
                        dst = mixT[hb:hb + HD, chunk, LAT:TOK]
                    V.tensor_copy(dst, src).then_inc(sem["att_oc"], 1)

                for n in range(len(ATT) + 2):
                    if n < len(ATT):
                        stage1(n)
                    if 1 <= n <= len(ATT):
                        stage2(n - 1)
                    if n >= 2:
                        stage3(n - 2)
                for c in range(KD):
                    dve.wait_ge(sem["out_mm"], l * INCS["out_mm"] + c + 1)
                    for cond, (lo, hi) in enumerate(SEGMENTS):
                        V.scalar_tensor_tensor(xT[:, c, lo:hi], bank(2 * (c % 2), 2)[:, lo:hi], mod[:, 16 + c, cond:cond + 1],
                                                                  xT[:, c, lo:hi], ALU.mult, ALU.add).then_inc(sem["out_done"], 1)
                dve.wait_ge(sem["out_done"], l * INCS["out_done"] + 2 * KD)
                norm(1)
                dve.wait_ge(sem["router_mm"], l * INCS["router_mm"] + 1)
                r = bank(2)[:, 0:NT * EXPERTS].rearrange("p (i e) -> p i e", i=NT)
                v(V.tensor_reduce(amx[:, :, 0:1], r, AX, ALU.max))
                out("r_sub", V.tensor_tensor(aff[:, :, :], r, amx[:, :, 0:1].to_broadcast([P, NT, EXPERTS]), ALU.subtract))
                dve.wait_ge(sem["r_exp"], l * INCS["r_exp"] + 1)
                v(V.tensor_reduce(amx[:, :, 1:2], aff[:, :, :], AX, ALU.add))
                v(V.reciprocal(amx[:, :, 0:1], amx[:, :, 1:2]))
                v(V.memset(aff_sp[:, :, :], -1.0))
                v(V.tensor_tensor(aff_sp[:, 0:4, 0:EXPERTS], aff[:, 0:4, :], amx[:, 0:4, 0:1].to_broadcast([P, 4, EXPERTS]), ALU.mult))
                out("aff_sp", V.tensor_tensor(aff_sp[:, 0, EXPERTS:32], aff[:, 4, :], amx[:, 4, 0:1].to_broadcast([P, EXPERTS]), ALU.mult))
                dve.wait_ge(sem["aff_tp"], l * INCS["aff_tp"] + 1)
                v(V.tensor_copy(affT[0:32, :], bank(3)[0:32, :]))
                for i in range(LCAP // 8):
                    t8, i8 = vals[0:32, 8 * i:8 * i + 8], idx_u[0:32, 8 * i:8 * i + 8].bitcast(U32)
                    for find in (lambda: V.max(t8, affT[0:32, :]), lambda: V.max_index(i8, t8, affT[0:32, :]),
                                 lambda: V.match_replace(affT[0:32, :], t8, affT[0:32, :], -2.0)):
                        V.tensor_copy(dummy[:, 3:4], ident[:, 0:1])
                        v(find())
                v(V.memset(tops_ctx[0:32, :, :], 0.0))
                for half in range(2):
                    v(V.tensor_copy(tops[0:32, 0, LCAP * half:LCAP * (half + 1)], idx_u[0:32, :].bitcast(U32)))
                    v(V.tensor_copy(tops[0:32, 1, LCAP * half:LCAP * (half + 1)], vals[0:32, :]))
                for half in range(2):
                    v(V.tensor_scalar(tops_ctx[0:32, 0, 32 * half:32 * half + CCAP], tops[0:32, 0, 0:CCAP], float(LAT), None, ALU.add))
                    out("idx_top", V.tensor_copy(tops_ctx[0:32, 1, 32 * half:32 * half + CCAP], vals[0:32, 0:CCAP]))
                dve.wait_ge(sem["slot_tp"], l * INCS["slot_tp"] + 1)
                st = bank(3)[:, 0:64].rearrange("p (a r) -> p a r", a=2)
                sc = bank(3)[:, 64:128].rearrange("p (a r) -> p a r", a=2)
                for a, (lat, ctx_) in enumerate(((id_lat, id_ctx), (gate_lat, gate_ctx))):
                    v(V.tensor_copy(lat[0:LCAP, :], st[0:LCAP, a, 0:EXPERTS:2]))
                    v(V.tensor_copy(lat[LCAP:P, :], st[LCAP:P, a, 1:EXPERTS:2]))
                    v(V.tensor_copy(ctx_[0:32, :], sc[0:32, a, EXPERTS:2 * EXPERTS:2]))
                    v(V.tensor_copy(ctx_[32:48, :], sc[32:48, a, EXPERTS + 1:2 * EXPERTS:2]))
                v(V.memset(ye_ctx[0:48, :], 0.0))
                out("xe_zero", V.memset(xe1[:, :, :], 0.0))
                dve.wait_ge(sem["idx_in"], l * INCS["idx_in"] + 32)

                def select(n, first=False):
                    if not first:
                        dve.wait_ge(sem["gather"], l * INCS["gather"] + n)
                    for t in range(4):
                        V.tensor_scalar(sel_lat[:, t, :], idx_lat[:, n, :], C("tokid")[:, t:t + 1], None, ALU.is_equal)
                    V.tensor_scalar(sel_ctx, idx_ctx[:, n, :], C("tokid")[:, 0:1], None, ALU.is_equal).then_inc(sem["sel"], 1)

                def select_T(n):
                    V.tensor_scalar(selT_lat, C("iota")[:, 0:LAT], id_lat[:, bass.ds(n, 1)],
                                    gate_lat[:, bass.ds(n, 1)], ALU.is_equal, ALU.mult)
                    V.tensor_scalar(selT_ctx[0:48, :], C("iota")[0:48, LAT:TOK], id_ctx[0:48, bass.ds(n, 1)],
                                    gate_ctx[0:48, bass.ds(n, 1)], ALU.is_equal, ALU.mult).then_inc(sem["selT"], 1)

                def hidden(e, odd):
                    m = P if odd else CAP
                    dve.wait_ge(sem["m_silu"], l * INCS["m_silu"] + e + 1)
                    V.tensor_tensor(he[0:m, :], sg[0:m, :], bank(2, 2)[0:m, :], ALU.mult).then_inc(sem["he"], 1)

                def accumulate(n):
                    for k in range(KD):
                        dve.wait_ge(sem["scatter"], l * INCS["scatter"] + KD * n - KD + k + 1)
                        b = (6, 4)[k % 2]
                        V.scalar_tensor_tensor(xT[:, k, 0:LAT], bank(b), mod[:, 40 + k, 0:1], xT[:, k, 0:LAT], ALU.mult, ALU.add)
                        V.scalar_tensor_tensor(xT[:, k, LAT:TOK], bank(b + 1)[:, 0:CTX], mod[:, 40 + k, 1:2], xT[:, k, LAT:TOK],
                                               ALU.mult, ALU.add).then_inc(sem["scattered"], 1)
                    dve.wait_ge(sem["scattered"], l * INCS["scattered"] + KD * n)

                select(0, True)
                select_T(0)
                hidden(0, False)
                select(1)
                hidden(1, True)
                with dve.Fori(1, PAIRS - 1) as i:
                    hidden(2 * i, False)
                    accumulate(i)
                    select_T(i)
                    select(i + 1)
                    hidden(2 * i + 1, True)
                hidden(EXPERTS - 2, False)
                accumulate(PAIRS - 1)
                select_T(PAIRS - 1)
                hidden(EXPERTS - 1, True)
                accumulate(PAIRS)
                assert count["vec_step"] == INCS["vec_step"], count["vec_step"]
                V.memset(dummy[:, 2:3], 0.0).then_inc(sem["layer_done"], 1)
                dve.wait_ge(sem["layer_done"], 4 * (l + 1))



def _layout(x):
    c = np.ascontiguousarray
    L = LAYERS

    def chunks(a):
        return a.reshape(L, -1, P).transpose(0, 2, 1)

    tokens = np.concatenate([x["x_sample"][0], x["x_prompt"][0]], 0)
    out = {"cst": _constants(), "xT": c(tokens.reshape(TOK, KD, P).transpose(2, 1, 0))}
    out["cond"] = c(np.stack([x["c"][0], x["c_ctx"]], 0).reshape(2, KD, P).transpose(2, 1, 0))
    par = np.zeros((L, P, PAR_N), np.float32)

    def put(name, a):
        lo, hi = PAR[name]
        par[:, :, lo:hi] = a.reshape(L, P, hi - lo)

    put("ada_b", chunks(x["ada_b"]))
    put("g1", chunks(x["norm1_g"]))
    put("g2", chunks(x["norm2_g"]))
    for name, key in (("na_q", "na_q_norm"), ("na_k", "na_k_norm"), ("sw_q", "swa_q_norm"), ("sw_k", "swa_k_norm")):
        put(name, np.concatenate([x[key], x[key]], 1))
    put("mu0", chunks(x["rw_mu"][:, 0]))
    put("mu1", chunks(x["rw_mu"][:, 1]))
    put("w0", chunks(x["rw_w0"].reshape(L, 512)))
    put("a0", chunks(x["rw_a0"].reshape(L, 512)))
    for name, key in (("k_k", "rw_k_k"), ("k_a", "rw_k_a"), ("r_k", "rw_r_k"), ("ln_g", "rw_ln_g"), ("ln_b", "rw_ln_b")):
        put(name, chunks(x[key].reshape(L, 256)))
    put("sink", np.broadcast_to(x["swa_sink"][:, None, :], (L, P, 6)))
    put("w2", x["rw_w2"].reshape(L, P, 256))
    put("a2", x["rw_a2"].reshape(L, P, 256))
    put("lg2", x["rw_g2"])
    put("router", x["w_router"].reshape(L, KD, P, EXPERTS).transpose(0, 2, 1, 3))
    out["par"] = par
    w = x["w_in"]
    q_order = [h for i in range(3) for h in (i, i + 3)]
    qc = w[:, :, 2304:2688].reshape(L, D, 6, HD)[:, :, q_order].reshape(L, D, 384)
    def pieces(a, n):
        return c(a.reshape(L, KD, P, n, PIECE).transpose(0, 3, 2, 1, 4))

    w_in = np.concatenate([w[:, :, 0:768], qc, w[:, :, 2688:2816], w[:, :, 768:1152], w[:, :, 2816:2944], w[:, :, 1152:2304],
                           np.zeros((L, D, P), np.float32)], 2)
    out["w_in"] = pieces(w_in, W_IN_PIECES)
    out["ada_w"], out["w_out"] = pieces(x["ada_w"], ADA_PIECES), pieces(x["w_out"], OUT_PIECES)
    out["w_gate"], out["w_up"], out["w_down"] = c(x["w_gate"]), c(x["w_up"]), c(x["w_down"])
    table = np.zeros((L, 6, 16, 64), np.float32)
    table[:, :, 0:15, 16:47] = x["na_rpb"]
    out["rpb"] = c(table.reshape(L, 6, 1024)[:, :, ::-1])
    heads = np.concatenate([x["cache_na_k"][0], x["cache_swa_k"][0]], 1)
    out["kcache"] = c(heads.reshape(L, 4, 2, P, HD).transpose(0, 2, 4, 1, 3).reshape(L, P, 4, P))
    heads = np.concatenate([x["cache_na_v"][0], x["cache_swa_v"][0]], 1)
    out["vcache"] = c(heads.transpose(0, 2, 1, 3).reshape(L, P, 512))
    s = x["state_rwkv"][0].reshape(L, 2, 2, 2, HD, HD)
    out["state"] = c(s.transpose(0, 3, 5, 1, 2, 4).reshape(L, P, 2, 2, HD))
    return out


_OUTS = {"y": (P, KD, TOK), "nk": (LAYERS, P, 4, P), "nv": (LAYERS, P, 512), "ns": (LAYERS, P, 2, 2, HD),
         "vscr": (LAT, 384), "tops": (32, P)}


def _returned(r):
    L = LAYERS
    y = r["out_y"].transpose(2, 1, 0).reshape(TOK, D)
    k = r["out_nk"].reshape(L, 2, HD, 4, P).transpose(0, 3, 1, 4, 2).reshape(1, L, 8, P, HD)
    v = r["out_nv"].reshape(L, P, 8, HD).transpose(0, 2, 1, 3)[None]
    s = r["out_ns"].reshape(L, 2, HD, 2, 2, HD).transpose(0, 3, 4, 1, 5, 2).reshape(1, L, 2, 4, HD, HD)
    c = np.ascontiguousarray
    return c(y[None, LAT:]), c(y[None, :LAT]), c(k[:, :, 0:6]), c(v[:, :, 0:6]), c(k[:, :, 6:8]), c(v[:, :, 6:8]), c(s)


def kernel(**inputs):
    import concourse.bacc as bacc
    from concourse.bass_utils import run_bass_kernel_spmd as run
    arrays = _layout({k: np.asarray(v) for k, v in inputs.items()})
    nc = bacc.Bacc("TRN2", target_bir_lowering=False, num_devices=1)
    nc.disable_value_cache = True
    io = {n: nc.dram_tensor(f"in_{n}", a.shape, F32, kind="ExternalInput").ap() for n, a in arrays.items()}
    io.update({n: nc.dram_tensor(f"out_{n}", shape, F32, kind="ExternalOutput").ap() for n, shape in _OUTS.items()})
    program(nc, io)
    r = run(nc, [{f"in_{k}": v for k, v in arrays.items()}], core_ids=[0])
    return _returned(r.results[0])
```

```python
from contextlib import ExitStack

import numpy as np

import concourse.bass as bass
from concourse import mybir

F32 = mybir.dt.float32
U32 = mybir.dt.uint32
ALU = mybir.AluOpType
ACT = mybir.ActivationFunctionType
AX = mybir.AxisListType.X

P = 128
LAYERS = 2
D = 1024
KD = D // P
LAT, CTX = 512, 128
TOK = LAT + CTX
SEGMENTS = ((0, LAT), (LAT, TOK))
HD = 64
PAIRS_A = 3
RWC = 9
NT = TOK // P
EXPERTS = 16
LCAP, CCAP = 2 * LAT // EXPERTS, 2 * CTX // EXPERTS
CAP = LCAP + CCAP
FF = 1024
PAIRS = EXPERTS // 2
NEG = -1e30
DECAY = float(-np.exp(np.float32(-0.5)))

PIECE = 256
STREAM = 2
ADA_PIECES = 6 * D // PIECE
W_IN_PIECES = 12
OUT_PIECES = D // PIECE
RW_PIECES = 5
ADA_FIRST = 8
PIECES = W_IN_PIECES + OUT_PIECES + ADA_PIECES - ADA_FIRST
RING = 6
EXPERT_PIECES = 12
MULTIPLIED = RING + 8

def _columns(sizes):
    at, out = 0, {}
    for name, n in sizes:
        out[name] = (at, at + n)
        at += n
    return out, at

PAR, PAR_N = _columns([("ada_b", 48), ("g1", 8), ("g2", 8), ("na_q", 1), ("na_k", 1), ("sw_q", 1), ("sw_k", 1),
                       ("mu0", 9), ("mu1", 9), ("w0", 4), ("a0", 4), ("k_k", 2), ("k_a", 2), ("r_k", 2),
                       ("ln_g", 2), ("ln_b", 2), ("sink", 6), ("w2", 256), ("a2", 256), ("lg2", 256), ("router", 128)])
CST, CST_N = _columns([("ident", 128), ("ones", 128), ("bones", 128), ("rot", 128), ("scmask", 1024),
                       ("lv", 2 * 7 * 128), ("namask", 768), ("swmask", 512), ("iota", 640), ("tokid", 5),
                       ("cos", 512), ("sin", 512), ("eps", 2)])


def _constants():
    c = np.zeros((P, CST_N), np.float32)

    def put(name, a):
        lo, hi = CST[name]
        c[:, lo:hi] = np.asarray(a, np.float32).reshape(P, hi - lo)

    p, q = np.arange(P)[:, None], np.arange(P)[None]
    put("ident", p == q)
    put("ones", np.ones((P, P)))
    put("bones", p // HD == q // HD)
    put("rot", np.where((q % HD < 32) & (p == q + 32), -1.0, 0.0) + np.where((q % HD >= 32) & (p == q - 32), 1.0, 0.0))
    sc, lv = [], []
    for d in range(2):
        strict, incl = ((p < q), (p <= q)) if d == 0 else ((p > q), (p >= q))
        sc += [strict, incl, strict, incl]
        for i in range(7):
            s = 1 << i
            a, b = (p, q) if d == 0 else (q, p)
            lv.append((b // s == a // s + 1) & (a // s % 2 == 0))
    put("scmask", np.stack(sc, 1))
    put("lv", np.stack(lv, 1))
    na = []
    for j in (0, 1, 3):
        start = min(max(j * 16 - 8, 0), 32)
        qc = 16 * j + np.arange(P)[:, None] % 16
        kc = start + np.arange(256)[None] % 32
        cs = np.clip(qc - 8, 0, 48)
        na.append(np.where((kc >= cs) & (kc < cs + 16), 0.0, NEG))
    put("namask", np.stack(na, 1))
    z = np.zeros((P, P))
    put("swmask", np.concatenate([np.where(q >= p, 0.0, NEG), z, z, np.where(q <= p, 0.0, NEG)], 1))
    put("iota", np.broadcast_to(np.arange(TOK), (P, TOK)))
    put("tokid", np.arange(P)[:, None] + P * np.arange(NT)[None])
    inv = np.float32(10000.0) ** (-np.arange(16, dtype=np.float32) / np.float32(16))
    t = np.arange(LAT)
    ang = np.concatenate([inv[:, None] * (t // 64).astype(np.float32), inv[:, None] * (t % 64).astype(np.float32)], 0)
    put("cos", np.tile(np.cos(ang), (4, 1)))
    put("sin", np.tile(np.sin(ang), (4, 1)))
    put("eps", np.broadcast_to(np.array([1e-6, 64e-5]), (P, 2)))
    return c


ARENA = 26200
LEVELS = 6
N_ATT = 6 * 4 + 6 * 4 + 6 + 6
VEC_STEPS = 257
INCS = {
    "stream_used": PIECES, "ada_used": ADA_FIRST,
    "par_in": 16, "rpb_in": 16 * 48, "cache_in": 32, "state_in": 16, "vscr": 16,
    "vwin_in": 16 * 32, "out_kv": 48, "out_state": 16, "idx_out": 16, "idx_in": 32, 
    "sq": 2 * KD, "rst_s": 2, "h_ready": 2 * KD, "shift_a": RWC, "rw_lora": 1, "rw_le": 8, "rw_kk_sq": 2,
    "rw_kk_s": 2, "rw_fs": 2,
    "rw_fsq": 2, "nsq": 10, "nsr": 10, "att_p": N_ATT, "att_ptc": N_ATT, "r_exp": 1, "act_step": 1,
    "xe_in": PAIRS, "m_silu": EXPERTS, "he_t": EXPERTS, "ye": EXPERTS,
    "ada": 1, "ada_tp": 1, "sq_used": 2 * KD, "proj_done": RWC, "lora_mm": 10, "kk_mm": 2, 
    "rw_fm": 6,
    "qk_done": 10, "qk_norm": 10, "rope_mm": 4, "v_mm": 2 * NT, "att_s": N_ATT, "att_t": N_ATT, "att_o": N_ATT,
    "out_mm": KD, "router_mm": 1, "aff_tp": 1, "h_tp": 2 * NT, "slot_tp": 1, "gather": PAIRS, "ring_free": 2,
    "ring_used": EXPERT_PIECES * EXPERTS + RING, "he_tp": EXPERTS, "scatter": KD * PAIRS,
    "vec_step": VEC_STEPS, "ms": 2, "h_part": 2 * KD, "shifted": RWC, "rw_sig": 1, "rw_kk": 2, "rw_kk_m": 2,
    "rw_prep_done": 1, 
    "rw_y_all": 1, "rw_yc2": 2, "rw_var": 2, "rw_bonus": 1, "rw_final": 1, "qk_ms": 10, "qk_used": 10,
    "k_ctx": 4, "roped": 4, "v_done": 2 * NT, "att_m": N_ATT, "att_bias": 24, "att_r": N_ATT, "bias_zero": 2, "att_pn": N_ATT, "att_oc": N_ATT,
    "out_done": 2 * KD, "r_sub": 1, "aff_sp": 1, "h_tok": 2 * NT, "idx_top": 2,
    "sel": PAIRS, "selT": PAIRS, "he": EXPERTS, "scattered": KD * PAIRS, "xe_zero": 1,
}
INCS.update({f"stream{s}": 16 * PIECES // STREAM for s in range(STREAM)})
INCS.update({f"ring{s}": 16 * EXPERT_PIECES * EXPERTS // RING for s in range(RING)})
INCS.update({f"ada{s}": 16 * -(-(ADA_FIRST - s) // RING) for s in range(RING)})
for b in range(2):
    INCS.update({f"rw_{name}{b}": NT for name in ("sums", "exp", "in", "s0", "tp", "tpc", "dt", "d0", "w", "wc", "u", "uc", "os", "state")})
    INCS.update({f"rw_mod{b}": NT - 1, f"rw_modc{b}": NT - 1})
    INCS.update({f"rw_{name}{b}": NT * LEVELS for name in ("x", "y", "yc", "z")})
    INCS.update({f"rw_sc{b}": NT * 4, f"rw_masked{b}": NT * 4, f"rw_dd{b}": NT * (LEVELS + 1)})
ONCE = ("boot", "cond_e", "silu_step", "silu", "layer_done", "out_y")


def program(nc, io):
    with ExitStack() as ctx:
        def sb(name, shape, dt=F32):
            return ctx.enter_context(nc.sbuf_tensor(name, shape, dt))

        sem = {name: ctx.enter_context(nc.semaphore(name)) for name in (*INCS, *ONCE)}

        cst = sb("cst", [P, CST_N])
        par = sb("par", [P, PAR_N])
        xT = sb("xT", [P, KD, TOK])
        hT = sb("hT", [P, KD, TOK])
        mixT = sb("mixT", [P, KD, TOK])
        stream = sb("stream", [P, STREAM, KD, PIECE])
        condT = sb("condT", [P, KD, 2])
        condE = sb("condE", [P, KD, 2])
        silu = sb("silu", [P, KD, 2])
        mod = sb("mod", [P, 48, 2])
        gain1 = sb("gain1", [P, KD, 2])
        gain2 = sb("gain2", [P, KD, 2])
        small = sb("small", [P, 64])
        dummy = sb("token", [P, 4])
        arena = sb("arena", [P, ARENA])
        psum = ctx.enter_context(nc.psum_tensor("psum", [P, 4096], F32))

        def C(name):
            return cst[:, CST[name][0]:CST[name][1]]

        def PV(name, i=0, n=1):
            return par[:, PAR[name][0] + i:PAR[name][0] + i + n]

        def bank(i, n=1):
            return psum[:, 512 * i:512 * (i + n)]

        def carve(at, *shape):
            n = int(np.prod(shape))
            assert at[0] + n <= ARENA, (at[0], n)
            v = arena[:, at[0]:at[0] + n]
            at[0] += n
            if len(shape) == 2:
                return v.rearrange("p (a b) -> p a b", a=shape[0])
            if len(shape) == 3:
                return v.rearrange("p (a b c) -> p a b c", a=shape[0], b=shape[1])
            if len(shape) == 4:
                return v.rearrange("p (a b c d) -> p a b c d", a=shape[0], b=shape[1], c=shape[2])
            return v

        ident, ones, bones = C("ident"), C("ones"), C("bones")
        scmask = C("scmask").rearrange("p (d n) -> p d n", d=2)
        lv = C("lv").rearrange("p (d s n) -> p d s n", d=2, s=7)
        namask = C("namask").rearrange("p (d n) -> p d n", d=3)

        mu_c = small[:, 8:17]
        one_ka, two_ka = small[:, 17:19], small[:, 19:21]
        naq8, swq8 = small[:, 21:22], small[:, 22:23]
        neg_sink = small[:, 24:30]

        at = [0]
        rT, kT, vT, kkT = (carve(at, 2, TOK) for _ in range(4))
        gT, yT = mixT[:, 0:2, :], mixT[:, 5:7, :]
        ldT, aT = carve(at, 2, 2, TOK), carve(at, 2, 2, TOK)
        rw_common = at[0]
        lora = carve(at, 3, TOK)
        scr = carve(at, 2, TOK)
        at = [rw_common]
        Wc, Wm, Ec = (carve(at, 2, P) for _ in range(3))
        eR, eA, eB = (carve(at, 2, P) for _ in range(3))
        Stmp = carve(at, 2, HD)

        class Unit:
            def __init__(self, b):
                self.AR = carve(at, 2, 2, 2 * P).rearrange("p u a (b t) -> p u a b t", b=2)
                self.e12 = carve(at, 2, 2, 2)
                self.BK = carve(at, 2, 2, P)
                self.BKt = carve(at, 2, 2 * P)
                self.Vt = carve(at, 2 * P)
                self.SC = carve(at, 4, 4 * P)
                self.X = carve(at, 4, P)
                x = self.X[:, :, :].rearrange("p h t -> p (h t)")
                self.W, self.U = x[:, 0:4 * HD], x[:, 4 * HD:8 * HD]
                self.Y = carve(at, 4, P)
                self.DD = carve(at, 4, 2, P)
                self.S0 = carve(at, 2, HD)
                self.banks = 4 * b

            def bank(self, i, n=1):
                return bank(self.banks + i, n)

        UNIT = [Unit(b) for b in range(2)]
        state = carve(at, 4, 2, HD)
        rw_end = at[0]

        at = [0]
        qa, ka, qc = (carve(at, 3, TOK) for _ in range(3))
        kc = carve(at, TOK)
        vtok = carve(at, NT, 512)
        vwin = carve(at, 8, 384)
        rpb = carve(at, 6, 512)
        kcache = carve(at, 4, P)
        vcache = carve(at, 512)
        nrm = carve(at, 2, TOK)
        swap = carve(at, LAT)
        Ssb, Pb, PT = carve(at, 2, 516), carve(at, 3, 516), carve(at, 2, 516)
        bias = carve(at, 2, 384)
        stats = carve(at, 4, 4)
        att_end = at[0]

        at = [0]
        ring = carve(at, RING, 2, FF)
        ada_ring = arena[:, 0:RING * KD * PIECE].rearrange("p (s k c) -> p s k c", s=RING, k=KD)
        moe_common = at[0]
        xe0, xe1 = carve(at, KD, CAP), carve(at, KD, P)
        routing = at[0]
        sg, he = carve(at, FF), carve(at, FF)
        heT = carve(at, KD, P)
        ye_lat, ye_ctx = carve(at, D), carve(at, D)
        selT_lat, selT_ctx = carve(at, LAT), carve(at, CTX)
        sel_lat, sel_ctx = carve(at, 4, P), carve(at, 2 * CCAP)
        idx_lat, idx_ctx = carve(at, PAIRS, P), carve(at, PAIRS, 2 * CCAP)
        id_lat, gate_lat, id_ctx, gate_ctx = (carve(at, PAIRS) for _ in range(4))
        moe_end, at = at[0], [routing]
        aff_sp = carve(at, 4, 32)
        aff = carve(at, NT, EXPERTS)
        amx = carve(at, NT, 2)
        affT = carve(at, 512)
        tops = carve(at, 2, P)
        tops_ctx = carve(at, 2, 48)
        idx_u = carve(at, LCAP)
        vals = carve(at, LCAP)
        at = [ARENA - 3 * TOK]
        assert at[0] >= moe_common
        sq, rst = carve(at, 2, TOK), carve(at, TOK)
        htok = mixT[:, :, :].rearrange("p k t -> p (k t)").rearrange("p (i d) -> p i d", i=NT)

        block = ctx.enter_context(nc.Block())

        RW_STEPS = ["transpose", "scores", "first"] + [x for i in range(LEVELS) for x in (("Y", i), ("Z", i))] + ["W", "U", "out"]
        RW_AHEAD = {("Z", 1): "sums", ("Z", 2): "products", ("Z", 3): "factors"}
        RW_ORDER = [(b, 0, step) for b in range(2) for step in RW_AHEAD.values()]
        for t in range((NT * 2 + 1) * len(RW_STEPS) // 2):
            for b in range(2):
                n, k = divmod(t - b * (len(RW_STEPS) // 2), len(RW_STEPS))
                if 0 <= n < NT:
                    RW_ORDER.append((b, n, RW_STEPS[k]))
                    if RW_STEPS[k] in RW_AHEAD and n + 1 < NT:
                        RW_ORDER.append((b, n + 1, RW_AHEAD[RW_STEPS[k]]))
        ada_rows = (mixT[:, 2, 0:512], mixT[:, 7, 0:512])
        RW_STATE = [[0, 0, 0, 0, 1], [2, 2, 2, 2, 3]]
        RW_TILE = [[0, 1, 2, 3, 4], [3, 2, 1, 0, 4]]

        ATT = []
        for h in range(6):
            for j in range(4):
                ATT.append(("na", h, j))
        for i in range(3):
            for g in range(2):
                for b in range(4):
                    ATT.append(("sw", i + 3 * g, b))
        for h in range(6):
            ATT.append(("cna", h, 0))
        for h in range(6):
            ATT.append(("csw", h, 0))

        def width(u):
            kind, h, j = u
            return {"na": 384, "sw": 384 if j in (0, 3) else 512}.get(kind, 128)

        @block.sync
        def _(sp):
            for dst, src in ((cst[:, :], io["cst"]), (xT[:, :, :], io["xT"]), (condT[:, :, :], io["cond"])):
                sp.dma_start(dst, src).then_inc(sem["boot"], 16)
            with sp.Fori(0, LAYERS) as l:
                sp.wait_ge(sem["ring_free"], l * INCS["ring_free"] + 2)
                sp.dma_start(par[:, :], io["par"][l]).then_inc(sem["par_in"], 16)
                for i in range(ADA_FIRST):
                    if i >= RING:
                        sp.wait_ge(sem["ada_used"], l * INCS["ada_used"] + i - RING + 1)
                    sp.dma_start(ada_ring[:, i % RING, :, :], io["ada_w"][l, i]).then_inc(sem[f"ada{i % RING}"], 16)
                n = 0

                def piece(name, i):
                    nonlocal n
                    if n >= STREAM:
                        sp.wait_ge(sem["stream_used"], l * INCS["stream_used"] + n - STREAM + 1)
                    sp.dma_start(stream[:, n % STREAM, :, :], io[name][l, i]).then_inc(sem[f"stream{n % STREAM}"], 16)
                    n += 1

                for i in range(RW_PIECES):
                    piece("w_in", W_IN_PIECES - RW_PIECES + i)
                for i in range(STREAM):
                    piece("ada_w", ADA_FIRST + i)
                sp.wait_ge(sem["rw_prep_done"], l * INCS["rw_prep_done"] + 1)
                sp.dma_start(state[:, 0:3:2, :, :], io["state"][l]).then_inc(sem["state_in"], 16)
                for i in range(ADA_FIRST + STREAM, ADA_PIECES):
                    piece("ada_w", i)
                order = [5, 6, 0, 1, 2, 3, 4]
                for i in order[:STREAM]:
                    piece("w_in", i)
                sp.wait_ge(sem["rw_final"], l * INCS["rw_final"] + 1)
                for b in range(2):
                    sp.wait_ge(sem[f"rw_state{b}"], l * INCS[f"rw_state{b}"] + NT)
                sp.dma_start(kcache[:, :, :], io["kcache"][l]).then_inc(sem["cache_in"], 16)
                sp.dma_start(vcache, io["vcache"][l]).then_inc(sem["cache_in"], 16)
                for h in range(6):
                    for r in range(8):
                        src = bass.AP(tensor=io["rpb"].tensor, offset=l * 6144 + 1024 * h + 64 * r + 49, ap=[[1, 16], [1, 512]])
                        sp.dma_start(rpb[16 * r:16 * r + 16, h, :], src).then_inc(sem["rpb_in"], 16)
                for i in order[STREAM:4]:
                    piece("w_in", i)
                for i in range(NT):
                    sp.wait_ge(sem["v_done"], l * INCS["v_done"] + 2 * (i + 1))
                sp.dma_start(io["vscr"].rearrange("(i p) c -> p i c", p=P), vtok[:, 0:4, 0:384]).then_inc(sem["vscr"], 16)
                sp.dma_start(io["nv"][l], vtok[:, 4, :]).then_inc(sem["out_kv"], 16)
                sp.wait_ge(sem["vscr"], l * INCS["vscr"] + 16)
                scr_v = io["vscr"].rearrange("(r c) f -> r c f", c=64)
                for j in range(4):
                    start = min(max(16 * j - 8, 0), 32)
                    for half in range(2):
                        for r in range(4):
                            sp.dma_start(vwin[32 * r:32 * r + 32, 2 * j + half, :],
                                                           scr_v[4 * half + r, start:start + 32, :]).then_inc(sem["vwin_in"], 16)
                for i in order[4:]:
                    piece("w_in", i)
                sp.wait_ge(sem["k_ctx"], l * INCS["k_ctx"] + 4)
                sp.dma_start(io["nk"][l][:, 0:3, :], ka[:, :, LAT:TOK]).then_inc(sem["out_kv"], 16)
                sp.dma_start(io["nk"][l][:, 3, :], kc[:, LAT:TOK]).then_inc(sem["out_kv"], 16)
                for i in range(OUT_PIECES):
                    piece("w_out", i)
                sp.wait_ge(sem["out_kv"], l * INCS["out_kv"] + 48)
                sp.wait_ge(sem["idx_top"], l * INCS["idx_top"] + 2)
                sp.dma_start(io["tops"], tops[0:32, 0, :]).then_inc(sem["idx_out"], 16)
                sp.wait_ge(sem["idx_out"], l * INCS["idx_out"] + 16)
                src = bass.AP(tensor=io["tops"].tensor, offset=0, ap=[[0, P], [P, EXPERTS], [1, LCAP]])
                sp.dma_start(idx_lat.rearrange("p e (h s) -> p (e h) s", h=2), src).then_inc(sem["idx_in"], 16)
                src = bass.AP(tensor=io["tops"].tensor, offset=EXPERTS * P, ap=[[0, P], [P, EXPERTS], [1, CCAP]])
                sp.dma_start(idx_ctx.rearrange("p e (h s) -> p (e h) s", h=2), src).then_inc(sem["idx_in"], 16)
                with sp.Fori(0, EXPERTS) as e:
                    for j in range(EXPERT_PIECES):
                        sp.wait_ge(sem["ring_used"], l * INCS["ring_used"] + e * EXPERT_PIECES + j + 1)
                        w, r = ("w_gate", j // 2) if j < 8 and j % 2 == 0 else ("w_up", j // 2) if j < 8 else ("w_down", j - 8)
                        sp.dma_start(ring[:, j % RING, :, :], io[w][l, e, 256 * r:256 * r + 256, :].rearrange("(k p) c -> p k c", p=P))\
                            .then_inc(sem[f"ring{j % RING}"], 16)
            sp.wait_ge(sem["layer_done"], 4 * LAYERS)
            sp.dma_start(io["y"], xT[:, :, :]).then_inc(sem["out_y"], 16)
            sp.wait_ge(sem["out_y"], 16)
            sp.wait_ge(sem["out_state"], 16 * LAYERS)
            sp.wait_ge(sem["out_kv"], 48 * LAYERS)
            sp.wait_ge(sem["idx_out"], 16 * LAYERS)
            sp.wait_ge(sem["vscr"], 16 * LAYERS)

        @block.gpsimd
        def _(pool):
            with pool.Fori(0, LAYERS) as l:
                for b, n, step in RW_ORDER:
                    g = UNIT[b]
                    if step == "first":
                        i = 0
                        pool.wait_ge(sem[f"rw_masked{b}"], l * INCS[f"rw_masked{b}"] + 4 * (n + 1))
                    elif step[0] == "Z" and step[1] < LEVELS - 1:
                        i = step[1] + 1
                        pool.wait_ge(sem[f"rw_y{b}"], l * INCS[f"rw_y{b}"] + LEVELS * n + i)
                    else:
                        continue
                    nc.gpsimd.tensor_tensor(g.X[:, :, :], g.SC[:, :, 0:P], lv[:, b, i + 1, :].unsqueeze(1).to_broadcast([P, 4, P]), ALU.mult)\
                        .then_inc(sem[f"rw_x{b}"], 1)
                for b in range(2):
                    pool.wait_ge(sem[f"rw_state{b}"], l * INCS[f"rw_state{b}"] + NT)
                nc.gpsimd.dma_start(io["ns"][l], state[:, 1:4:2, :, :]).then_inc(sem["out_state"], 16)
                pool.wait_ge(sem["out_state"], l * INCS["out_state"] + 16)
                pool.wait_ge(sem["v_done"], l * INCS["v_done"] + 1)
                for i in range(2):
                    nc.gpsimd.tensor_tensor(bias[:, i, 256:384], ident, C("swmask")[:, P:2 * P], ALU.mult).then_inc(sem["bias_zero"], 1)
                pool.wait_ge(sem["rpb_in"], l * INCS["rpb_in"] + 16 * 48)

                def bias_of(n):
                    kind, h, j = ATT[n]
                    if kind == "na":
                        if n >= 2:
                            pool.wait_ge(sem["att_m"], l * INCS["att_m"] + n - 1)
                        x0 = min(max(16 * j - 8, 0), 32) - 16 * j + 16
                        table = rpb[:, h, :].rearrange("p (r x) -> p r x", x=64)[:, ::-1, ::-1][:, :, x0:x0 + 32]
                        nc.gpsimd.tensor_tensor(bias[:, n % 2, 0:256].rearrange("p (r c) -> p r c", c=32), table,
                                                namask[:, (0, 1, 1, 2)[j], :].rearrange("p (r c) -> p r c", c=32), ALU.add).then_inc(sem["att_bias"], 1)

                def normalize(n):
                    w = width(ATT[n])
                    pool.wait_ge(sem["att_r"], l * INCS["att_r"] + n + 1)
                    nc.gpsimd.tensor_tensor(Pb[:, n % 3, 0:w], Pb[:, n % 3, 0:w], stats[:, n % 4, 2:3].to_broadcast([P, w]), ALU.mult)\
                        .then_inc(sem["att_pn"], 1)

                bias_of(0)
                for n in range(len(ATT) + 1):
                    if n + 1 < len(ATT):
                        bias_of(n + 1)
                    if n >= 1:
                        normalize(n - 1)
                nc.gpsimd.tensor_tensor(dummy[:, 0:1], ident[:, 0:1], ident[:, 0:1], ALU.mult).then_inc(sem["layer_done"], 1)
                pool.wait_ge(sem["layer_done"], 4 * (l + 1))

        @block.scalar
        def _(act):
            A = nc.scalar.activation
            act.wait_ge(sem["boot"], 48)
            A(condE[:, :, :], condT[:, :, :], ACT.Exp, scale=-1.0).then_inc(sem["cond_e"], 1)
            with act.Fori(0, LAYERS) as l:

                def norm(first):
                    for k in range(KD):
                        if k >= 2:
                            act.wait_ge(sem["sq_used"], l * INCS["sq_used"] + first * KD + k - 1)
                        A(sq[:, k % 2, :], xT[:, k, :], ACT.Square).then_inc(sem["sq"], 1)
                    act.wait_ge(sem["sq_used"], l * INCS["sq_used"] + KD * (first + 1))
                    A(rst, bank(0, 2)[:, 0:TOK], ACT.Ln, scale=1.0 / D, bias=C("eps")[:, 0:1]).then_inc(sem["ms"], 1)
                    act.wait_ge(sem["ms"], l * INCS["ms"] + first + 1)
                    A(rst, rst, ACT.Exp, scale=-0.5).then_inc(sem["rst_s"], 1)
                    gain, shift = ((gain1, 0), (gain2, 24))[first]
                    for k in range(KD):
                        act.wait_ge(sem["h_part"], l * INCS["h_part"] + first * KD + k + 1)
                        for cond, (lo, hi) in enumerate(SEGMENTS):
                            i = A(hT[:, k, lo:hi], hT[:, k, lo:hi], ACT.Identity, scale=gain[:, k, cond:cond + 1],
                                  bias=mod[:, shift + k, cond:cond + 1])
                        i.then_inc(sem["h_ready"], 1)

                norm(0)
                for c in range(RWC):
                    act.wait_ge(sem["proj_done"], l * INCS["proj_done"] + c + 1)
                    dst = (rT[:, c % 2, :], kT[:, c % 2, :], vT[:, c % 2, :])[c // 2] if c < 6 else lora[:, c - 6, :]
                    A(dst, bank(2 * (c % 2), 2)[:, 0:TOK], ACT.Identity, scale=mu_c[:, c:c + 1]).then_inc(sem["shift_a"], 1)
                act.wait_ge(sem["shifted"], l * INCS["shifted"] + RWC)
                A(lora[:, 0, :], lora[:, 0, :], ACT.Tanh).then_inc(sem["rw_lora"], 1)
                A(lora[:, 2, :], lora[:, 2, :], ACT.Sigmoid).then_inc(sem["rw_sig"], 1)
                for g in range(8):
                    act.wait_ge(sem["lora_mm"], l * INCS["lora_mm"] + g + 1)
                    dst, bias = ((ldT, "w0"), (aT, "a0"))[g // 4]
                    i = g % 4
                    A(dst[:, i // 2, i % 2, :], bank(2 * (g % 2), 2)[:, 0:TOK], ACT.Sigmoid, bias=PV(bias, i)).then_inc(sem["rw_le"], 1)
                act.wait_ge(sem["rw_kk"], l * INCS["rw_kk"] + 2)
                for p in range(2):
                    A(scr[:, p, :], kkT[:, p, :], ACT.Square).then_inc(sem["rw_kk_sq"], 1)
                act.wait_ge(sem["rw_kk_m"], l * INCS["rw_kk_m"] + 2)
                A(scr[:, :, :], scr[:, :, :], ACT.Ln, scale=2.0 ** 20).then_inc(sem["rw_kk_s"], 1)
                act.wait_ge(sem["rw_kk_s"], l * INCS["rw_kk_s"] + 1)
                A(scr[:, :, :], scr[:, :, :], ACT.Exp, scale=-0.5).then_inc(sem["rw_kk_s"], 1)
                for b, n, step in RW_ORDER:
                    g = UNIT[b]
                    if step == "sums":
                        act.wait_ge(sem[f"rw_sums{b}"], l * INCS[f"rw_sums{b}"] + n + 1)
                        A(g.e12[:, n % 2, 0, :].unsqueeze(2), Wc[:, :, 63:64], ACT.Exp)
                        A(g.e12[:, n % 2, 1, :].unsqueeze(2), Wm[:, :, P - 1:P], ACT.Exp)
                        for dst, src, sign in (((eR, Wm, 1.0), (eB, Wm, -1.0), (eA, Ec, 1.0)) if b == 0 else
                                               ((eR, Ec, -1.0), (eB, Ec, 1.0), (eA, Wm, -1.0))):
                            i = A(dst[:, :, :], src[:, :, :], ACT.Exp, scale=sign)
                        i.then_inc(sem[f"rw_exp{b}"], 1)
                    elif step == "transpose":
                        if n:
                            m = 2 * (n - 1) + b
                            rows = slice(32 * (m % 4), 32 * (m % 4) + 2)
                            act.wait_ge(sem[f"rw_mod{b}"], l * INCS[f"rw_mod{b}"] + n)
                            nc.scalar.copy(ada_rows[m // 4][rows, :], g.bank(2)[rows, :]).then_inc(sem[f"rw_modc{b}"], 1)
                        act.wait_ge(sem[f"rw_tp{b}"], l * INCS[f"rw_tp{b}"] + n + 1)
                        nc.scalar.copy(g.BKt[:, :, :].rearrange("p a b -> p (a b)"), g.bank(0))
                        nc.scalar.copy(g.Vt, g.bank(1)[:, 0:2 * P]).then_inc(sem[f"rw_tpc{b}"], 1)
                    elif step[0] == "Y":
                        act.wait_ge(sem[f"rw_y{b}"], l * INCS[f"rw_y{b}"] + LEVELS * n + step[1] + 1)
                        nc.scalar.copy(g.Y[:, :, :].rearrange("p a b -> p (a b)"), g.bank(0)).then_inc(sem[f"rw_yc{b}"], 1)
                    elif step == "W":
                        act.wait_ge(sem[f"rw_w{b}"], l * INCS[f"rw_w{b}"] + n + 1)
                        for h in range(2):
                            i = nc.scalar.copy(g.W.rearrange("p (a b v) -> p a b v", a=2, b=2)[:, :, h, :],
                                               g.bank(1 + h)[:, 0:P].rearrange("p (a v) -> p a v", a=2))
                        i.then_inc(sem[f"rw_wc{b}"], 1)
                    elif step == "U":
                        act.wait_ge(sem[f"rw_u{b}"], l * INCS[f"rw_u{b}"] + n + 1)
                        nc.scalar.copy(g.U, g.bank(3)[:, 0:256]).then_inc(sem[f"rw_uc{b}"], 1)
                for p in range(2):
                    act.wait_ge(sem["rw_yc2"], l * INCS["rw_yc2"] + p + 1)
                    A(scr[:, p, :], yT[:, p, :], ACT.Square).then_inc(sem["rw_fsq"], 1)
                for p in range(2):
                    act.wait_ge(sem["rw_fm"], l * INCS["rw_fm"] + 3 + p)
                    A(scr[:, p, :], bank(4 + 2 * p, 2)[:, 0:TOK], ACT.Ln, scale=1.0 / HD, bias=C("eps")[:, 1:2]).then_inc(sem["rw_var"], 1)
                    act.wait_ge(sem["rw_var"], l * INCS["rw_var"] + p + 1)
                    A(scr[:, p, :], scr[:, p, :], ACT.Exp, scale=-0.5).then_inc(sem["rw_fs"], 1)
                act.wait_ge(sem["out_state"], l * INCS["out_state"] + 16)
                for c in range(10):
                    act.wait_ge(sem["qk_done"], l * INCS["qk_done"] + c + 1)
                    if c >= 2:
                        act.wait_ge(sem["qk_used"], l * INCS["qk_used"] + c - 1)
                    A(nrm[:, c % 2, :], bank(2 * (c % 3), 2)[:, 0:TOK], ACT.Square).then_inc(sem["nsq"], 1)
                    act.wait_ge(sem["qk_norm"], l * INCS["qk_norm"] + c + 1)
                    A(nrm[:, c % 2, :], bank(6, 2)[:, 0:TOK], ACT.Ln, scale=1.0 / HD, bias=C("eps")[:, 0:1]).then_inc(sem["qk_ms"], 1)
                    act.wait_ge(sem["qk_ms"], l * INCS["qk_ms"] + c + 1)
                    A(nrm[:, c % 2, :], nrm[:, c % 2, :], ACT.Exp, scale=-0.5).then_inc(sem["nsr"], 1)
                def exp(n):
                    w = width(ATT[n]) + (ATT[n][0] in ("sw", "csw"))
                    act.wait_ge(sem["att_m"], l * INCS["att_m"] + n + 1)
                    if n >= 3:
                        act.wait_ge(sem["att_t"], l * INCS["att_t"] + n - 2)
                    A(Pb[:, n % 3, 0:w], Ssb[:, n % 2, 0:w], ACT.Exp, scale=-1.0, bias=stats[:, n % 4, 0:1],
                      accum_out=stats[:, n % 4, 1:2]).then_inc(sem["att_p"], 1)

                def pt(n):
                    w = width(ATT[n])
                    act.wait_ge(sem["att_t"], l * INCS["att_t"] + n + 1)
                    if n >= 2:
                        act.wait_ge(sem["att_o"], l * INCS["att_o"] + n - 1)
                    nc.scalar.copy(PT[:, n % 2, 0:w], bank(2 + n % 2)[:, 0:w]).then_inc(sem["att_ptc"], 1)

                for n in range(len(ATT) + 2):
                    if n < len(ATT):
                        exp(n)
                    if n >= 2:
                        pt(n - 2)
                act.wait_ge(sem["out_done"], l * INCS["out_done"] + 2 * KD)
                norm(1)
                act.wait_ge(sem["r_sub"], l * INCS["r_sub"] + 1)
                A(aff[:, :, :], aff[:, :, :], ACT.Exp).then_inc(sem["r_exp"], 1)
                for q in range(2 * NT):
                    act.wait_ge(sem["h_tp"], l * INCS["h_tp"] + q + 1)
                    nc.scalar.copy(htok[:, q // 2, 512 * (q % 2):512 * (q % 2) + 512], bank(4 + q % 2)).then_inc(sem["h_tok"], 1)
                gat = bank(6, 2).rearrange("p (k s) -> p k s", k=KD)
                gac = bank(4)[:, 0:256].rearrange("p (k s) -> p k s", k=KD)

                def gathered(n, used):
                    act.wait_ge(sem["gather"], l * INCS["gather"] + n)
                    if used is not None:
                        act.wait_ge(sem["ring_used"], l * INCS["ring_used"] + MULTIPLIED + EXPERT_PIECES * used)
                    nc.scalar.copy(xe0[:, :, 0:LCAP], gat[:, :, 0:LCAP])
                    nc.scalar.copy(xe0[:, :, LCAP:CAP], gac[:, :, 0:CCAP])
                    nc.scalar.copy(xe1[:, :, LCAP:P], gat[:, :, LCAP:P])
                    nc.scalar.copy(xe1[:, :, 0:CCAP], gac[:, :, CCAP:2 * CCAP]).then_inc(sem["xe_in"], 1)

                def expert(e, odd):
                    m = P if odd else CAP
                    act.wait_ge(sem["ring_used"], l * INCS["ring_used"] + MULTIPLIED + EXPERT_PIECES * e)
                    A(sg[0:m, :], bank(0, 2)[0:m, :], ACT.Silu).then_inc(sem["m_silu"], 1)

                def finish(e, odd):
                    m = P if odd else CAP
                    act.wait_ge(sem["he_tp"], l * INCS["he_tp"] + e + 1)
                    nc.scalar.copy(heT[:, :, 0:m], bank(0, 2).rearrange("p (k s) -> p k s", k=KD)[:, :, 0:m]).then_inc(sem["he_t"], 1)
                    act.wait_ge(sem["ring_used"], l * INCS["ring_used"] + RING + EXPERT_PIECES * (e + 1))
                    y = bank(4, 2)
                    if odd:
                        nc.scalar.copy(ye_lat[LCAP:P, :], y[LCAP:P, :])
                        nc.scalar.copy(ye_ctx[32:32 + CCAP, :], y[0:CCAP, :]).then_inc(sem["ye"], 1)
                    else:
                        nc.scalar.copy(ye_lat[0:LCAP, :], y[0:LCAP, :])
                        nc.scalar.copy(ye_ctx[0:CCAP, :], y[LCAP:CAP, :]).then_inc(sem["ye"], 1)

                act.wait_ge(sem["xe_zero"], l * INCS["xe_zero"] + 1)
                gathered(1, None)
                with act.Fori(0, PAIRS - 1) as i:
                    expert(2 * i, False)
                    finish(2 * i, False)
                    expert(2 * i + 1, True)
                    gathered(i + 2, 2 * i + 1)
                    finish(2 * i + 1, True)
                expert(EXPERTS - 2, False)
                finish(EXPERTS - 2, False)
                expert(EXPERTS - 1, True)
                finish(EXPERTS - 1, True)
                nc.scalar.copy(dummy[:, 1:2], C("ones")[:, 0:1]).then_inc(sem["act_step"], 1)
                act.wait_ge(sem["act_step"], l + 1)
                nc.scalar.copy(dummy[:, 1:2], C("ones")[:, 0:1]).then_inc(sem["layer_done"], 1)
                act.wait_ge(sem["layer_done"], 4 * (l + 1))

        @block.tensor
        def _(pe):
            mm = nc.tensor.matmul

            pe.wait_ge(sem["boot"], 48)
            mm(psum[0:1, 3584:3586], ident[:, 0:1], ident[:, 0:2], start=True, stop=True).then_inc(sem["ring_free"], 2)
            with pe.Fori(0, LAYERS) as l:
                pe.wait_ge(sem["par_in"], l * INCS["par_in"] + 16)
                n = 0

                def arrived():
                    nonlocal n
                    pe.wait_ge(sem[f"stream{n % STREAM}"], l * INCS[f"stream{n % STREAM}"] + 16 * (n // STREAM + 1))
                    n += 1
                    return (n - 1) % STREAM

                pe.wait_ge(sem["silu"], 1)
                def modulation(weights, o):
                    for j in range(2):
                        for k in range(KD):
                            last = mm(o[:, 2 * j:2 * j + 2], weights[:, k, j * P:(j + 1) * P], silu[:, k, :], start=k == 0, stop=k == KD - 1)
                    return last

                for i in range(ADA_FIRST):
                    pe.wait_ge(sem[f"ada{i % RING}"], l * INCS[f"ada{i % RING}"] + 16 * (i // RING + 1))
                    modulation(ada_ring[:, i % RING, :, :], bank(4)[:, 4 * i:4 * i + 4]).then_inc(sem["ada_used"], 1)
                mm(psum[0:1, 3072:3074], ident[:, 0:1], ident[:, 0:2], start=True, stop=True).then_inc(sem["ada"], 1)

                def norm(first):
                    for k in range(KD):
                        pe.wait_ge(sem["sq"], l * INCS["sq"] + first * KD + k + 1)
                        for lo, hi in SEGMENTS:
                            last = mm(bank(0, 2)[:, lo:hi], ones, sq[:, k % 2, lo:hi], start=k == 0, stop=k == KD - 1)
                        last.then_inc(sem["sq_used"], 1)

                norm(0)
                pe.wait_ge(sem["h_ready"], l * INCS["h_ready"] + KD)
                c = 0
                for i in range(RW_PIECES):
                    s = arrived()
                    for j in range(2 if i < RW_PIECES - 1 else 1):
                        if c >= 2:
                            pe.wait_ge(sem["shifted"], l * INCS["shifted"] + c - 1)
                        else:
                            pe.wait_ge(sem["ms"], l * INCS["ms"] + 1)
                        for lo, hi in SEGMENTS:
                            for k in range(KD):
                                last = mm(bank(2 * (c % 2), 2)[:, lo:hi], stream[:, s, k, j * P:(j + 1) * P], hT[:, k, lo:hi],
                                          start=k == 0, stop=k == KD - 1)
                        last.then_inc(sem["proj_done"], 1)
                        c += 1
                    mm(psum[0:1, 3072:3074], ident[:, 0:1], ident[:, 0:2], start=True, stop=True).then_inc(sem["stream_used"], 1)
                pe.wait_ge(sem["rw_lora"], l * INCS["rw_lora"] + 1)
                pe.wait_ge(sem["shifted"], l * INCS["shifted"] + RWC)
                for g in range(8):
                    d, p = g % 4 // 2, g % 2
                    w = PAR["w2" if g < 4 else "a2"][0] + p * P
                    if g >= 2:
                        pe.wait_ge(sem["rw_le"], l * INCS["rw_le"] + g - 1)
                    for lo, hi in SEGMENTS:
                        last = mm(bank(2 * (g % 2), 2)[:, lo:hi], par[HD * d:HD * d + HD, w:w + P],
                                  lora[HD * d:HD * d + HD, g // 4, lo:hi], start=True, stop=True)
                    last.then_inc(sem["lora_mm"], 1)
                pe.wait_ge(sem["rw_sig"], l * INCS["rw_sig"] + 1)
                for p in range(2):
                    w = PAR["lg2"][0] + p * P
                    pe.wait_ge(sem["rw_le"], l * INCS["rw_le"] + 7 + p)
                    for lo, hi in SEGMENTS:
                        last = mm(bank(2 * p, 2)[:, lo:hi], par[:, w:w + P], lora[:, 2, lo:hi], start=True, stop=True)
                    last.then_inc(sem["lora_mm"], 1)
                for p in range(2):
                    pe.wait_ge(sem["rw_kk_sq"], l * INCS["rw_kk_sq"] + p + 1)
                    for lo, hi in SEGMENTS:
                        last = mm(bank(4 + 2 * p, 2)[:, lo:hi], bones, scr[:, p, lo:hi], start=True, stop=True)
                    last.then_inc(sem["kk_mm"], 1)
                slot = None

                def modulation_rows(b, n_, first, end):
                    nonlocal slot
                    if n_ == NT - 1:
                        return
                    at_ = 32 * ((2 * n_ + b) % 4)
                    for i in range(first, end):
                        k = i % KD
                        if k == 0:
                            slot = arrived()
                        last = mm(UNIT[b].bank(2)[at_:at_ + 2, PIECE * (i // KD):PIECE * (i // KD + 1)], silu[:, k, :], stream[:, slot, k, :],
                                  start=k == 0, stop=k == KD - 1)
                        if k == KD - 1:
                            last.then_inc(sem["stream_used"], 1)
                    if end == 2 * KD:
                        carrier(b).then_inc(sem[f"rw_mod{b}"], 1)

                def carrier(b):
                    return mm(UNIT[b].bank(1)[0:1, 0:2], ident[:, 0:1], ident[:, 0:2], start=True, stop=True)

                for b, n_, step in RW_ORDER:
                    g = UNIT[b]
                    if step == "transpose":
                        if n_:
                            pe.wait_ge(sem[f"rw_state{b}"], l * INCS[f"rw_state{b}"] + n_)
                        pe.wait_ge(sem[f"rw_in{b}"], l * INCS[f"rw_in{b}"] + n_ + 1)
                        for i in range(4):
                            nc.tensor.transpose(g.bank(0)[:, P * i:P * i + P], g.BK[:, i // 2, i % 2, :], ident)
                        for p in range(2):
                            last = nc.tensor.transpose(g.bank(1)[:, P * p:P * p + P], vT[:, p, P * RW_TILE[b][n_]:P * RW_TILE[b][n_] + P], ident)
                        last.then_inc(sem[f"rw_tp{b}"], 1)
                    elif step == "scores":
                        if n_:
                            pe.wait_ge(sem[f"rw_modc{b}"], l * INCS[f"rw_modc{b}"] + n_)
                        for h in range(4):
                            hb, p = HD * (h % 2), h // 2
                            if h >= 2:
                                pe.wait_ge(sem[f"rw_masked{b}"], l * INCS[f"rw_masked{b}"] + 4 * n_ + h - 1)
                            rhs = g.AR[hb:hb + HD, n_ % 2, p, :, :].rearrange("p a t -> p (a t)")
                            mm(g.bank(2 + h % 2)[:, 0:256], g.BK[hb:hb + HD, 0, p, :], rhs, start=True, stop=True)
                            mm(g.bank(2 + h % 2)[:, 256:512], g.BK[hb:hb + HD, 1, p, :], rhs, start=True, stop=True).then_inc(sem[f"rw_sc{b}"], 1)
                    elif step == "first":
                        pe.wait_ge(sem[f"rw_tpc{b}"], l * INCS[f"rw_tpc{b}"] + n_ + 1)
                        pe.wait_ge(sem[f"rw_dt{b}"], l * INCS[f"rw_dt{b}"] + n_ + 1)
                        for h in range(4):
                            last = nc.tensor.transpose(g.bank(0)[:, P * h:P * h + P], g.DD[:, h, 1, :], ident)
                        last.then_inc(sem[f"rw_d0{b}"], 1)
                    elif step[0] == "Y":
                        i = step[1]
                        pe.wait_ge(sem[f"rw_dd{b}"], l * INCS[f"rw_dd{b}"] + (LEVELS + 1) * n_ + i + 1)
                        pe.wait_ge(sem[f"rw_x{b}"], l * INCS[f"rw_x{b}"] + LEVELS * n_ + i + 1)
                        for h in range(4):
                            last = mm(g.bank(0)[:, P * h:P * h + P], g.X[:, h, :], g.DD[:, h, 0, :], start=True, stop=True)
                        last.then_inc(sem[f"rw_y{b}"], 1)
                    elif step[0] == "Z":
                        i = step[1]
                        pe.wait_ge(sem[f"rw_yc{b}"], l * INCS[f"rw_yc{b}"] + LEVELS * n_ + i + 1)
                        for h in range(4):
                            z = g.bank(1, 2)[:, 256 * h:256 * h + 256]
                            if i < LEVELS - 1:
                                mm(z[:, 0:P], g.DD[:, h, 1, :], g.Y[:, h, :], start=True, stop=True)
                            last = mm(z[:, P:2 * P], g.Y[:, h, :], g.DD[:, h, 1, :], start=True, stop=True)
                        last.then_inc(sem[f"rw_z{b}"], 1)
                    elif step == "W":
                        pe.wait_ge(sem[f"rw_dd{b}"], l * INCS[f"rw_dd{b}"] + (LEVELS + 1) * (n_ + 1))
                        pe.wait_ge(sem[f"rw_s0{b}"], l * INCS[f"rw_s0{b}"] + n_ + 1)
                        for h in range(4):
                            hb, p = HD * (h % 2), h // 2
                            o = g.bank(1 + h % 2)[:, HD * p:HD * p + HD]
                            mm(o, g.AR[hb:hb + HD, n_ % 2, p, 0, :], g.S0[hb:hb + HD, p, :], start=True, stop=False)
                            last = mm(o, g.SC[:, h, 2 * P:3 * P], g.Vt[:, HD * h:HD * h + HD], start=False, stop=True)
                        last.then_inc(sem[f"rw_w{b}"], 1)
                    elif step == "U":
                        pe.wait_ge(sem[f"rw_wc{b}"], l * INCS[f"rw_wc{b}"] + n_ + 1)
                        for h in range(4):
                            last = mm(g.bank(3)[:, HD * h:HD * h + HD], g.DD[:, h, 1, :], g.W[:, HD * h:HD * h + HD], start=True, stop=True)
                        last.then_inc(sem[f"rw_u{b}"], 1)
                        modulation_rows(b, n_, 0, 6)
                    elif step == "out":
                        pe.wait_ge(sem[f"rw_uc{b}"], l * INCS[f"rw_uc{b}"] + n_ + 1)
                        for h in range(4):
                            hb, p = HD * (h % 2), h // 2
                            o = g.bank(3)[hb:hb + HD, 256 + HD * p:256 + HD * p + HD]
                            mm(o, g.BKt[:, 0, HD * h:HD * h + HD], g.U[:, HD * h:HD * h + HD], start=True, stop=False)
                            mm(o, g.BKt[:, 1, HD * h:HD * h + HD], g.Vt[:, HD * h:HD * h + HD], start=False, stop=True)
                            o = g.bank(0)[hb:hb + HD, P * p:P * p + P]
                            mm(o, g.S0[hb:hb + HD, p, :], g.AR[hb:hb + HD, n_ % 2, p, 1, :], start=True, stop=False)
                            mm(o, g.U[:, HD * h:HD * h + HD], g.SC[:, h, P:2 * P], start=False, stop=False)
                            last = mm(o, g.Vt[:, HD * h:HD * h + HD], g.SC[:, h, 3 * P:4 * P], start=False, stop=True)
                        last.then_inc(sem[f"rw_os{b}"], 1)
                        modulation_rows(b, n_, 6, 2 * KD)
                def head_sums(src, b, name, v):
                    pe.wait_ge(sem[name], l * INCS[name] + v)
                    for lo, hi in SEGMENTS:
                        last = mm(bank(b, 2)[:, lo:hi], bones, src[:, lo:hi], start=True, stop=True)
                    last.then_inc(sem["rw_fm"], 1)

                pe.wait_ge(sem["rw_y_all"], l * INCS["rw_y_all"] + 1)
                for i in range(8):
                    last = nc.tensor.transpose(bank(0, 2)[:, P * i:P * i + P], ada_rows[i // 4][:, P * (i % 4):P * (i % 4) + P], ident)
                last.then_inc(sem["ada_tp"], 1)
                for p in range(2):
                    head_sums(yT[:, p, :], 4 + 2 * p, "rw_y_all", 1)
                for p in range(2):
                    head_sums(scr[:, p, :], 4 + 2 * p, "rw_fsq", p + 1)
                for p in range(2):
                    head_sums(kT[:, p, :], 2 * p, "rw_bonus", 1)
                pe.wait_ge(sem["rw_final"], l * INCS["rw_final"] + 1)
                slots_v = [arrived(), arrived()]
                v = 0
                for i in range(NT):
                    for j in range(2):
                        if v >= 2:
                            pe.wait_ge(sem["v_done"], l * INCS["v_done"] + v - 1)
                        for k in range(KD):
                            last = mm(bank(v % 2)[:, 0:PIECE], hT[:, k, i * P:(i + 1) * P], stream[:, slots_v[j], k, :],
                                      start=k == 0, stop=k == KD - 1)
                        last.then_inc(sem["v_mm"], 1)
                        v += 1
                for _ in range(2):
                    mm(psum[0:1, 3584:3586], ident[:, 0:1], ident[:, 0:2], start=True, stop=True).then_inc(sem["stream_used"], 1)
                c = 0

                def qk_norm(c):
                    pe.wait_ge(sem["nsq"], l * INCS["nsq"] + c + 1)
                    if c >= 1:
                        pe.wait_ge(sem["qk_ms"], l * INCS["qk_ms"] + c)
                    for lo, hi in SEGMENTS:
                        last = mm(bank(6, 2)[:, lo:hi], bones, nrm[:, c % 2, lo:hi], start=True, stop=True)
                        if c == 9 and lo == 0:
                            last.then_inc(sem["stream_used"], 1)
                    last.then_inc(sem["qk_norm"], 1)

                for i in range(5):
                    s = arrived()
                    for j in range(2):
                        if c >= 3:
                            pe.wait_ge(sem["qk_used"], l * INCS["qk_used"] + c - 2)
                        elif c == 0:
                            pe.wait_ge(sem["v_done"], l * INCS["v_done"] + 10)
                        for lo, hi in SEGMENTS:
                            for k in range(KD):
                                last = mm(bank(2 * (c % 3), 2)[:, lo:hi], stream[:, s, k, j * P:(j + 1) * P], hT[:, k, lo:hi],
                                          start=k == 0, stop=k == KD - 1)
                                if i and j == 0 and lo == 0 and k == 0:
                                    last.then_inc(sem["stream_used"], 1)
                        last.then_inc(sem["qk_done"], 1)
                        if c >= 1:
                            qk_norm(c - 1)
                        c += 1
                qk_norm(9)
                pe.wait_ge(sem["qk_used"], l * INCS["qk_used"] + 10)
                for i in range(4):
                    dst = kc if i == 3 else qc[:, i, :]
                    mm(bank(i), C("rot"), dst[:, 0:LAT], start=True, stop=True).then_inc(sem["rope_mm"], 1)
                pe.wait_ge(sem["roped"], l * INCS["roped"] + 4)
                pe.wait_ge(sem["cache_in"], l * INCS["cache_in"] + 32)

                def scores(n):
                    kind, h, j = ATT[n]
                    o = bank(n % 2)
                    if n >= 2:
                        pe.wait_ge(sem["att_m"], l * INCS["att_m"] + n - 1)
                    if kind == "na":
                        hb, p = HD * (h % 2), h // 2
                        start = min(max(16 * j - 8, 0), 32)
                        q = qa[hb:hb + HD, p, P * j:P * j + P]
                        keys = ka[hb:hb + HD, p, 0:LAT].rearrange("p (r c) -> p r c", c=64)[:, :, start:start + 32]
                        mm(o[:, 0:256].rearrange("p (r c) -> p r c", c=32), q, keys, start=True, stop=True)
                        last = mm(o[:, 256:384], q, kcache[hb:hb + HD, p, :], start=True, stop=True)
                    elif kind == "cna":
                        hb, p = HD * (h % 2), h // 2
                        last = mm(o[:, 0:P], qa[hb:hb + HD, p, LAT:TOK], ka[hb:hb + HD, p, LAT:TOK], start=True, stop=True)
                    else:
                        g, i = h // 3, h % 3
                        hb = HD * g
                        if kind == "csw":
                            last = mm(o[:, 0:P], qc[hb:hb + HD, i, LAT:TOK], kc[hb:hb + HD, LAT:TOK], start=True, stop=True)
                        else:
                            q = qc[hb:hb + HD, i, P * j:P * j + P]
                            lo = max(j - 1, 0)
                            own = (j + 1 - lo) * P
                            mm(o[:, 0:own], q, kc[hb:hb + HD, lo * P:(j + 1) * P], start=True, stop=True)
                            last = mm(o[:, own:own + P], q, kcache[hb:hb + HD, 3, :], start=True, stop=True)
                            if j < 3:
                                last = mm(o[:, own + P:own + 2 * P], q, kc[hb:hb + HD, (j + 1) * P:(j + 2) * P], start=True, stop=True)
                    last.then_inc(sem["att_s"], 1)

                def values(n):
                    kind, h, j = ATT[n]
                    f = HD * h if kind in ("na", "cna") else 384 + HD * (h // 3)
                    if kind == "na":
                        return [vwin[:, 2 * j, f:f + HD], vwin[:, 2 * j + 1, f:f + HD], vcache[:, f:f + HD]]
                    if kind == "sw":
                        lo = max(j - 1, 0)
                        out = [vtok[:, b, f:f + HD] for b in range(lo, j + 1)] + [vcache[:, f:f + HD]]
                        return out + ([vtok[:, j + 1, f:f + HD]] if j < 3 else [])
                    return [vtok[:, 4, f:f + HD]]

                def probs_T(n):
                    pe.wait_ge(sem["att_pn"], l * INCS["att_pn"] + n + 1)
                    if n >= 2:
                        pe.wait_ge(sem["att_ptc"], l * INCS["att_ptc"] + n - 1)
                    for i in range(width(ATT[n]) // P):
                        last = nc.tensor.transpose(bank(2 + n % 2)[:, P * i:P * i + P], Pb[:, n % 3, P * i:P * i + P], ident)
                    last.then_inc(sem["att_t"], 1)

                def outputs(n):
                    kind, h, j = ATT[n]
                    hb = HD * (h % 2)
                    pe.wait_ge(sem["att_ptc"], l * INCS["att_ptc"] + n + 1)
                    if n >= 2:
                        pe.wait_ge(sem["att_oc"], l * INCS["att_oc"] + n - 1)
                    vs = values(n)
                    for i, v in enumerate(vs):
                        last = mm(bank(4 + n % 2)[hb:hb + HD, 0:P], v, PT[:, n % 2, P * i:P * i + P], start=i == 0, stop=i == len(vs) - 1)
                    last.then_inc(sem["att_o"], 1)

                for n_ in range(len(ATT) + 3):
                    if n_ < len(ATT):
                        scores(n_)
                    if 2 <= n_ < len(ATT) + 2:
                        probs_T(n_ - 2)
                    if n_ == 3:
                        pe.wait_ge(sem["vwin_in"], l * INCS["vwin_in"] + 16 * 32)
                    if n_ >= 3:
                        outputs(n_ - 3)
                pe.wait_ge(sem["att_oc"], l * INCS["att_oc"] + len(ATT))
                mm(psum[0:1, 3584:3586], ident[:, 0:1], ident[:, 0:2], start=True, stop=True).then_inc(sem["ring_used"], RING)
                c = 0
                for i in range(OUT_PIECES):
                    s = arrived()
                    for j in range(2):
                        if c >= 2:
                            pe.wait_ge(sem["out_done"], l * INCS["out_done"] + 2 * (c - 1))
                        for lo, hi in SEGMENTS:
                            for k in range(KD):
                                last = mm(bank(2 * (c % 2), 2)[:, lo:hi], stream[:, s, k, j * P:(j + 1) * P], mixT[:, k, lo:hi],
                                          start=k == 0, stop=k == KD - 1)
                        last.then_inc(sem["out_mm"], 1)
                        c += 1
                    mm(psum[0:1, 3584:3586], ident[:, 0:1], ident[:, 0:2], start=True, stop=True).then_inc(sem["stream_used"], 1)
                pe.wait_ge(sem["out_done"], l * INCS["out_done"] + 2 * KD)
                norm(1)
                pe.wait_ge(sem["h_ready"], l * INCS["h_ready"] + 2 * KD)
                router = par[:, PAR["router"][0]:PAR["router"][1]].rearrange("p (k e) -> p k e", k=KD)
                for i in range(NT):
                    for k in range(KD):
                        last = mm(bank(2)[:, EXPERTS * i:EXPERTS * (i + 1)], hT[:, k, i * P:(i + 1) * P], router[:, k, :],
                                  start=k == 0, stop=k == KD - 1)
                last.then_inc(sem["router_mm"], 1)
                for i in range(NT):
                    for j in range(2):
                        q = 2 * i + j
                        if q >= 2:
                            pe.wait_ge(sem["h_tok"], l * INCS["h_tok"] + q - 1)
                        for k in range(4):
                            last = nc.tensor.transpose(bank(4 + q % 2)[:, P * k:P * k + P], hT[:, 4 * j + k, i * P:(i + 1) * P], ident)
                        last.then_inc(sem["h_tp"], 1)
                pe.wait_ge(sem["aff_sp"], l * INCS["aff_sp"] + 1)
                for i in range(4):
                    last = nc.tensor.transpose(bank(3)[0:32, P * i:P * i + P], aff_sp[:, i, :], ident)
                last.then_inc(sem["aff_tp"], 1)
                pe.wait_ge(sem["idx_top"], l * INCS["idx_top"] + 2)
                mm(bank(2)[0:1, 0:2], ident[:, 0:1], ident[:, 0:2], start=True, stop=True)
                for i in range(2):
                    nc.tensor.transpose(bank(3)[:, 32 * i:32 * i + 32], tops[0:32, i, :], ident[0:32, 0:32])
                    last = nc.tensor.transpose(bank(3)[0:48, 64 + 32 * i:96 + 32 * i], tops_ctx[0:32, i, :], ident[0:32, 0:32])
                last.then_inc(sem["slot_tp"], 1)
                pe.wait_ge(sem["h_tok"], l * INCS["h_tok"] + 10)
                gat = bank(6, 2).rearrange("p (k s) -> p k s", k=KD)
                gac = bank(4)[:, 0:256].rearrange("p (k s) -> p k s", k=KD)
                heT_ps = bank(0, 2).rearrange("p (k s) -> p k s", k=KD)

                def gather(n):
                    pe.wait_ge(sem["sel"], l * INCS["sel"] + n)
                    for k in range(KD):
                        for i in range(4):
                            mm(gat[:, k, :], htok[:, i, k * P:(k + 1) * P], sel_lat[:, i, :], start=i == 0, stop=i == 3)
                        last = mm(gac[:, k, :], htok[:, 4, k * P:(k + 1) * P], sel_ctx, start=True, stop=True)
                    last.then_inc(sem["gather"], 1)

                def gate_up(e, odd):
                    m, x = (P, xe1) if odd else (CAP, xe0)
                    for j in range(8):
                        pe.wait_ge(sem[f"ring{j % RING}"], l * INCS[f"ring{j % RING}"] + 32 * e + 16 * (j // RING + 1))
                        for kk in range(2):
                            k = 2 * (j // 2) + kk
                            for f in range(2):
                                last = mm(bank(2 * (j % 2) + f)[0:m, :], x[:, k, 0:m], ring[:, j % RING, kk, 512 * f:512 * f + 512],
                                          start=k == 0, stop=k == KD - 1)
                        last.then_inc(sem["ring_used"], 1)

                def down(e, odd):
                    m = P if odd else CAP
                    pe.wait_ge(sem["he"], l * INCS["he"] + e + 1)
                    for k in range(KD):
                        last = nc.tensor.transpose(heT_ps[:, k, 0:m], he[0:m, k * P:(k + 1) * P], ident[0:m, 0:m])
                    last.then_inc(sem["he_tp"], 1)
                    pe.wait_ge(sem["he_t"], l * INCS["he_t"] + e + 1)
                    for j in range(8, EXPERT_PIECES):
                        pe.wait_ge(sem[f"ring{j % RING}"], l * INCS[f"ring{j % RING}"] + 32 * e + 16 * (j // RING + 1))
                        for kk in range(2):
                            k = 2 * (j - 8) + kk
                            for f in range(2):
                                last = mm(bank(4 + f)[0:m, :], heT[:, k, 0:m], ring[:, j % RING, kk, 512 * f:512 * f + 512],
                                          start=k == 0, stop=k == KD - 1)
                        last.then_inc(sem["ring_used"], 1)

                def scatter(n):
                    pe.wait_ge(sem["ye"], l * INCS["ye"] + 2 * n)
                    pe.wait_ge(sem["selT"], l * INCS["selT"] + n)
                    for k in range(KD):
                        b = (6, 4)[k % 2]
                        if k >= 2:
                            pe.wait_ge(sem["scattered"], l * INCS["scattered"] + KD * n - KD + k - 1)
                        mm(bank(b), ye_lat[:, k * P:(k + 1) * P], selT_lat, start=True, stop=True)
                        mm(bank(b + 1)[:, 0:CTX], ye_ctx[0:48, k * P:(k + 1) * P], selT_ctx[0:48, :], start=True, stop=True)\
                            .then_inc(sem["scatter"], 1)

                gather(1)
                pe.wait_ge(sem["xe_in"], l * INCS["xe_in"] + 1)
                gate_up(0, False)
                down(0, False)
                gate_up(1, True)
                pe.wait_ge(sem["ye"], l * INCS["ye"] + 1)
                gather(2)
                pe.wait_ge(sem["xe_in"], l * INCS["xe_in"] + 2)
                down(1, True)
                with pe.Fori(1, PAIRS - 1) as i:
                    gate_up(2 * i, False)
                    scatter(i)
                    pe.wait_ge(sem["scattered"], l * INCS["scattered"] + KD * i)
                    down(2 * i, False)
                    gate_up(2 * i + 1, True)
                    pe.wait_ge(sem["ye"], l * INCS["ye"] + 2 * i + 1)
                    gather(i + 2)
                    pe.wait_ge(sem["xe_in"], l * INCS["xe_in"] + i + 2)
                    down(2 * i + 1, True)
                gate_up(EXPERTS - 2, False)
                scatter(PAIRS - 1)
                pe.wait_ge(sem["scattered"], l * INCS["scattered"] + KD * (PAIRS - 1))
                down(EXPERTS - 2, False)
                gate_up(EXPERTS - 1, True)
                down(EXPERTS - 1, True)
                mm(psum[0:1, 3584:3586], ident[:, 0:1], ident[:, 0:2], start=True, stop=True).then_inc(sem["ring_free"], 2)
                scatter(PAIRS)
                pe.wait_ge(sem["scattered"], l * INCS["scattered"] + KD * PAIRS)
                mm(psum[0:1, 3584:3586], ident[:, 0:1], ident[:, 0:2], start=True, stop=True).then_inc(sem["layer_done"], 1)
                pe.wait_ge(sem["layer_done"], 4 * (l + 1))

        @block.vector
        def _(dve):
            V = nc.vector
            dve.wait_ge(sem["boot"], 48)
            dve.wait_ge(sem["cond_e"], 1)
            V.tensor_scalar(condE[:, :, :], condE[:, :, :], 1.0, None, ALU.add).then_inc(sem["silu_step"], 1)
            dve.wait_ge(sem["silu_step"], 1)
            V.reciprocal(condE[:, :, :], condE[:, :, :]).then_inc(sem["silu_step"], 1)
            dve.wait_ge(sem["silu_step"], 2)
            V.tensor_tensor(silu[:, :, :], condT[:, :, :], condE[:, :, :], ALU.mult).then_inc(sem["silu"], 1)
            with dve.Fori(0, LAYERS) as l:

                count = dict.fromkeys(INCS, 0)

                def v(ins):
                    count["vec_step"] += 1
                    ins.then_inc(sem["vec_step"], 1)
                    dve.wait_ge(sem["vec_step"], l * INCS["vec_step"] + count["vec_step"])

                def out(name, ins):
                    count[name] += 1
                    ins.then_inc(sem[name], 1)
                    dve.wait_ge(sem[name], l * INCS[name] + count[name])

                dve.wait_ge(sem["par_in"], l * INCS["par_in"] + 16)
                v(V.tensor_tensor(mu_c, PV("mu0", 0, 9), PV("mu1", 0, 9), ALU.add))
                v(V.tensor_scalar(mu_c, mu_c, -1.0, 1.0, ALU.mult, ALU.add))
                v(V.tensor_scalar(one_ka, PV("k_a", 0, 2), -1.0, 1.0, ALU.mult, ALU.add))
                v(V.tensor_scalar(two_ka, one_ka, 2.0, None, ALU.mult))
                v(V.tensor_scalar(naq8, PV("na_q"), 0.125, None, ALU.mult))
                v(V.tensor_scalar(swq8, PV("sw_q"), 0.125, None, ALU.mult))
                v(V.tensor_scalar(neg_sink, PV("sink", 0, 6), -1.0, None, ALU.mult))
                dve.wait_ge(sem["ada"], l * INCS["ada"] + 1)

                def modulation(q, m, src):
                    v(V.tensor_tensor(mod[:, q:q + m, :], src.rearrange("p (q c) -> p q c", c=2),
                                      PV("ada_b", q, m).unsqueeze(2).to_broadcast([P, m, 2]), ALU.add))

                def gain(g, name, q):
                    v(V.scalar_tensor_tensor(g[:, :, :], mod[:, q:q + 8, :], 1.0, PV(name, 0, 8).unsqueeze(2).to_broadcast([P, 8, 2]),
                                             ALU.add, ALU.mult))

                modulation(0, 2 * ADA_FIRST, bank(4)[:, 0:4 * ADA_FIRST])
                gain(gain1, "g1", 8)

                def norm(first):
                    dve.wait_ge(sem["rst_s"], l * INCS["rst_s"] + first + 1)
                    for k in range(KD):
                        V.tensor_tensor(hT[:, k, :], xT[:, k, :], rst, ALU.mult).then_inc(sem["h_part"], 1)

                norm(0)
                for c in range(RWC):
                    dve.wait_ge(sem["shift_a"], l * INCS["shift_a"] + c + 1)
                    dst = (rT[:, c % 2, :], kT[:, c % 2, :], vT[:, c % 2, :])[c // 2] if c < 6 else lora[:, c - 6, :]
                    u = bank(2 * (c % 2), 2)
                    for n, (lo, hi) in enumerate(SEGMENTS):
                        v(V.scalar_tensor_tensor(dst[:, lo + 1:hi], u[:, lo:hi - 1], PV("mu0", c), dst[:, lo + 1:hi], ALU.mult, ALU.add))
                        ins = V.scalar_tensor_tensor(dst[:, lo:hi - 1], u[:, lo + 1:hi], PV("mu1", c), dst[:, lo:hi - 1], ALU.mult, ALU.add)
                        (out if n else lambda _, i: v(i))("shifted", ins)
                for p in range(2):
                    out("rw_kk", V.tensor_scalar(kkT[:, p, :], kT[:, p, :], PV("k_k", p), None, ALU.mult))
                dve.wait_ge(sem["rw_le"], l * INCS["rw_le"] + 8)
                v(V.tensor_scalar(ldT[:, :, :, :], ldT[:, :, :, :], DECAY, None, ALU.mult))
                dve.wait_ge(sem["lora_mm"], l * INCS["lora_mm"] + 10)
                for p in range(2):
                    v(V.tensor_copy(gT[:, p, :], bank(2 * p, 2)[:, 0:TOK]))
                dve.wait_ge(sem["kk_mm"], l * INCS["kk_mm"] + 2)
                for p in range(2):
                    out("rw_kk_m", V.tensor_scalar(scr[:, p, :], bank(4 + 2 * p, 2)[:, 0:TOK], 1e-24, None, ALU.max))
                dve.wait_ge(sem["rw_kk_s"], l * INCS["rw_kk_s"] + 2)
                out("rw_prep_done", V.scalar_tensor_tensor(kkT[:, :, :], kkT[:, :, :], 2.0 ** 10, scr[:, :, :], ALU.mult, ALU.mult))
                v(V.memset(state[:, 1:4:2, :, :], 0.0))
                v(V.memset(yT[:, :, :], 0.0))
                for rows in ada_rows:
                    v(V.memset(rows, 0.0))
                dve.wait_ge(sem["state_in"], l * INCS["state_in"] + 16)
                for b, n, step in RW_ORDER:
                    g, s = UNIT[b], RW_STATE[b][n]
                    T = slice(RW_TILE[b][n] * P, (RW_TILE[b][n] + 1) * P)
                    ends = lambda n: (g.e12[:, n % 2, b, :].unsqueeze(2).to_broadcast([P, 2, HD]), g.e12[:, n % 2, 1 - b, :].unsqueeze(2).to_broadcast([P, 2, HD]))

                    def incoming(n):
                        out(f"rw_s0{b}", V.tensor_tensor(g.S0[:, :, :], state[:, RW_STATE[b][n], :, :], ends(n)[0], ALU.mult))

                    if step == "sums":
                        for p in range(2):
                            v(V.tensor_tensor_scan(Wc[:, p, :], ones, ldT[:, b, p, T], 0.0, ALU.mult, ALU.add))
                        v(V.tensor_tensor(Wm[:, :, :], Wc[:, :, :], Wc[:, :, 63:64].to_broadcast([P, 2, P]), ALU.subtract))
                        out(f"rw_sums{b}", V.tensor_tensor(Ec[:, :, :], Wm[:, :, :], ldT[:, b, :, T], ALU.subtract))
                    elif step == "products":
                        for p in range(2):
                            v(V.tensor_scalar(g.BK[:, 1, p, :], aT[:, b, p, T], PV("k_a", p), one_ka[:, p:p + 1], ALU.mult, ALU.add))
                        v(V.tensor_tensor(g.BK[:, 1, :, :], g.BK[:, 1, :, :], kT[:, :, T], ALU.mult))
                        v(V.tensor_tensor(g.BK[:, 0, :, :], kkT[:, :, T], aT[:, b, :, T], ALU.mult))
                    elif step == "factors":
                        dve.wait_ge(sem[f"rw_exp{b}"], l * INCS[f"rw_exp{b}"] + n + 1)
                        v(V.scalar_tensor_tensor(g.AR[:, n % 2, :, 0, :], kkT[:, :, T], -1.0, eA[:, :, :], ALU.mult, ALU.mult))
                        v(V.tensor_tensor(g.AR[:, n % 2, :, 1, :], rT[:, :, T], eR[:, :, :], ALU.mult))
                        v(V.tensor_tensor(g.BK[:, 0, :, :], g.BK[:, 0, :, :], eB[:, :, :], ALU.mult))
                        out(f"rw_in{b}", V.tensor_tensor(g.BK[:, 1, :, :], g.BK[:, 1, :, :], eB[:, :, :], ALU.mult))
                        if n == 0:
                            incoming(0)
                    elif step == "scores":
                        for h in range(4):
                            dve.wait_ge(sem[f"rw_sc{b}"], l * INCS[f"rw_sc{b}"] + 4 * n + h + 1)
                            out(f"rw_masked{b}", V.tensor_tensor(g.SC[:, h, :], g.bank(2 + h % 2), scmask[:, b, :], ALU.mult))
                        v(V.tensor_tensor(g.DD[:, :, 1, :], g.SC[:, :, 0:P], lv[:, b, 0, :].unsqueeze(1).to_broadcast([P, 4, P]), ALU.mult))
                        out(f"rw_dt{b}", V.tensor_tensor(g.DD[:, :, 1, :], g.DD[:, :, 1, :], ident.unsqueeze(1).to_broadcast([P, 4, P]), ALU.add))
                    elif step == "first":
                        dve.wait_ge(sem[f"rw_d0{b}"], l * INCS[f"rw_d0{b}"] + n + 1)
                        out(f"rw_dd{b}", V.tensor_copy(g.DD[:, :, 0, :], g.bank(0).rearrange("p (h t) -> p h t", h=4)))
                    elif step[0] == "Z":
                        dve.wait_ge(sem[f"rw_z{b}"], l * INCS[f"rw_z{b}"] + LEVELS * n + step[1] + 1)
                        z = g.bank(1, 2).rearrange("p (h n) -> p h n", h=4)
                        flat = g.DD[:, :, :, :].rearrange("p h a t -> p h (a t)")
                        part = slice(0 if step[1] < LEVELS - 1 else P, 2 * P)
                        out(f"rw_dd{b}", V.tensor_tensor(flat[:, :, part], flat[:, :, part], z[:, :, part], ALU.add))
                    elif step == "out":
                        dve.wait_ge(sem[f"rw_os{b}"], l * INCS[f"rw_os{b}"] + n + 1)
                        v(V.tensor_tensor(yT[:, :, T], yT[:, :, T], g.bank(0)[:, 0:256].rearrange("p (a t) -> p a t", a=2), ALU.add))
                        v(V.tensor_tensor(Stmp[:, :, :], g.S0[:, :, :], g.bank(3)[:, 256:256 + P].rearrange("p (a t) -> p a t", a=2), ALU.add))
                        out(f"rw_state{b}", V.tensor_tensor(state[:, s, :, :], Stmp[:, :, :], ends(n)[1], ALU.mult))
                        if n + 1 < NT:
                            incoming(n + 1)
                V.tensor_copy(small[:, 60:61], ident[:, 0:1]).then_inc(sem["rw_y_all"], 1)
                for p in range(2):
                    dve.wait_ge(sem["rw_fm"], l * INCS["rw_fm"] + p + 1)
                    out("rw_yc2", V.scalar_tensor_tensor(yT[:, p, :], bank(4 + 2 * p, 2)[:, 0:TOK], -1.0 / HD, yT[:, p, :], ALU.mult, ALU.add))
                dve.wait_ge(sem["ada_tp"], l * INCS["ada_tp"] + 1)
                for i in range(2):
                    q = 2 * ADA_FIRST + 16 * i
                    v(V.tensor_tensor(mod[:, q:q + 16, :].rearrange("p (j i) c -> p j i c", j=4),
                                      bank(i).rearrange("p (i j r) -> p j i r", i=4, j=4)[:, :, :, 0:2],
                                      PV("ada_b", q, 16).rearrange("p (j i) -> p j i", j=4).unsqueeze(3).to_broadcast([P, 4, 4, 2]), ALU.add))
                gain(gain2, "g2", 32)
                v(V.tensor_tensor(aT[:, 0, :, :], aT[:, 0, :, :], aT[:, 1, :, :], ALU.add))
                for p in range(2):
                    v(V.tensor_scalar(aT[:, 0, p, :], aT[:, 0, p, :], PV("k_a", p), two_ka[:, p:p + 1], ALU.mult, ALU.add))
                v(V.tensor_tensor(kT[:, :, :], kT[:, :, :], aT[:, 0, :, :], ALU.mult))
                v(V.tensor_tensor(kT[:, :, :], kT[:, :, :], rT[:, :, :], ALU.mult))
                v(V.tensor_scalar(kT[:, 0, :], kT[:, 0, :], PV("r_k", 0), None, ALU.mult))
                out("rw_bonus", V.tensor_scalar(kT[:, 1, :], kT[:, 1, :], PV("r_k", 1), None, ALU.mult))
                dve.wait_ge(sem["rw_fs"], l * INCS["rw_fs"] + 2)
                v(V.tensor_tensor(yT[:, :, :], yT[:, :, :], scr[:, :, :], ALU.mult))
                for p in range(2):
                    v(V.tensor_scalar(yT[:, p, :], yT[:, p, :], PV("ln_g", p), PV("ln_b", p), ALU.mult, ALU.add))
                for p in range(2):
                    dve.wait_ge(sem["rw_fm"], l * INCS["rw_fm"] + 5 + p)
                    v(V.tensor_tensor(vT[:, p, :], vT[:, p, :], bank(2 * p, 2)[:, 0:TOK], ALU.mult))
                v(V.tensor_tensor(yT[:, :, :], yT[:, :, :], vT[:, :, :], ALU.add))
                out("rw_final", V.tensor_tensor(mixT[:, 3:5, :], yT[:, :, :], gT[:, :, :], ALU.mult))
                for i in range(NT):
                    for j in range(2):
                        q = 2 * i + j
                        dve.wait_ge(sem["v_mm"], l * INCS["v_mm"] + q + 1)
                        V.tensor_copy(vtok[:, i, PIECE * j:PIECE * (j + 1)], bank(q % 2)[:, 0:PIECE]).then_inc(sem["v_done"], 1)
                for c in range(10):
                    x = bank(2 * (c % 3), 2)
                    r = nrm[:, c % 2, :]
                    dve.wait_ge(sem["nsr"], l * INCS["nsr"] + c + 1)
                    g = naq8 if c < 3 else PV("na_k") if c < 6 else swq8 if c < 9 else PV("sw_k")
                    if c < 3:
                        v(V.tensor_scalar(r, r, g, None, ALU.mult))
                        for j in range(4):
                            view = lambda t: t[:, 0:LAT].rearrange("p (r j c) -> p r j c", r=8, j=4)[:, :, j, :]
                            v(V.tensor_tensor(qa[:, c, P * j:P * j + P].rearrange("p (r c) -> p r c", r=8)[:, :, :],
                                              view(x), view(r), ALU.mult))
                        out("qk_used", V.tensor_tensor(qa[:, c, LAT:TOK], x[:, LAT:TOK], r[:, LAT:TOK], ALU.mult))
                    else:
                        dst = ka[:, c - 3, :] if c < 6 else qc[:, c - 6, :] if c < 9 else kc
                        out("qk_used", V.scalar_tensor_tensor(dst, x[:, 0:TOK], g, r, ALU.mult, ALU.mult))
                        if c < 6 or c == 9:
                            out("k_ctx", V.tensor_copy(small[:, 61:62], ident[:, 0:1]))
                for i in range(4):
                    dst = kc if i == 3 else qc[:, i, :]
                    dve.wait_ge(sem["rope_mm"], l * INCS["rope_mm"] + i + 1)
                    v(V.tensor_tensor(swap, bank(i), C("sin"), ALU.mult))
                    v(V.tensor_tensor(dst[:, 0:LAT], dst[:, 0:LAT], C("cos"), ALU.mult))
                    out("roped", V.tensor_tensor(dst[:, 0:LAT], dst[:, 0:LAT], swap, ALU.add))
                dve.wait_ge(sem["bias_zero"], l * INCS["bias_zero"] + 2)

                def negated(n):
                    kind, h, j = ATT[n]
                    w = width(ATT[n])
                    dve.wait_ge(sem["att_s"], l * INCS["att_s"] + n + 1)
                    if kind == "na":
                        dve.wait_ge(sem["att_bias"], l * INCS["att_bias"] + n + 1)
                        add = bias[:, n % 2, :]
                    elif kind == "sw":
                        add = C("swmask")[:, P:] if j == 0 else C("swmask")
                    else:
                        add = C("swmask")[:, P:2 * P]
                    if kind in ("sw", "csw"):
                        V.tensor_copy(Ssb[:, n % 2, w:w + 1], neg_sink[:, h:h + 1])
                    else:
                        V.tensor_copy(stats[:, n % 4, 3:4], ident[:, 0:1])
                    V.tensor_tensor_reduce(Ssb[:, n % 2, 0:w], bank(n % 2)[:, 0:w], add[:, 0:w], -1.0,
                                           neg_sink[:, h:h + 1] if kind in ("sw", "csw") else -NEG, ALU.add, ALU.min,
                                           stats[:, n % 4, 0:1]).then_inc(sem["att_m"], 1)

                def inverse_sum(n):
                    dve.wait_ge(sem["att_p"], l * INCS["att_p"] + n + 1)
                    V.reciprocal(stats[:, n % 4, 2:3], stats[:, n % 4, 1:2]).then_inc(sem["att_r"], 1)

                def merged(n):
                    kind, h, j = ATT[n]
                    hb = HD * (h % 2)
                    dve.wait_ge(sem["att_o"], l * INCS["att_o"] + n + 1)
                    src = bank(4 + n % 2)[hb:hb + HD, 0:P]
                    chunk = h // 2 + (0 if kind in ("na", "cna") else 5)
                    if kind == "na":
                        dst = mixT[hb:hb + HD, chunk, 0:LAT].rearrange("p (r j c) -> p r j c", r=8, j=4)[:, :, j, :]
                        src = src.rearrange("p (r c) -> p r c", r=8)
                    elif kind == "sw":
                        dst = mixT[hb:hb + HD, chunk, P * j:P * j + P]
                    else:
                        dst = mixT[hb:hb + HD, chunk, LAT:TOK]
                    V.tensor_copy(dst, src).then_inc(sem["att_oc"], 1)

                for n in range(len(ATT) + 3):
                    if n < len(ATT):
                        negated(n)
                    if 1 <= n <= len(ATT):
                        inverse_sum(n - 1)
                    if n >= 3:
                        merged(n - 3)
                for c in range(KD):
                    dve.wait_ge(sem["out_mm"], l * INCS["out_mm"] + c + 1)
                    for cond, (lo, hi) in enumerate(SEGMENTS):
                        V.scalar_tensor_tensor(xT[:, c, lo:hi], bank(2 * (c % 2), 2)[:, lo:hi], mod[:, 16 + c, cond:cond + 1],
                                                                  xT[:, c, lo:hi], ALU.mult, ALU.add).then_inc(sem["out_done"], 1)
                dve.wait_ge(sem["out_done"], l * INCS["out_done"] + 2 * KD)
                norm(1)
                dve.wait_ge(sem["router_mm"], l * INCS["router_mm"] + 1)
                r = bank(2)[:, 0:NT * EXPERTS].rearrange("p (i e) -> p i e", i=NT)
                v(V.tensor_reduce(amx[:, :, 0:1], r, AX, ALU.max))
                out("r_sub", V.tensor_tensor(aff[:, :, :], r, amx[:, :, 0:1].to_broadcast([P, NT, EXPERTS]), ALU.subtract))
                dve.wait_ge(sem["r_exp"], l * INCS["r_exp"] + 1)
                v(V.tensor_reduce(amx[:, :, 1:2], aff[:, :, :], AX, ALU.add))
                v(V.reciprocal(amx[:, :, 0:1], amx[:, :, 1:2]))
                v(V.memset(aff_sp[:, :, :], -1.0))
                v(V.tensor_tensor(aff_sp[:, 0:4, 0:EXPERTS], aff[:, 0:4, :], amx[:, 0:4, 0:1].to_broadcast([P, 4, EXPERTS]), ALU.mult))
                out("aff_sp", V.tensor_tensor(aff_sp[:, 0, EXPERTS:32], aff[:, 4, :], amx[:, 4, 0:1].to_broadcast([P, EXPERTS]), ALU.mult))
                dve.wait_ge(sem["aff_tp"], l * INCS["aff_tp"] + 1)
                v(V.tensor_copy(affT[0:32, :], bank(3)[0:32, :]))
                for i in range(LCAP // 8):
                    t8, i8 = vals[0:32, 8 * i:8 * i + 8], idx_u[0:32, 8 * i:8 * i + 8].bitcast(U32)
                    for find in (lambda: V.max(t8, affT[0:32, :]), lambda: V.max_index(i8, t8, affT[0:32, :]),
                                 lambda: V.match_replace(affT[0:32, :], t8, affT[0:32, :], -2.0)):
                        V.tensor_copy(dummy[:, 3:4], ident[:, 0:1])
                        v(find())
                v(V.memset(tops_ctx[0:32, :, :], 0.0))
                for half in range(2):
                    v(V.tensor_copy(tops[0:32, 0, LCAP * half:LCAP * (half + 1)], idx_u[0:32, :].bitcast(U32)))
                    v(V.tensor_copy(tops[0:32, 1, LCAP * half:LCAP * (half + 1)], vals[0:32, :]))
                for half in range(2):
                    v(V.tensor_scalar(tops_ctx[0:32, 0, 32 * half:32 * half + CCAP], tops[0:32, 0, 0:CCAP], float(LAT), None, ALU.add))
                    out("idx_top", V.tensor_copy(tops_ctx[0:32, 1, 32 * half:32 * half + CCAP], vals[0:32, 0:CCAP]))
                dve.wait_ge(sem["slot_tp"], l * INCS["slot_tp"] + 1)
                st = bank(3)[:, 0:64].rearrange("p (a r) -> p a r", a=2)
                sc = bank(3)[:, 64:128].rearrange("p (a r) -> p a r", a=2)
                for a, (lat, ctx_) in enumerate(((id_lat, id_ctx), (gate_lat, gate_ctx))):
                    v(V.tensor_copy(lat[0:LCAP, :], st[0:LCAP, a, 0:EXPERTS:2]))
                    v(V.tensor_copy(lat[LCAP:P, :], st[LCAP:P, a, 1:EXPERTS:2]))
                    v(V.tensor_copy(ctx_[0:32, :], sc[0:32, a, EXPERTS:2 * EXPERTS:2]))
                    v(V.tensor_copy(ctx_[32:48, :], sc[32:48, a, EXPERTS + 1:2 * EXPERTS:2]))
                v(V.memset(ye_ctx[0:48, :], 0.0))
                out("xe_zero", V.memset(xe1[:, :, :], 0.0))
                dve.wait_ge(sem["idx_in"], l * INCS["idx_in"] + 32)

                def select(n, first=False):
                    if not first:
                        dve.wait_ge(sem["gather"], l * INCS["gather"] + n)
                    for t in range(4):
                        V.tensor_scalar(sel_lat[:, t, :], idx_lat[:, n, :], C("tokid")[:, t:t + 1], None, ALU.is_equal)
                    V.tensor_scalar(sel_ctx, idx_ctx[:, n, :], C("tokid")[:, 0:1], None, ALU.is_equal).then_inc(sem["sel"], 1)

                def select_T(n):
                    V.tensor_scalar(selT_lat, C("iota")[:, 0:LAT], id_lat[:, bass.ds(n, 1)],
                                    gate_lat[:, bass.ds(n, 1)], ALU.is_equal, ALU.mult)
                    V.tensor_scalar(selT_ctx[0:48, :], C("iota")[0:48, LAT:TOK], id_ctx[0:48, bass.ds(n, 1)],
                                    gate_ctx[0:48, bass.ds(n, 1)], ALU.is_equal, ALU.mult).then_inc(sem["selT"], 1)

                def hidden(e, odd):
                    m = P if odd else CAP
                    dve.wait_ge(sem["m_silu"], l * INCS["m_silu"] + e + 1)
                    V.tensor_tensor(he[0:m, :], sg[0:m, :], bank(2, 2)[0:m, :], ALU.mult).then_inc(sem["he"], 1)

                def accumulate(n):
                    for k in range(KD):
                        dve.wait_ge(sem["scatter"], l * INCS["scatter"] + KD * n - KD + k + 1)
                        b = (6, 4)[k % 2]
                        V.scalar_tensor_tensor(xT[:, k, 0:LAT], bank(b), mod[:, 40 + k, 0:1], xT[:, k, 0:LAT], ALU.mult, ALU.add)
                        V.scalar_tensor_tensor(xT[:, k, LAT:TOK], bank(b + 1)[:, 0:CTX], mod[:, 40 + k, 1:2], xT[:, k, LAT:TOK],
                                               ALU.mult, ALU.add).then_inc(sem["scattered"], 1)
                    dve.wait_ge(sem["scattered"], l * INCS["scattered"] + KD * n)

                select(0, True)
                select_T(0)
                hidden(0, False)
                select(1)
                hidden(1, True)
                with dve.Fori(1, PAIRS - 1) as i:
                    hidden(2 * i, False)
                    accumulate(i)
                    select_T(i)
                    select(i + 1)
                    hidden(2 * i + 1, True)
                hidden(EXPERTS - 2, False)
                accumulate(PAIRS - 1)
                select_T(PAIRS - 1)
                hidden(EXPERTS - 1, True)
                accumulate(PAIRS)
                assert count["vec_step"] == INCS["vec_step"], count["vec_step"]
                V.memset(dummy[:, 2:3], 0.0).then_inc(sem["layer_done"], 1)
                dve.wait_ge(sem["layer_done"], 4 * (l + 1))



def _layout(x):
    c = np.ascontiguousarray
    L = LAYERS

    def chunks(a):
        return a.reshape(L, -1, P).transpose(0, 2, 1)

    tokens = np.concatenate([x["x_sample"][0], x["x_prompt"][0]], 0)
    out = {"cst": _constants(), "xT": c(tokens.reshape(TOK, KD, P).transpose(2, 1, 0))}
    out["cond"] = c(np.stack([x["c"][0], x["c_ctx"]], 0).reshape(2, KD, P).transpose(2, 1, 0))
    par = np.zeros((L, P, PAR_N), np.float32)

    def put(name, a):
        lo, hi = PAR[name]
        par[:, :, lo:hi] = a.reshape(L, P, hi - lo)

    put("ada_b", chunks(x["ada_b"]))
    put("g1", chunks(x["norm1_g"]))
    put("g2", chunks(x["norm2_g"]))
    for name, key in (("na_q", "na_q_norm"), ("na_k", "na_k_norm"), ("sw_q", "swa_q_norm"), ("sw_k", "swa_k_norm")):
        put(name, np.concatenate([x[key], x[key]], 1))
    put("mu0", chunks(x["rw_mu"][:, 0]))
    put("mu1", chunks(x["rw_mu"][:, 1]))
    put("w0", chunks(x["rw_w0"].reshape(L, 512)))
    put("a0", chunks(x["rw_a0"].reshape(L, 512)))
    for name, key in (("k_k", "rw_k_k"), ("k_a", "rw_k_a"), ("r_k", "rw_r_k"), ("ln_g", "rw_ln_g"), ("ln_b", "rw_ln_b")):
        put(name, chunks(x[key].reshape(L, 256)))
    put("sink", np.broadcast_to(x["swa_sink"][:, None, :], (L, P, 6)))
    put("w2", x["rw_w2"].reshape(L, P, 256))
    put("a2", x["rw_a2"].reshape(L, P, 256))
    put("lg2", x["rw_g2"])
    put("router", x["w_router"].reshape(L, KD, P, EXPERTS).transpose(0, 2, 1, 3))
    out["par"] = par
    w = x["w_in"]
    q_order = [h for i in range(3) for h in (i, i + 3)]
    qc = w[:, :, 2304:2688].reshape(L, D, 6, HD)[:, :, q_order].reshape(L, D, 384)
    def pieces(a, n):
        return c(a.reshape(L, KD, P, n, PIECE).transpose(0, 3, 2, 1, 4))

    w_in = np.concatenate([w[:, :, 0:768], qc, w[:, :, 2688:2816], w[:, :, 768:1152], w[:, :, 2816:2944], w[:, :, 1152:2304],
                           np.zeros((L, D, P), np.float32)], 2)
    out["w_in"] = pieces(w_in, W_IN_PIECES)
    out["ada_w"], out["w_out"] = pieces(x["ada_w"], ADA_PIECES), pieces(x["w_out"], OUT_PIECES)
    out["w_gate"], out["w_up"], out["w_down"] = c(x["w_gate"]), c(x["w_up"]), c(x["w_down"])
    table = np.zeros((L, 6, 16, 64), np.float32)
    table[:, :, 0:15, 16:47] = x["na_rpb"]
    out["rpb"] = c(table.reshape(L, 6, 1024)[:, :, ::-1])
    heads = np.concatenate([x["cache_na_k"][0], x["cache_swa_k"][0]], 1)
    out["kcache"] = c(heads.reshape(L, 4, 2, P, HD).transpose(0, 2, 4, 1, 3).reshape(L, P, 4, P))
    heads = np.concatenate([x["cache_na_v"][0], x["cache_swa_v"][0]], 1)
    out["vcache"] = c(heads.transpose(0, 2, 1, 3).reshape(L, P, 512))
    s = x["state_rwkv"][0].reshape(L, 2, 2, 2, HD, HD)
    out["state"] = c(s.transpose(0, 3, 5, 1, 2, 4).reshape(L, P, 2, 2, HD))
    return out


_OUTS = {"y": (P, KD, TOK), "nk": (LAYERS, P, 4, P), "nv": (LAYERS, P, 512), "ns": (LAYERS, P, 2, 2, HD),
         "vscr": (LAT, 384), "tops": (32, P)}


def _returned(r):
    L = LAYERS
    y = r["out_y"].transpose(2, 1, 0).reshape(TOK, D)
    k = r["out_nk"].reshape(L, 2, HD, 4, P).transpose(0, 3, 1, 4, 2).reshape(1, L, 8, P, HD)
    v = r["out_nv"].reshape(L, P, 8, HD).transpose(0, 2, 1, 3)[None]
    s = r["out_ns"].reshape(L, 2, HD, 2, 2, HD).transpose(0, 3, 4, 1, 5, 2).reshape(1, L, 2, 4, HD, HD)
    c = np.ascontiguousarray
    return c(y[None, LAT:]), c(y[None, :LAT]), c(k[:, :, 0:6]), c(v[:, :, 0:6]), c(k[:, :, 6:8]), c(v[:, :, 6:8]), c(s)


def kernel(**inputs):
    import concourse.bacc as bacc
    from concourse.bass_utils import run_bass_kernel_spmd as run
    arrays = _layout({k: np.asarray(v) for k, v in inputs.items()})
    nc = bacc.Bacc("TRN2", target_bir_lowering=False, num_devices=1)
    nc.disable_value_cache = True
    io = {n: nc.dram_tensor(f"in_{n}", a.shape, F32, kind="ExternalInput").ap() for n, a in arrays.items()}
    io.update({n: nc.dram_tensor(f"out_{n}", shape, F32, kind="ExternalOutput").ap() for n, shape in _OUTS.items()})
    program(nc, io)
    r = run(nc, [{f"in_{k}": v for k, v in arrays.items()}], core_ids=[0])
    return _returned(r.results[0])
```

```python
from contextlib import ExitStack

import numpy as np

import concourse.bass as bass
from concourse import mybir

F32 = mybir.dt.float32
U32 = mybir.dt.uint32
ALU = mybir.AluOpType
ACT = mybir.ActivationFunctionType
AX = mybir.AxisListType.X

P = 128
LAYERS = 2
D = 1024
KD = D // P
LAT, CTX = 512, 128
TOK = LAT + CTX
SEGMENTS = ((0, LAT), (LAT, TOK))
HD = 64
PAIRS_A = 3
RWC = 9
NT = TOK // P
EXPERTS = 16
LCAP, CCAP = 2 * LAT // EXPERTS, 2 * CTX // EXPERTS
CAP = LCAP + CCAP
FF = 1024
PAIRS = EXPERTS // 2
NEG = -1e30
DECAY = float(-np.exp(np.float32(-0.5)))

PIECE = 256
STREAM = 2
ADA_PIECES = 6 * D // PIECE
W_IN_PIECES = 12
OUT_PIECES = D // PIECE
RW_PIECES = 5
RW_CHUNKS = (6, 7, 8, 2, 3, 0, 1, 4, 5)
ADA_FIRST = 8
PIECES = W_IN_PIECES + OUT_PIECES + ADA_PIECES - ADA_FIRST
RING = 6
EXPERT_PIECES = 12
MULTIPLIED = RING + 8

def _columns(sizes):
    at, out = 0, {}
    for name, n in sizes:
        out[name] = (at, at + n)
        at += n
    return out, at

PAR, PAR_N = _columns([("ada_b", 48), ("g1", 8), ("g2", 8), ("na_q", 1), ("na_k", 1), ("sw_q", 1), ("sw_k", 1),
                       ("mu0", 9), ("mu1", 9), ("w0", 4), ("a0", 4), ("k_k", 2), ("k_a", 2), ("r_k", 2),
                       ("ln_g", 2), ("ln_b", 2), ("sink", 6), ("w2", 256), ("a2", 256), ("lg2", 256), ("router", 128)])
CST, CST_N = _columns([("ident", 128), ("ones", 128), ("bones", 128), ("rot", 128), ("scmask", 1024),
                       ("lv", 2 * 7 * 128), ("namask", 768), ("swmask", 512), ("iota", 640), ("tokid", 5),
                       ("cos", 512), ("sin", 512), ("eps", 2)])


def _constants():
    c = np.zeros((P, CST_N), np.float32)

    def put(name, a):
        lo, hi = CST[name]
        c[:, lo:hi] = np.asarray(a, np.float32).reshape(P, hi - lo)

    p, q = np.arange(P)[:, None], np.arange(P)[None]
    put("ident", p == q)
    put("ones", np.ones((P, P)))
    put("bones", p // HD == q // HD)
    put("rot", np.where((q % HD < 32) & (p == q + 32), -1.0, 0.0) + np.where((q % HD >= 32) & (p == q - 32), 1.0, 0.0))
    sc, lv = [], []
    for d in range(2):
        strict, incl = ((p < q), (p <= q)) if d == 0 else ((p > q), (p >= q))
        sc += [strict, incl, strict, incl]
        for i in range(7):
            s = 1 << i
            a, b = (p, q) if d == 0 else (q, p)
            lv.append((b // s == a // s + 1) & (a // s % 2 == 0))
    put("scmask", np.stack(sc, 1))
    put("lv", np.stack(lv, 1))
    na = []
    for j in (0, 1, 3):
        start = min(max(j * 16 - 8, 0), 32)
        qc = 16 * j + np.arange(P)[:, None] % 16
        kc = start + np.arange(256)[None] % 32
        cs = np.clip(qc - 8, 0, 48)
        na.append(np.where((kc >= cs) & (kc < cs + 16), 0.0, NEG))
    put("namask", np.stack(na, 1))
    z = np.zeros((P, P))
    put("swmask", np.concatenate([np.where(q >= p, 0.0, NEG), z, z, np.where(q <= p, 0.0, NEG)], 1))
    put("iota", np.broadcast_to(np.arange(TOK), (P, TOK)))
    put("tokid", np.arange(P)[:, None] + P * np.arange(NT)[None])
    inv = np.float32(10000.0) ** (-np.arange(16, dtype=np.float32) / np.float32(16))
    t = np.arange(LAT)
    ang = np.concatenate([inv[:, None] * (t // 64).astype(np.float32), inv[:, None] * (t % 64).astype(np.float32)], 0)
    put("cos", np.tile(np.cos(ang), (4, 1)))
    put("sin", np.tile(np.sin(ang), (4, 1)))
    put("eps", np.broadcast_to(np.array([1e-6, 64e-5]), (P, 2)))
    return c


ARENA = 26200
LEVELS = 6
N_ATT = 6 * 4 + 6 * 4 + 6 + 6
VEC_STEPS = 258
INCS = {
    "stream_used": PIECES, "ada_used": ADA_FIRST,
    "par_in": 16, "rpb_in": 16 * 48, "cache_in": 32, "state_in": 16, "vscr": 16,
    "vwin_in": 16 * 32, "out_kv": 48, "out_state": 16, "idx_out": 16, "idx_in": 32, 
    "sq": 2 * KD, "rst_s": 2, "h_ready": 2 * KD, "shift_a": RWC, "rw_lora": 2, "rw_le": 8, "rw_kk_sq": 2,
    "rw_kk_s": 2, "rw_fs": 2,
    "rw_fsq": 2, "nsq": 10, "nsr": 10, "att_p": N_ATT, "att_ptc": N_ATT, "r_exp": 1,
    "xe_in": PAIRS, "m_silu": EXPERTS, "he_t": 2 * EXPERTS, "xe_ctx": PAIRS, "ye": EXPERTS,
    "ada": 3, "gain1": 1, "ada_rows": 1, "sq_used": 2 * KD, "proj_done": RWC, "lora_mm": 10, "kk_mm": 2, 
    "rw_fm": 6,
    "qk_done": 10, "qk_norm": 10, "rope_mm": 4, "v_mm": 2 * NT, "att_s": N_ATT, "att_t": N_ATT, "att_o": N_ATT,
    "out_mm": KD, "router_mm": 1, "aff_tp": 1, "h_tp": 2 * NT, "slot_tp": 1, "gather": PAIRS, "ring_free": 2,
    "ring_used": EXPERT_PIECES * EXPERTS + RING, "he_tp": 2 * EXPERTS, "scatter": KD * PAIRS,
    "vec_step": VEC_STEPS, "ms": 2, "h_part": 2 * KD, "shifted": RWC, "rw_kk": 2, "rw_kk_m": 2,
    
    "rw_y_all": 1, "rw_yc2": 2, "rw_var": 2, "rw_bonus": 1, "rw_final": 1, "qk_ms": 10, "qk_used": 10,
    "k_ctx": 4, "roped": 4, "v_done": 2 * NT, "att_m": N_ATT, "att_bias": 24, "att_r": N_ATT, "bias_zero": 2, "att_pn": N_ATT, "att_oc": N_ATT,
    "out_done": 2 * KD, "r_sub": 1, "aff_sp": 1, "h_tok": 2 * NT, "idx_top": 2,
    "sel": PAIRS, "selT": PAIRS, "he": EXPERTS, "scattered": KD * PAIRS, "xe_zero": 1,
}
INCS.update({f"stream{s}": 16 * PIECES // STREAM for s in range(STREAM)})
INCS.update({f"ring{s}": 16 * EXPERT_PIECES * EXPERTS // RING for s in range(RING)})
INCS.update({f"ada{s}": 16 * -(-(ADA_FIRST - s) // RING) for s in range(RING)})
for b in range(2):
    INCS.update({f"rw_{name}{b}": NT for name in ("sums", "exp", "in", "s0", "tp", "tpc", "dt", "d0", "w", "wc", "u", "uc", "os", "state")})
    INCS.update({f"rw_mod{b}": NT - 1, f"rw_modc{b}": NT - 1})
    INCS.update({f"rw_{name}{b}": NT * LEVELS for name in ("x", "y", "yc", "z")})
    INCS.update({f"rw_sc{b}": NT * 4, f"rw_masked{b}": NT * 4, f"rw_dd{b}": NT * (LEVELS + 1)})
ONCE = ("boot", "cond_e", "silu_step", "silu", "layer_done", "out_y")


def program(nc, io):
    with ExitStack() as ctx:
        def sb(name, shape, dt=F32):
            return ctx.enter_context(nc.sbuf_tensor(name, shape, dt))

        sem = {name: ctx.enter_context(nc.semaphore(name)) for name in (*INCS, *ONCE)}

        cst = sb("cst", [P, CST_N])
        par = sb("par", [P, PAR_N])
        xT = sb("xT", [P, KD, TOK])
        hT = sb("hT", [P, KD, TOK])
        mixT = sb("mixT", [P, KD, TOK])
        stream = sb("stream", [P, STREAM, KD, PIECE])
        condT = sb("condT", [P, KD, 2])
        condE = sb("condE", [P, KD, 2])
        silu = sb("silu", [P, KD, 2])
        mod = sb("mod", [P, 48, 2])
        gain1 = sb("gain1", [P, KD, 2])
        gain2 = sb("gain2", [P, KD, 2])
        small = sb("small", [P, 64])
        dummy = sb("token", [P, 4])
        arena = sb("arena", [P, ARENA])
        psum = ctx.enter_context(nc.psum_tensor("psum", [P, 4096], F32))

        def C(name):
            return cst[:, CST[name][0]:CST[name][1]]

        def PV(name, i=0, n=1):
            return par[:, PAR[name][0] + i:PAR[name][0] + i + n]

        def bank(i, n=1):
            return psum[:, 512 * i:512 * (i + n)]

        def carve(at, *shape):
            n = int(np.prod(shape))
            assert at[0] + n <= ARENA, (at[0], n)
            v = arena[:, at[0]:at[0] + n]
            at[0] += n
            if len(shape) == 2:
                return v.rearrange("p (a b) -> p a b", a=shape[0])
            if len(shape) == 3:
                return v.rearrange("p (a b c) -> p a b c", a=shape[0], b=shape[1])
            if len(shape) == 4:
                return v.rearrange("p (a b c d) -> p a b c d", a=shape[0], b=shape[1], c=shape[2])
            return v

        ident, ones, bones = C("ident"), C("ones"), C("bones")
        scmask = C("scmask").rearrange("p (d n) -> p d n", d=2)
        lv = C("lv").rearrange("p (d s n) -> p d s n", d=2, s=7)
        namask = C("namask").rearrange("p (d n) -> p d n", d=3)

        mu_c = small[:, 8:17]
        one_ka, two_ka = small[:, 17:19], small[:, 19:21]
        naq8, swq8 = small[:, 21:22], small[:, 22:23]
        neg_sink = small[:, 24:30]

        at = [0]
        rT, kT, vT, kkT = (carve(at, 2, TOK) for _ in range(4))
        gT, yT = mixT[:, 0:2, :], mixT[:, 5:7, :]
        ldT, aT = carve(at, 2, 2, TOK), carve(at, 2, 2, TOK)
        rw_common = at[0]
        lora = carve(at, 3, TOK)

        def rw_chunk(c):
            return (rT[:, c % 2, :], kT[:, c % 2, :], vT[:, c % 2, :])[c // 2] if c < 6 else lora[:, c - 6, :]

        scr = carve(at, 2, TOK)
        at = [rw_common]
        Wc, Wm, Ec = (carve(at, 2, P) for _ in range(3))
        eR, eA, eB = (carve(at, 2, P) for _ in range(3))
        Stmp = carve(at, 2, HD)

        class Unit:
            def __init__(self, b):
                self.AR = carve(at, 2, 2, 2 * P).rearrange("p u a (b t) -> p u a b t", b=2)
                self.e12 = carve(at, 2, 2, 2)
                self.BK = carve(at, 2, 2, P)
                self.BKt = carve(at, 2, 2 * P)
                self.Vt = carve(at, 2 * P)
                self.SC = carve(at, 4, 4 * P)
                self.X = carve(at, 4, P)
                x = self.X[:, :, :].rearrange("p h t -> p (h t)")
                self.W, self.U = x[:, 0:4 * HD], x[:, 4 * HD:8 * HD]
                self.Y = carve(at, 4, P)
                self.DD = carve(at, 4, 2, P)
                self.S0 = carve(at, 2, HD)
                self.banks = 4 * b

            def bank(self, i, n=1):
                return bank(self.banks + i, n)

        UNIT = [Unit(b) for b in range(2)]
        state = carve(at, 4, 2, HD)
        rw_end = at[0]

        at = [0]
        qa, ka, qc = (carve(at, 3, TOK) for _ in range(3))
        kc = carve(at, TOK)
        vwin = carve(at, 8, 384)
        rpb = carve(at, 6, 512)
        kcache = carve(at, 4, P)
        vcache = carve(at, 512)
        nrm = carve(at, 2, TOK)
        assert at[0] >= rw_common + 5 * TOK
        vtok = carve(at, NT, 512)
        swap = carve(at, LAT)
        Ssb, Pb, PT = carve(at, 2, 516), carve(at, 3, 516), carve(at, 2, 516)
        bias = carve(at, 2, 384)
        stats = carve(at, 4, 4)
        att_end = at[0]

        at = [0]
        ring = carve(at, RING, 2, FF)
        ada_ring = arena[:, 0:RING * KD * PIECE].rearrange("p (s k c) -> p s k c", s=RING, k=KD)
        moe_common = at[0]
        xe0, xe1 = carve(at, KD, CAP), carve(at, KD, P)
        routing = at[0]
        sg, he = carve(at, FF), carve(at, FF)
        heT = carve(at, KD, P)
        ye_lat, ye_ctx = carve(at, D), carve(at, D)
        selT_lat, selT_ctx = carve(at, LAT), carve(at, CTX)
        sel_lat, sel_ctx = carve(at, 4, P), carve(at, 2 * CCAP)
        idx_lat, idx_ctx = carve(at, PAIRS, P), carve(at, PAIRS, 2 * CCAP)
        id_lat, gate_lat, id_ctx, gate_ctx = (carve(at, PAIRS) for _ in range(4))
        moe_end, at = at[0], [routing]
        aff_sp = carve(at, 4, 32)
        aff = carve(at, NT, EXPERTS)
        amx = carve(at, NT, 2)
        affT = carve(at, 512)
        tops = carve(at, 2, P)
        tops_ctx = carve(at, 2, 48)
        idx_u = carve(at, LCAP)
        vals = carve(at, LCAP)
        at = [ARENA - 3 * TOK]
        assert at[0] >= moe_common
        sq, rst = carve(at, 2, TOK), carve(at, TOK)
        htok = mixT[:, :, :].rearrange("p k t -> p (k t)").rearrange("p (i d) -> p i d", i=NT)

        block = ctx.enter_context(nc.Block())

        RW_STEPS = ["transpose", "scores", "first"] + [x for i in range(LEVELS) for x in (("Y", i), ("Z", i))] + ["W", "U", "out"]
        RW_AHEAD = {("Y", 0): "sums", ("Z", 0): "products", ("Y", 1): "factors"}
        RW_ORDER = [(b, 0, step) for b in range(2) for step in RW_AHEAD.values()]
        for t in range((NT * 2 + 1) * len(RW_STEPS) // 2):
            for b in range(2):
                n, k = divmod(t - b * (len(RW_STEPS) // 2), len(RW_STEPS))
                if 0 <= n < NT:
                    RW_ORDER.append((b, n, RW_STEPS[k]))
                    if RW_STEPS[k] in RW_AHEAD and n + 1 < NT:
                        RW_ORDER.append((b, n + 1, RW_AHEAD[RW_STEPS[k]]))
        ada_rows = (mixT[:, 2, 0:512], mixT[:, 7, 0:512])
        RW_STATE = [[0, 0, 0, 0, 1], [2, 2, 2, 2, 3]]
        RW_TILE = [[0, 1, 2, 3, 4], [3, 2, 1, 0, 4]]

        ATT = []
        for h in range(6):
            for j in range(4):
                ATT.append(("na", h, j))
        for i in range(3):
            for g in range(2):
                for b in range(4):
                    ATT.append(("sw", i + 3 * g, b))
        for h in range(6):
            ATT.append(("cna", h, 0))
        for h in range(6):
            ATT.append(("csw", h, 0))

        def width(u):
            kind, h, j = u
            return {"na": 384, "sw": 384 if j in (0, 3) else 512}.get(kind, 128)

        @block.sync
        def _(sp):
            for dst, src in ((cst[:, :], io["cst"]), (xT[:, :, :], io["xT"]), (condT[:, :, :], io["cond"])):
                sp.dma_start(dst, src).then_inc(sem["boot"], 16)
            with sp.Fori(0, LAYERS) as l:
                sp.wait_ge(sem["ring_free"], l * INCS["ring_free"] + 2)
                sp.dma_start(par[:, :], io["par"][l]).then_inc(sem["par_in"], 16)
                for i in range(ADA_FIRST):
                    if i >= RING:
                        sp.wait_ge(sem["ada_used"], l * INCS["ada_used"] + i - RING + 1)
                    sp.dma_start(ada_ring[:, i % RING, :, :], io["ada_w"][l, i]).then_inc(sem[f"ada{i % RING}"], 16)
                n = 0

                def piece(name, i):
                    nonlocal n
                    if n >= STREAM:
                        sp.wait_ge(sem["stream_used"], l * INCS["stream_used"] + n - STREAM + 1)
                    sp.dma_start(stream[:, n % STREAM, :, :], io[name][l, i]).then_inc(sem[f"stream{n % STREAM}"], 16)
                    n += 1

                for i in range(RW_PIECES):
                    if i == STREAM:
                        sp.wait_ge(sem["h_part"], l * INCS["h_part"] + KD)
                        sp.dma_start(state[:, 0:3:2, :, :], io["state"][l]).then_inc(sem["state_in"], 16)
                    piece("w_in", W_IN_PIECES - RW_PIECES + i)
                for i in range(STREAM):
                    piece("ada_w", ADA_FIRST + i)
                for i in range(ADA_FIRST + STREAM, ADA_PIECES):
                    piece("ada_w", i)
                order = [5, 6, 0, 1, 2, 3, 4]
                for i in order[:STREAM]:
                    piece("w_in", i)
                sp.wait_ge(sem["rw_final"], l * INCS["rw_final"] + 1)
                for b in range(2):
                    sp.wait_ge(sem[f"rw_state{b}"], l * INCS[f"rw_state{b}"] + NT)
                sp.dma_start(kcache[:, :, :], io["kcache"][l]).then_inc(sem["cache_in"], 16)
                sp.dma_start(vcache, io["vcache"][l]).then_inc(sem["cache_in"], 16)
                piece("w_in", order[STREAM])
                for h in range(6):
                    for r in range(8):
                        src = bass.AP(tensor=io["rpb"].tensor, offset=l * 6144 + 1024 * h + 64 * r + 49, ap=[[1, 16], [1, 512]])
                        sp.dma_start(rpb[16 * r:16 * r + 16, h, :], src).then_inc(sem["rpb_in"], 16)
                piece("w_in", order[STREAM + 1])
                sp.wait_ge(sem["v_done"], l * INCS["v_done"] + 2 * NT)
                sp.dma_start(io["vscr"].rearrange("(i p) c -> p i c", p=P), vtok[:, 0:4, 0:384]).then_inc(sem["vscr"], 16)
                sp.dma_start(io["nv"][l], vtok[:, 4, :]).then_inc(sem["out_kv"], 16)
                sp.wait_ge(sem["vscr"], l * INCS["vscr"] + 16)
                scr_v = io["vscr"].rearrange("(r c) f -> r c f", c=64)
                for j in range(4):
                    start = min(max(16 * j - 8, 0), 32)
                    for half in range(2):
                        for r in range(4):
                            sp.dma_start(vwin[32 * r:32 * r + 32, 2 * j + half, :],
                                                           scr_v[4 * half + r, start:start + 32, :]).then_inc(sem["vwin_in"], 16)
                for i in order[4:]:
                    piece("w_in", i)
                sp.wait_ge(sem["k_ctx"], l * INCS["k_ctx"] + 4)
                sp.dma_start(io["nk"][l][:, 0:3, :], ka[:, :, LAT:TOK]).then_inc(sem["out_kv"], 16)
                sp.dma_start(io["nk"][l][:, 3, :], kc[:, LAT:TOK]).then_inc(sem["out_kv"], 16)

                def expert_piece(e, j, t):
                    sp.wait_ge(sem["ring_used"], l * INCS["ring_used"] + t + 1)
                    w, row = ("w_gate", j // 2) if j < 8 and j % 2 == 0 else ("w_up", j // 2) if j < 8 else ("w_down", j - 8)
                    sp.dma_start(ring[:, j % RING, :, :], io[w][l, e, 256 * row:256 * row + 256, :].rearrange("(k p) c -> p k c", p=P))\
                        .then_inc(sem[f"ring{j % RING}"], 16)

                for i in range(OUT_PIECES):
                    piece("w_out", i)
                    if i % 2:
                        for j in range(RING // 2):
                            expert_piece(0, RING // 2 * (i // 2) + j, RING // 2 * (i // 2) + j)
                sp.wait_ge(sem["out_kv"], l * INCS["out_kv"] + 48)
                sp.wait_ge(sem["idx_top"], l * INCS["idx_top"] + 2)
                sp.dma_start(io["tops"], tops[0:32, 0, :]).then_inc(sem["idx_out"], 16)
                sp.wait_ge(sem["idx_out"], l * INCS["idx_out"] + 16)
                src = bass.AP(tensor=io["tops"].tensor, offset=0, ap=[[0, P], [P, EXPERTS], [1, LCAP]])
                sp.dma_start(idx_lat.rearrange("p e (h s) -> p (e h) s", h=2), src).then_inc(sem["idx_in"], 16)
                src = bass.AP(tensor=io["tops"].tensor, offset=EXPERTS * P, ap=[[0, P], [P, EXPERTS], [1, CCAP]])
                sp.dma_start(idx_ctx.rearrange("p e (h s) -> p (e h) s", h=2), src).then_inc(sem["idx_in"], 16)
                with sp.Fori(0, EXPERTS - 1) as e:
                    for j in range(EXPERT_PIECES):
                        expert_piece(e if j < EXPERT_PIECES - RING else e + 1, (j + RING) % EXPERT_PIECES, e * EXPERT_PIECES + j + RING)
                for j in range(RING, EXPERT_PIECES):
                    expert_piece(EXPERTS - 1, j, (EXPERTS - 1) * EXPERT_PIECES + j)

            sp.wait_ge(sem["layer_done"], 4 * LAYERS)
            sp.dma_start(io["y"], xT[:, :, :]).then_inc(sem["out_y"], 16)
            sp.wait_ge(sem["out_y"], 16)
            sp.wait_ge(sem["out_state"], 16 * LAYERS)
            sp.wait_ge(sem["out_kv"], 48 * LAYERS)
            sp.wait_ge(sem["idx_out"], 16 * LAYERS)
            sp.wait_ge(sem["vscr"], 16 * LAYERS)

        @block.gpsimd
        def _(pool):
            with pool.Fori(0, LAYERS) as l:
                for b, n, step in RW_ORDER:
                    g = UNIT[b]
                    if step == "first":
                        i = 0
                        pool.wait_ge(sem[f"rw_masked{b}"], l * INCS[f"rw_masked{b}"] + 4 * (n + 1))
                    elif step[0] == "Z" and step[1] < LEVELS - 1:
                        i = step[1] + 1
                        pool.wait_ge(sem[f"rw_y{b}"], l * INCS[f"rw_y{b}"] + LEVELS * n + i)
                    else:
                        continue
                    nc.gpsimd.tensor_tensor(g.X[:, :, :], g.SC[:, :, 0:P], lv[:, b, i + 1, :].unsqueeze(1).to_broadcast([P, 4, P]), ALU.mult)\
                        .then_inc(sem[f"rw_x{b}"], 1)
                for b in range(2):
                    pool.wait_ge(sem[f"rw_state{b}"], l * INCS[f"rw_state{b}"] + NT)
                nc.gpsimd.dma_start(io["ns"][l], state[:, 1:4:2, :, :]).then_inc(sem["out_state"], 16)
                pool.wait_ge(sem["out_state"], l * INCS["out_state"] + 16)
                pool.wait_ge(sem["rw_final"], l * INCS["rw_final"] + 1)
                for i in range(2):
                    nc.gpsimd.tensor_tensor(bias[:, i, 256:384], ident, C("swmask")[:, P:2 * P], ALU.mult).then_inc(sem["bias_zero"], 1)
                pool.wait_ge(sem["rpb_in"], l * INCS["rpb_in"] + 16 * 48)

                def bias_of(n):
                    kind, h, j = ATT[n]
                    if kind == "na":
                        if n >= 2:
                            pool.wait_ge(sem["att_m"], l * INCS["att_m"] + n - 1)
                        x0 = min(max(16 * j - 8, 0), 32) - 16 * j + 16
                        table = rpb[:, h, :].rearrange("p (r x) -> p r x", x=64)[:, ::-1, ::-1][:, :, x0:x0 + 32]
                        nc.gpsimd.tensor_tensor(bias[:, n % 2, 0:256].rearrange("p (r c) -> p r c", c=32), table,
                                                namask[:, (0, 1, 1, 2)[j], :].rearrange("p (r c) -> p r c", c=32), ALU.add).then_inc(sem["att_bias"], 1)

                def normalize(n):
                    w = width(ATT[n])
                    pool.wait_ge(sem["att_r"], l * INCS["att_r"] + n + 1)
                    nc.gpsimd.tensor_tensor(Pb[:, n % 3, 0:w], Pb[:, n % 3, 0:w], stats[:, n % 4, 2:3].to_broadcast([P, w]), ALU.mult)\
                        .then_inc(sem["att_pn"], 1)

                bias_of(0)
                for n in range(len(ATT) + 1):
                    if n + 1 < len(ATT):
                        bias_of(n + 1)
                    if n >= 1:
                        normalize(n - 1)
                nc.gpsimd.tensor_tensor(dummy[:, 0:1], ident[:, 0:1], ident[:, 0:1], ALU.mult).then_inc(sem["layer_done"], 1)
                pool.wait_ge(sem["layer_done"], 4 * (l + 1))

        @block.scalar
        def _(act):
            A = nc.scalar.activation
            act.wait_ge(sem["boot"], 48)
            A(condE[:, :, :], condT[:, :, :], ACT.Exp, scale=-1.0).then_inc(sem["cond_e"], 1)
            with act.Fori(0, LAYERS) as l:

                def norm(first):
                    for k in range(KD):
                        if k >= 2:
                            act.wait_ge(sem["sq_used"], l * INCS["sq_used"] + first * KD + k - 1)
                        A(sq[:, k % 2, :], xT[:, k, :], ACT.Square).then_inc(sem["sq"], 1)
                    act.wait_ge(sem["sq_used"], l * INCS["sq_used"] + KD * (first + 1))
                    A(rst, bank(0, 2)[:, 0:TOK], ACT.Ln, scale=1.0 / D, bias=C("eps")[:, 0:1]).then_inc(sem["ms"], 1)
                    act.wait_ge(sem["ms"], l * INCS["ms"] + first + 1)
                    A(rst, rst, ACT.Exp, scale=-0.5).then_inc(sem["rst_s"], 1)
                    gain, shift = ((gain1, 0), (gain2, 24))[first]
                    if not first:
                        act.wait_ge(sem["h_part"], l * INCS["h_part"] + 1)
                        act.wait_ge(sem["ada"], l * INCS["ada"] + 1)
                        for j in range(ADA_FIRST // 2):
                            i = nc.scalar.copy(ada_rows[0][32 * j:32 * j + 2, :], bank(4)[32 * j:32 * j + 2, :])
                        i.then_inc(sem["ada_rows"], 1)
                        act.wait_ge(sem["gain1"], l * INCS["gain1"] + 1)
                    for k in range(KD):
                        act.wait_ge(sem["h_part"], l * INCS["h_part"] + first * KD + k + 1)
                        for cond, (lo, hi) in enumerate(SEGMENTS):
                            i = A(hT[:, k, lo:hi], hT[:, k, lo:hi], ACT.Identity, scale=gain[:, k, cond:cond + 1],
                                  bias=mod[:, shift + k, cond:cond + 1])
                        i.then_inc(sem["h_ready"], 1)

                norm(0)
                def own_share(q):
                    c = RW_CHUNKS[q]
                    act.wait_ge(sem["proj_done"], l * INCS["proj_done"] + q + 1)
                    A(rw_chunk(c), bank(2 * (q % 2), 2)[:, 0:TOK], ACT.Identity, scale=mu_c[:, c:c + 1]).then_inc(sem["shift_a"], 1)

                def sigmoids(first, end):
                    for g in range(first, end):
                        act.wait_ge(sem["lora_mm"], l * INCS["lora_mm"] + g + 1)
                        dst, bias = ((ldT, "w0"), (aT, "a0"))[g // 4]
                        i = g % 4
                        A(dst[:, i // 2, i % 2, :], bank(4 + 2 * (g % 2), 2)[:, 0:TOK], ACT.Sigmoid, bias=PV(bias, i)).then_inc(sem["rw_le"], 1)

                for q in range(4):
                    own_share(q)
                act.wait_ge(sem["shifted"], l * INCS["shifted"] + 3)
                A(lora[:, 0, :], lora[:, 0, :], ACT.Tanh).then_inc(sem["rw_lora"], 1)
                A(lora[:, 2, :], lora[:, 2, :], ACT.Sigmoid).then_inc(sem["rw_lora"], 1)
                own_share(4)
                sigmoids(0, 3)
                own_share(5)
                sigmoids(3, 6)
                own_share(6)
                sigmoids(6, 8)
                act.wait_ge(sem["rw_kk"], l * INCS["rw_kk"] + 2)
                for p in range(2):
                    A(scr[:, p, :], kkT[:, p, :], ACT.Square).then_inc(sem["rw_kk_sq"], 1)
                own_share(7)
                act.wait_ge(sem["rw_kk_m"], l * INCS["rw_kk_m"] + 2)
                A(scr[:, :, :], scr[:, :, :], ACT.Ln, scale=2.0 ** 20).then_inc(sem["rw_kk_s"], 1)
                act.wait_ge(sem["rw_kk_s"], l * INCS["rw_kk_s"] + 1)
                A(scr[:, :, :], scr[:, :, :], ACT.Exp, scale=-0.5).then_inc(sem["rw_kk_s"], 1)
                own_share(8)
                for b, n, step in RW_ORDER:
                    g = UNIT[b]
                    if step == "sums":
                        act.wait_ge(sem[f"rw_sums{b}"], l * INCS[f"rw_sums{b}"] + n + 1)
                        A(g.e12[:, n % 2, 0, :].unsqueeze(2), Wc[:, :, 63:64], ACT.Exp)
                        A(g.e12[:, n % 2, 1, :].unsqueeze(2), Wm[:, :, P - 1:P], ACT.Exp)
                        for dst, src, sign in (((eR, Wm, 1.0), (eB, Wm, -1.0), (eA, Ec, 1.0)) if b == 0 else
                                               ((eR, Ec, -1.0), (eB, Ec, 1.0), (eA, Wm, -1.0))):
                            i = A(dst[:, :, :], src[:, :, :], ACT.Exp, scale=sign)
                        i.then_inc(sem[f"rw_exp{b}"], 1)
                    elif step == "transpose":
                        if n:
                            m = 2 * (n - 1) + b
                            rows = slice(32 * (m % 4), 32 * (m % 4) + 2)
                            act.wait_ge(sem[f"rw_mod{b}"], l * INCS[f"rw_mod{b}"] + n)
                            nc.scalar.copy(ada_rows[m // 4][rows, :], g.bank(2)[rows, :]).then_inc(sem[f"rw_modc{b}"], 1)
                        act.wait_ge(sem[f"rw_tp{b}"], l * INCS[f"rw_tp{b}"] + n + 1)
                        nc.scalar.copy(g.BKt[:, :, :].rearrange("p a b -> p (a b)"), g.bank(0))
                        nc.scalar.copy(g.Vt, g.bank(1)[:, 0:2 * P]).then_inc(sem[f"rw_tpc{b}"], 1)
                    elif step[0] == "Y":
                        act.wait_ge(sem[f"rw_y{b}"], l * INCS[f"rw_y{b}"] + LEVELS * n + step[1] + 1)
                        nc.scalar.copy(g.Y[:, :, :].rearrange("p a b -> p (a b)"), g.bank(0)).then_inc(sem[f"rw_yc{b}"], 1)
                    elif step == "W":
                        act.wait_ge(sem[f"rw_w{b}"], l * INCS[f"rw_w{b}"] + n + 1)
                        for h in range(2):
                            i = nc.scalar.copy(g.W.rearrange("p (a b v) -> p a b v", a=2, b=2)[:, :, h, :],
                                               g.bank(1 + h)[:, 0:P].rearrange("p (a v) -> p a v", a=2))
                        i.then_inc(sem[f"rw_wc{b}"], 1)
                    elif step == "U":
                        act.wait_ge(sem[f"rw_u{b}"], l * INCS[f"rw_u{b}"] + n + 1)
                        nc.scalar.copy(g.U, g.bank(3)[:, 0:256]).then_inc(sem[f"rw_uc{b}"], 1)
                for p in range(2):
                    act.wait_ge(sem["rw_yc2"], l * INCS["rw_yc2"] + p + 1)
                    A(scr[:, p, :], yT[:, p, :], ACT.Square).then_inc(sem["rw_fsq"], 1)
                for p in range(2):
                    act.wait_ge(sem["rw_fm"], l * INCS["rw_fm"] + 3 + p)
                    A(scr[:, p, :], bank(4 + 2 * p, 2)[:, 0:TOK], ACT.Ln, scale=1.0 / HD, bias=C("eps")[:, 1:2]).then_inc(sem["rw_var"], 1)
                    act.wait_ge(sem["rw_var"], l * INCS["rw_var"] + p + 1)
                    A(scr[:, p, :], scr[:, p, :], ACT.Exp, scale=-0.5).then_inc(sem["rw_fs"], 1)
                act.wait_ge(sem["out_state"], l * INCS["out_state"] + 16)
                for c in range(10):
                    act.wait_ge(sem["qk_done"], l * INCS["qk_done"] + c + 1)
                    if c >= 2:
                        act.wait_ge(sem["qk_used"], l * INCS["qk_used"] + c - 1)
                    A(nrm[:, c % 2, :], bank(2 * (c % 3), 2)[:, 0:TOK], ACT.Square).then_inc(sem["nsq"], 1)
                    act.wait_ge(sem["qk_norm"], l * INCS["qk_norm"] + c + 1)
                    A(nrm[:, c % 2, :], bank(6, 2)[:, 0:TOK], ACT.Ln, scale=1.0 / HD, bias=C("eps")[:, 0:1]).then_inc(sem["qk_ms"], 1)
                    act.wait_ge(sem["qk_ms"], l * INCS["qk_ms"] + c + 1)
                    A(nrm[:, c % 2, :], nrm[:, c % 2, :], ACT.Exp, scale=-0.5).then_inc(sem["nsr"], 1)
                def exp(n):
                    w = width(ATT[n]) + (ATT[n][0] in ("sw", "csw"))
                    act.wait_ge(sem["att_m"], l * INCS["att_m"] + n + 1)
                    if n >= 3:
                        act.wait_ge(sem["att_t"], l * INCS["att_t"] + n - 2)
                    A(Pb[:, n % 3, 0:w], Ssb[:, n % 2, 0:w], ACT.Exp, scale=-1.0, bias=stats[:, n % 4, 0:1],
                      accum_out=stats[:, n % 4, 1:2]).then_inc(sem["att_p"], 1)

                def pt(n):
                    w = width(ATT[n])
                    act.wait_ge(sem["att_t"], l * INCS["att_t"] + n + 1)
                    if n >= 2:
                        act.wait_ge(sem["att_o"], l * INCS["att_o"] + n - 1)
                    nc.scalar.copy(PT[:, n % 2, 0:w], bank(2 + n % 2)[:, 0:w]).then_inc(sem["att_ptc"], 1)

                for n in range(len(ATT) + 2):
                    if n < len(ATT):
                        exp(n)
                    if n >= 2:
                        pt(n - 2)
                act.wait_ge(sem["out_done"], l * INCS["out_done"] + 2 * KD)
                norm(1)
                act.wait_ge(sem["r_sub"], l * INCS["r_sub"] + 1)
                A(aff[:, :, :], aff[:, :, :], ACT.Exp).then_inc(sem["r_exp"], 1)
                for q in range(2 * NT):
                    act.wait_ge(sem["h_tp"], l * INCS["h_tp"] + q + 1)
                    nc.scalar.copy(htok[:, q // 2, 512 * (q % 2):512 * (q % 2) + 512], bank(4 + q % 2)).then_inc(sem["h_tok"], 1)
                gat = bank(6, 2).rearrange("p (k s) -> p k s", k=KD)
                gac = bank(4)[:, 0:256].rearrange("p (k s) -> p k s", k=KD)

                def gathered_ctx(n, used):
                    act.wait_ge(sem["gather"], l * INCS["gather"] + n)
                    if used is not None:
                        act.wait_ge(sem["ring_used"], l * INCS["ring_used"] + MULTIPLIED + EXPERT_PIECES * used)
                    nc.scalar.copy(xe0[:, :, LCAP:CAP], gac[:, :, 0:CCAP])
                    nc.scalar.copy(xe1[:, :, 0:CCAP], gac[:, :, CCAP:2 * CCAP]).then_inc(sem["xe_ctx"], 1)

                def gathered_lat():
                    nc.scalar.copy(xe0[:, :, 0:LCAP], gat[:, :, 0:LCAP])
                    nc.scalar.copy(xe1[:, :, LCAP:P], gat[:, :, LCAP:P]).then_inc(sem["xe_in"], 1)

                def expert(e, odd):
                    m = P if odd else CAP
                    act.wait_ge(sem["ring_used"], l * INCS["ring_used"] + MULTIPLIED + EXPERT_PIECES * e)
                    A(sg[0:m, :], bank(0, 2)[0:m, :], ACT.Silu).then_inc(sem["m_silu"], 1)

                def hidden_T(e, odd):
                    m = P if odd else CAP
                    for half in range(2):
                        act.wait_ge(sem["he_tp"], l * INCS["he_tp"] + 2 * e + half + 1)
                        nc.scalar.copy(heT[:, 4 * half:4 * half + 4, 0:m], bank(half).rearrange("p (k s) -> p k s", k=4)[:, :, 0:m])\
                            .then_inc(sem["he_t"], 1)

                def result(e, odd):
                    act.wait_ge(sem["ring_used"], l * INCS["ring_used"] + RING + EXPERT_PIECES * (e + 1))
                    y = bank(4, 2)
                    if odd:
                        nc.scalar.copy(ye_lat[LCAP:P, :], y[LCAP:P, :])
                        nc.scalar.copy(ye_ctx[32:32 + CCAP, :], y[0:CCAP, :]).then_inc(sem["ye"], 1)
                    else:
                        nc.scalar.copy(ye_lat[0:LCAP, :], y[0:LCAP, :])
                        nc.scalar.copy(ye_ctx[0:CCAP, :], y[LCAP:CAP, :]).then_inc(sem["ye"], 1)

                act.wait_ge(sem["xe_zero"], l * INCS["xe_zero"] + 1)
                gathered_ctx(1, None)
                gathered_lat()
                with act.Fori(0, PAIRS - 1) as i:
                    expert(2 * i, False)
                    hidden_T(2 * i, False)
                    result(2 * i, False)
                    expert(2 * i + 1, True)
                    gathered_ctx(i + 2, 2 * i + 1)
                    hidden_T(2 * i + 1, True)
                    gathered_lat()
                    result(2 * i + 1, True)
                for e, odd in ((EXPERTS - 2, False), (EXPERTS - 1, True)):
                    expert(e, odd)
                    hidden_T(e, odd)
                    result(e, odd)
                nc.scalar.copy(dummy[:, 1:2], C("ones")[:, 0:1]).then_inc(sem["layer_done"], 1)
                act.wait_ge(sem["layer_done"], 4 * (l + 1))

        @block.tensor
        def _(pe):
            mm = nc.tensor.matmul

            pe.wait_ge(sem["boot"], 48)
            mm(psum[0:1, 3584:3586], ident[:, 0:1], ident[:, 0:2], start=True, stop=True).then_inc(sem["ring_free"], 2)
            with pe.Fori(0, LAYERS) as l:
                pe.wait_ge(sem["par_in"], l * INCS["par_in"] + 16)
                n = 0

                def arrived():
                    nonlocal n
                    pe.wait_ge(sem[f"stream{n % STREAM}"], l * INCS[f"stream{n % STREAM}"] + 16 * (n // STREAM + 1))
                    n += 1
                    return (n - 1) % STREAM

                def norm(first):
                    for k in range(KD):
                        pe.wait_ge(sem["sq"], l * INCS["sq"] + first * KD + k + 1)
                        for lo, hi in SEGMENTS:
                            last = mm(bank(0, 2)[:, lo:hi], ones, sq[:, k % 2, lo:hi], start=k == 0, stop=k == KD - 1)
                        last.then_inc(sem["sq_used"], 1)

                norm(0)
                pe.wait_ge(sem["silu"], 1)
                for i in range(ADA_FIRST):
                    pe.wait_ge(sem[f"ada{i % RING}"], l * INCS[f"ada{i % RING}"] + 16 * (i // RING + 1))
                    rows = slice(32 * (i // 2), 32 * (i // 2) + 2)
                    for k in range(KD):
                        last = mm(bank(4)[rows, PIECE * (i % 2):PIECE * (i % 2 + 1)], silu[:, k, :], ada_ring[:, i % RING, k, :],
                                  start=k == 0, stop=k == KD - 1)
                    last.then_inc(sem["ada_used"], 1)
                mm(psum[0:1, 3072:3074], ident[:, 0:1], ident[:, 0:2], start=True, stop=True).then_inc(sem["ada"], 1)
                pe.wait_ge(sem["ada_rows"], l * INCS["ada_rows"] + 1)
                for i in range(4):
                    last = nc.tensor.transpose(bank(5)[:, P * i:P * i + P], ada_rows[0][:, P * i:P * i + P], ident)
                last.then_inc(sem["ada"], 1)
                def low_rank(first, end):
                    for g in range(first, end):
                        d, p = g % 4 // 2, g % 2
                        w = PAR["w2" if g < 4 else "a2"][0] + p * P
                        if g >= 2:
                            pe.wait_ge(sem["rw_le"], l * INCS["rw_le"] + g - 1)
                        for lo, hi in SEGMENTS:
                            last = mm(bank(4 + 2 * (g % 2), 2)[:, lo:hi], par[HD * d:HD * d + HD, w:w + P],
                                      lora[HD * d:HD * d + HD, g // 4, lo:hi], start=True, stop=True)
                        last.then_inc(sem["lora_mm"], 1)

                for q in range(RWC):
                    if q % 2 == 0:
                        s = arrived()
                    if q >= 2:
                        pe.wait_ge(sem["shifted"], l * INCS["shifted"] + q - 1)
                    else:
                        pe.wait_ge(sem["ms"], l * INCS["ms"] + 1)
                    for lo, hi in SEGMENTS:
                        for k in range(KD):
                            if q == 0 and lo == 0:
                                pe.wait_ge(sem["h_ready"], l * INCS["h_ready"] + k + 1)
                            last = mm(bank(2 * (q % 2), 2)[:, lo:hi], stream[:, s, k, (q % 2) * P:(q % 2 + 1) * P], hT[:, k, lo:hi],
                                      start=k == 0, stop=k == KD - 1)
                            if q and q % 2 == 0 and lo == 0 and k == 0:
                                last.then_inc(sem["stream_used"], 1)
                    last.then_inc(sem["proj_done"], 1)
                    if q == 4:
                        pe.wait_ge(sem["rw_lora"], l * INCS["rw_lora"] + 1)
                        low_rank(0, 3)
                    elif q == 5:
                        low_rank(3, 6)
                    elif q == 6:
                        low_rank(6, 8)
                    elif q == 7:
                        for p in range(2):
                            pe.wait_ge(sem["rw_kk_sq"], l * INCS["rw_kk_sq"] + p + 1)
                            pe.wait_ge(sem["rw_le"], l * INCS["rw_le"] + 7 + p)
                            for lo, hi in SEGMENTS:
                                last = mm(bank(4 + 2 * p, 2)[:, lo:hi], bones, scr[:, p, lo:hi], start=True, stop=True)
                            last.then_inc(sem["kk_mm"], 1)
                pe.wait_ge(sem["rw_lora"], l * INCS["rw_lora"] + 2)
                for p in range(2):
                    w = PAR["lg2"][0] + p * P
                    pe.wait_ge(sem["rw_kk_m"], l * INCS["rw_kk_m"] + p + 1)
                    for lo, hi in SEGMENTS:
                        last = mm(bank(4 + 2 * p, 2)[:, lo:hi], par[:, w:w + P], lora[:, 2, lo:hi], start=True, stop=True)
                        if p == 0 and lo == 0:
                            last.then_inc(sem["stream_used"], 1)
                    last.then_inc(sem["lora_mm"], 1)
                slot = None

                def modulation_rows(b, n_, first, end):
                    nonlocal slot
                    if n_ == NT - 1:
                        return
                    at_ = 32 * ((2 * n_ + b) % 4)
                    for i in range(first, end):
                        k = i % KD
                        if k == 0:
                            slot = arrived()
                        last = mm(UNIT[b].bank(2)[at_:at_ + 2, PIECE * (i // KD):PIECE * (i // KD + 1)], silu[:, k, :], stream[:, slot, k, :],
                                  start=k == 0, stop=k == KD - 1)
                        if k == KD - 1:
                            last.then_inc(sem["stream_used"], 1)
                    if end == 2 * KD:
                        carrier(b).then_inc(sem[f"rw_mod{b}"], 1)

                def carrier(b):
                    return mm(UNIT[b].bank(1)[0:1, 0:2], ident[:, 0:1], ident[:, 0:2], start=True, stop=True)

                for b, n_, step in RW_ORDER:
                    g = UNIT[b]
                    if step == "transpose":
                        if n_:
                            pe.wait_ge(sem[f"rw_state{b}"], l * INCS[f"rw_state{b}"] + n_)
                        pe.wait_ge(sem[f"rw_in{b}"], l * INCS[f"rw_in{b}"] + n_ + 1)
                        for i in range(4):
                            nc.tensor.transpose(g.bank(0)[:, P * i:P * i + P], g.BK[:, i // 2, i % 2, :], ident)
                        for p in range(2):
                            last = nc.tensor.transpose(g.bank(1)[:, P * p:P * p + P], vT[:, p, P * RW_TILE[b][n_]:P * RW_TILE[b][n_] + P], ident)
                        last.then_inc(sem[f"rw_tp{b}"], 1)
                    elif step == "scores":
                        if n_:
                            pe.wait_ge(sem[f"rw_modc{b}"], l * INCS[f"rw_modc{b}"] + n_)
                        for h in range(4):
                            hb, p = HD * (h % 2), h // 2
                            if h >= 2:
                                pe.wait_ge(sem[f"rw_masked{b}"], l * INCS[f"rw_masked{b}"] + 4 * n_ + h - 1)
                            rhs = g.AR[hb:hb + HD, n_ % 2, p, :, :].rearrange("p a t -> p (a t)")
                            mm(g.bank(2 + h % 2)[:, 0:256], g.BK[hb:hb + HD, 0, p, :], rhs, start=True, stop=True)
                            mm(g.bank(2 + h % 2)[:, 256:512], g.BK[hb:hb + HD, 1, p, :], rhs, start=True, stop=True).then_inc(sem[f"rw_sc{b}"], 1)
                    elif step == "first":
                        pe.wait_ge(sem[f"rw_tpc{b}"], l * INCS[f"rw_tpc{b}"] + n_ + 1)
                        pe.wait_ge(sem[f"rw_dt{b}"], l * INCS[f"rw_dt{b}"] + n_ + 1)
                        for h in range(4):
                            last = nc.tensor.transpose(g.bank(0)[:, P * h:P * h + P], g.DD[:, h, 1, :], ident)
                        last.then_inc(sem[f"rw_d0{b}"], 1)
                    elif step[0] == "Y":
                        i = step[1]
                        pe.wait_ge(sem[f"rw_dd{b}"], l * INCS[f"rw_dd{b}"] + (LEVELS + 1) * n_ + i + 1)
                        pe.wait_ge(sem[f"rw_x{b}"], l * INCS[f"rw_x{b}"] + LEVELS * n_ + i + 1)
                        for h in range(4):
                            last = mm(g.bank(0)[:, P * h:P * h + P], g.X[:, h, :], g.DD[:, h, 0, :], start=True, stop=True)
                        last.then_inc(sem[f"rw_y{b}"], 1)
                    elif step[0] == "Z":
                        i = step[1]
                        pe.wait_ge(sem[f"rw_yc{b}"], l * INCS[f"rw_yc{b}"] + LEVELS * n_ + i + 1)
                        for h in range(4):
                            z = g.bank(1, 2)[:, 256 * h:256 * h + 256]
                            if i < LEVELS - 1:
                                mm(z[:, 0:P], g.DD[:, h, 1, :], g.Y[:, h, :], start=True, stop=True)
                            last = mm(z[:, P:2 * P], g.Y[:, h, :], g.DD[:, h, 1, :], start=True, stop=True)
                        last.then_inc(sem[f"rw_z{b}"], 1)
                    elif step == "W":
                        pe.wait_ge(sem[f"rw_dd{b}"], l * INCS[f"rw_dd{b}"] + (LEVELS + 1) * (n_ + 1))
                        pe.wait_ge(sem[f"rw_s0{b}"], l * INCS[f"rw_s0{b}"] + n_ + 1)
                        for h in range(4):
                            hb, p = HD * (h % 2), h // 2
                            o = g.bank(1 + h % 2)[:, HD * p:HD * p + HD]
                            mm(o, g.AR[hb:hb + HD, n_ % 2, p, 0, :], g.S0[hb:hb + HD, p, :], start=True, stop=False)
                            last = mm(o, g.SC[:, h, 2 * P:3 * P], g.Vt[:, HD * h:HD * h + HD], start=False, stop=True)
                        last.then_inc(sem[f"rw_w{b}"], 1)
                    elif step == "U":
                        pe.wait_ge(sem[f"rw_wc{b}"], l * INCS[f"rw_wc{b}"] + n_ + 1)
                        for h in range(4):
                            last = mm(g.bank(3)[:, HD * h:HD * h + HD], g.DD[:, h, 1, :], g.W[:, HD * h:HD * h + HD], start=True, stop=True)
                        last.then_inc(sem[f"rw_u{b}"], 1)
                        modulation_rows(b, n_, 0, 10)
                    elif step == "out":
                        pe.wait_ge(sem[f"rw_uc{b}"], l * INCS[f"rw_uc{b}"] + n_ + 1)
                        for h in range(4):
                            hb, p = HD * (h % 2), h // 2
                            o = g.bank(3)[hb:hb + HD, 256 + HD * p:256 + HD * p + HD]
                            mm(o, g.BKt[:, 0, HD * h:HD * h + HD], g.U[:, HD * h:HD * h + HD], start=True, stop=False)
                            mm(o, g.BKt[:, 1, HD * h:HD * h + HD], g.Vt[:, HD * h:HD * h + HD], start=False, stop=True)
                            o = g.bank(0)[hb:hb + HD, P * p:P * p + P]
                            mm(o, g.S0[hb:hb + HD, p, :], g.AR[hb:hb + HD, n_ % 2, p, 1, :], start=True, stop=False)
                            mm(o, g.U[:, HD * h:HD * h + HD], g.SC[:, h, P:2 * P], start=False, stop=False)
                            last = mm(o, g.Vt[:, HD * h:HD * h + HD], g.SC[:, h, 3 * P:4 * P], start=False, stop=True)
                        last.then_inc(sem[f"rw_os{b}"], 1)
                        modulation_rows(b, n_, 10, 2 * KD)
                def head_sums(src, b, name, v):
                    pe.wait_ge(sem[name], l * INCS[name] + v)
                    for lo, hi in SEGMENTS:
                        last = mm(bank(b, 2)[:, lo:hi], bones, src[:, lo:hi], start=True, stop=True)
                    last.then_inc(sem["rw_fm"], 1)

                pe.wait_ge(sem["rw_y_all"], l * INCS["rw_y_all"] + 1)
                for i in range(8):
                    last = nc.tensor.transpose(bank(0, 2)[:, P * i:P * i + P], ada_rows[i // 4][:, P * (i % 4):P * (i % 4) + P], ident)
                last.then_inc(sem["ada"], 1)
                slots_v = [arrived(), arrived()]

                def value_products(first, end):
                    for q in range(first, end):
                        j, i = divmod(q, NT)
                        if q >= 2:
                            pe.wait_ge(sem["v_done"], l * INCS["v_done"] + q - 1)
                        for k in range(KD):
                            last = mm(bank(2 + q % 2)[:, 0:PIECE], hT[:, k, i * P:(i + 1) * P], stream[:, slots_v[j], k, :],
                                      start=k == 0, stop=k == KD - 1)
                            if q == NT and k == 0:
                                last.then_inc(sem["stream_used"], 1)
                        last.then_inc(sem["v_mm"], 1)

                for p in range(2):
                    head_sums(yT[:, p, :], 4 + 2 * p, "rw_y_all", 1)
                value_products(0, 2)
                for p in range(2):
                    head_sums(scr[:, p, :], 4 + 2 * p, "rw_fsq", p + 1)
                value_products(2, 4)
                head_sums(kT[:, 0, :], 0, "rw_bonus", 1)
                pe.wait_ge(sem["rw_var"], l * INCS["rw_var"] + 1)
                head_sums(kT[:, 1, :], 4, "rw_bonus", 1)
                value_products(4, 2 * NT)
                c = 0

                def qk_norm(c):
                    pe.wait_ge(sem["nsq"], l * INCS["nsq"] + c + 1)
                    if c >= 1:
                        pe.wait_ge(sem["qk_ms"], l * INCS["qk_ms"] + c)
                    for lo, hi in SEGMENTS:
                        last = mm(bank(6, 2)[:, lo:hi], bones, nrm[:, c % 2, lo:hi], start=True, stop=True)
                        if c == 9 and lo == 0:
                            last.then_inc(sem["stream_used"], 1)
                    last.then_inc(sem["qk_norm"], 1)

                for i in range(5):
                    s = arrived()
                    for j in range(2):
                        if c >= 3:
                            pe.wait_ge(sem["qk_used"], l * INCS["qk_used"] + c - 2)
                        elif c == 0:
                            pe.wait_ge(sem["rw_final"], l * INCS["rw_final"] + 1)
                        elif c == 1:
                            pe.wait_ge(sem["v_done"], l * INCS["v_done"] + 10)
                        for lo, hi in SEGMENTS:
                            for k in range(KD):
                                last = mm(bank(2 * (c % 3), 2)[:, lo:hi], stream[:, s, k, j * P:(j + 1) * P], hT[:, k, lo:hi],
                                          start=k == 0, stop=k == KD - 1)
                                if j == 0 and lo == 0 and k == 0:
                                    last.then_inc(sem["stream_used"], 1)
                        last.then_inc(sem["qk_done"], 1)
                        if c >= 1:
                            qk_norm(c - 1)
                        c += 1
                qk_norm(9)
                pe.wait_ge(sem["qk_used"], l * INCS["qk_used"] + 10)
                for i in range(4):
                    dst = kc if i == 3 else qc[:, i, :]
                    mm(bank(i), C("rot"), dst[:, 0:LAT], start=True, stop=True).then_inc(sem["rope_mm"], 1)
                pe.wait_ge(sem["roped"], l * INCS["roped"] + 4)
                pe.wait_ge(sem["cache_in"], l * INCS["cache_in"] + 32)

                def scores(n):
                    kind, h, j = ATT[n]
                    o = bank(n % 2)
                    if n >= 2:
                        pe.wait_ge(sem["att_m"], l * INCS["att_m"] + n - 1)
                    if kind == "na":
                        hb, p = HD * (h % 2), h // 2
                        start = min(max(16 * j - 8, 0), 32)
                        q = qa[hb:hb + HD, p, P * j:P * j + P]
                        keys = ka[hb:hb + HD, p, 0:LAT].rearrange("p (r c) -> p r c", c=64)[:, :, start:start + 32]
                        mm(o[:, 0:256].rearrange("p (r c) -> p r c", c=32), q, keys, start=True, stop=True)
                        last = mm(o[:, 256:384], q, kcache[hb:hb + HD, p, :], start=True, stop=True)
                    elif kind == "cna":
                        hb, p = HD * (h % 2), h // 2
                        last = mm(o[:, 0:P], qa[hb:hb + HD, p, LAT:TOK], ka[hb:hb + HD, p, LAT:TOK], start=True, stop=True)
                    else:
                        g, i = h // 3, h % 3
                        hb = HD * g
                        if kind == "csw":
                            last = mm(o[:, 0:P], qc[hb:hb + HD, i, LAT:TOK], kc[hb:hb + HD, LAT:TOK], start=True, stop=True)
                        else:
                            q = qc[hb:hb + HD, i, P * j:P * j + P]
                            lo = max(j - 1, 0)
                            own = (j + 1 - lo) * P
                            mm(o[:, 0:own], q, kc[hb:hb + HD, lo * P:(j + 1) * P], start=True, stop=True)
                            last = mm(o[:, own:own + P], q, kcache[hb:hb + HD, 3, :], start=True, stop=True)
                            if j < 3:
                                last = mm(o[:, own + P:own + 2 * P], q, kc[hb:hb + HD, (j + 1) * P:(j + 2) * P], start=True, stop=True)
                    last.then_inc(sem["att_s"], 1)

                def values(n):
                    kind, h, j = ATT[n]
                    f = HD * h if kind in ("na", "cna") else 384 + HD * (h // 3)
                    if kind == "na":
                        return [vwin[:, 2 * j, f:f + HD], vwin[:, 2 * j + 1, f:f + HD], vcache[:, f:f + HD]]
                    if kind == "sw":
                        lo = max(j - 1, 0)
                        out = [vtok[:, b, f:f + HD] for b in range(lo, j + 1)] + [vcache[:, f:f + HD]]
                        return out + ([vtok[:, j + 1, f:f + HD]] if j < 3 else [])
                    return [vtok[:, 4, f:f + HD]]

                def probs_T(n):
                    pe.wait_ge(sem["att_pn"], l * INCS["att_pn"] + n + 1)
                    if n >= 2:
                        pe.wait_ge(sem["att_ptc"], l * INCS["att_ptc"] + n - 1)
                    for i in range(width(ATT[n]) // P):
                        last = nc.tensor.transpose(bank(2 + n % 2)[:, P * i:P * i + P], Pb[:, n % 3, P * i:P * i + P], ident)
                    last.then_inc(sem["att_t"], 1)

                def outputs(n):
                    kind, h, j = ATT[n]
                    hb = HD * (h % 2)
                    pe.wait_ge(sem["att_ptc"], l * INCS["att_ptc"] + n + 1)
                    if n >= 2:
                        pe.wait_ge(sem["att_oc"], l * INCS["att_oc"] + n - 1)
                    vs = values(n)
                    for i, v in enumerate(vs):
                        last = mm(bank(4 + n % 2)[hb:hb + HD, 0:P], v, PT[:, n % 2, P * i:P * i + P], start=i == 0, stop=i == len(vs) - 1)
                    last.then_inc(sem["att_o"], 1)

                for n_ in range(len(ATT) + 3):
                    if n_ < len(ATT):
                        scores(n_)
                    if 2 <= n_ < len(ATT) + 2:
                        probs_T(n_ - 2)
                    if n_ == 3:
                        pe.wait_ge(sem["vwin_in"], l * INCS["vwin_in"] + 16 * 32)
                    if n_ >= 3:
                        outputs(n_ - 3)
                pe.wait_ge(sem["att_oc"], l * INCS["att_oc"] + len(ATT))
                mm(psum[0:1, 3584:3586], ident[:, 0:1], ident[:, 0:2], start=True, stop=True).then_inc(sem["ring_used"], RING)
                c = 0
                for i in range(OUT_PIECES):
                    s = arrived()
                    for j in range(2):
                        if c >= 2:
                            pe.wait_ge(sem["out_done"], l * INCS["out_done"] + 2 * (c - 1))
                        for lo, hi in SEGMENTS:
                            for k in range(KD):
                                last = mm(bank(2 * (c % 2), 2)[:, lo:hi], stream[:, s, k, j * P:(j + 1) * P], mixT[:, k, lo:hi],
                                          start=k == 0, stop=k == KD - 1)
                        last.then_inc(sem["out_mm"], 1)
                        c += 1
                    mm(psum[0:1, 3584:3586], ident[:, 0:1], ident[:, 0:2], start=True, stop=True).then_inc(sem["stream_used"], 1)
                pe.wait_ge(sem["out_done"], l * INCS["out_done"] + 2 * KD)
                norm(1)
                router = par[:, PAR["router"][0]:PAR["router"][1]].rearrange("p (k e) -> p k e", k=KD)
                for i in range(NT):
                    for k in range(KD):
                        if i == 0:
                            pe.wait_ge(sem["h_ready"], l * INCS["h_ready"] + KD + k + 1)
                        last = mm(bank(2)[:, EXPERTS * i:EXPERTS * (i + 1)], hT[:, k, i * P:(i + 1) * P], router[:, k, :],
                                  start=k == 0, stop=k == KD - 1)
                last.then_inc(sem["router_mm"], 1)
                for q in range(2 * NT):
                    if q == 2:
                        pe.wait_ge(sem["aff_sp"], l * INCS["aff_sp"] + 1)
                        for i in range(4):
                            last = nc.tensor.transpose(bank(3)[0:32, P * i:P * i + P], aff_sp[:, i, :], ident)
                        last.then_inc(sem["aff_tp"], 1)
                    if q >= 2:
                        pe.wait_ge(sem["h_tok"], l * INCS["h_tok"] + q - 1)
                    for k in range(4):
                        last = nc.tensor.transpose(bank(4 + q % 2)[:, P * k:P * k + P], hT[:, 4 * (q % 2) + k, P * (q // 2):P * (q // 2) + P], ident)
                    last.then_inc(sem["h_tp"], 1)
                pe.wait_ge(sem["idx_top"], l * INCS["idx_top"] + 2)
                mm(bank(2)[0:1, 0:2], ident[:, 0:1], ident[:, 0:2], start=True, stop=True)
                for i in range(2):
                    nc.tensor.transpose(bank(3)[:, 32 * i:32 * i + 32], tops[0:32, i, :], ident[0:32, 0:32])
                    last = nc.tensor.transpose(bank(3)[0:48, 64 + 32 * i:96 + 32 * i], tops_ctx[0:32, i, :], ident[0:32, 0:32])
                last.then_inc(sem["slot_tp"], 1)
                pe.wait_ge(sem["h_tok"], l * INCS["h_tok"] + 10)
                gat = bank(6, 2).rearrange("p (k s) -> p k s", k=KD)
                gac = bank(4)[:, 0:256].rearrange("p (k s) -> p k s", k=KD)
                heT_ps = bank(0, 2).rearrange("p (k s) -> p k s", k=KD)

                def gather(n):
                    pe.wait_ge(sem["sel"], l * INCS["sel"] + n)
                    for k in range(KD):
                        for i in range(4):
                            mm(gat[:, k, :], htok[:, i, k * P:(k + 1) * P], sel_lat[:, i, :], start=i == 0, stop=i == 3)
                        last = mm(gac[:, k, :], htok[:, 4, k * P:(k + 1) * P], sel_ctx, start=True, stop=True)
                    last.then_inc(sem["gather"], 1)

                def gate_up(e, odd):
                    m, x = (P, xe1) if odd else (CAP, xe0)
                    for j in range(8):
                        pe.wait_ge(sem[f"ring{j % RING}"], l * INCS[f"ring{j % RING}"] + 32 * e + 16 * (j // RING + 1))
                        for kk in range(2):
                            k = 2 * (j // 2) + kk
                            for f in range(2):
                                last = mm(bank(2 * (j % 2) + f)[0:m, :], x[:, k, 0:m], ring[:, j % RING, kk, 512 * f:512 * f + 512],
                                          start=k == 0, stop=k == KD - 1)
                        last.then_inc(sem["ring_used"], 1)

                def hidden_T(e, odd):
                    m = P if odd else CAP
                    pe.wait_ge(sem["he"], l * INCS["he"] + e + 1)
                    for k in range(KD):
                        last = nc.tensor.transpose(heT_ps[:, k, 0:m], he[0:m, k * P:(k + 1) * P], ident[0:m, 0:m])
                        if k % 4 == 3:
                            last.then_inc(sem["he_tp"], 1)

                def down(e, odd):
                    m = P if odd else CAP
                    for j in range(8, EXPERT_PIECES):
                        if j % 2 == 0:
                            pe.wait_ge(sem["he_t"], l * INCS["he_t"] + 2 * e + (1 if j == 8 else 2))
                        pe.wait_ge(sem[f"ring{j % RING}"], l * INCS[f"ring{j % RING}"] + 32 * e + 16 * (j // RING + 1))
                        for kk in range(2):
                            k = 2 * (j - 8) + kk
                            for f in range(2):
                                last = mm(bank(4 + f)[0:m, :], heT[:, k, 0:m], ring[:, j % RING, kk, 512 * f:512 * f + 512],
                                          start=k == 0, stop=k == KD - 1)
                        last.then_inc(sem["ring_used"], 1)

                def scatter(n):
                    pe.wait_ge(sem["ye"], l * INCS["ye"] + 2 * n)
                    pe.wait_ge(sem["selT"], l * INCS["selT"] + n)
                    for k in range(KD):
                        b = (6, 4)[k % 2]
                        if k >= 2:
                            pe.wait_ge(sem["scattered"], l * INCS["scattered"] + KD * n - KD + k - 1)
                        mm(bank(b), ye_lat[:, k * P:(k + 1) * P], selT_lat, start=True, stop=True)
                        mm(bank(b + 1)[:, 0:CTX], ye_ctx[0:48, k * P:(k + 1) * P], selT_ctx[0:48, :], start=True, stop=True)\
                            .then_inc(sem["scatter"], 1)

                gather(1)
                pe.wait_ge(sem["xe_ctx"], l * INCS["xe_ctx"] + 1)
                pe.wait_ge(sem["xe_in"], l * INCS["xe_in"] + 1)
                gate_up(0, False)
                hidden_T(0, False)
                down(0, False)
                gate_up(1, True)
                pe.wait_ge(sem["ye"], l * INCS["ye"] + 1)
                gather(2)
                hidden_T(1, True)
                pe.wait_ge(sem["xe_ctx"], l * INCS["xe_ctx"] + 2)
                down(1, True)
                with pe.Fori(1, PAIRS - 1) as i:
                    pe.wait_ge(sem["xe_in"], l * INCS["xe_in"] + i + 1)
                    gate_up(2 * i, False)
                    scatter(i)
                    hidden_T(2 * i, False)
                    pe.wait_ge(sem["scattered"], l * INCS["scattered"] + KD * i)
                    down(2 * i, False)
                    gate_up(2 * i + 1, True)
                    pe.wait_ge(sem["ye"], l * INCS["ye"] + 2 * i + 1)
                    gather(i + 2)
                    hidden_T(2 * i + 1, True)
                    pe.wait_ge(sem["xe_ctx"], l * INCS["xe_ctx"] + i + 2)
                    down(2 * i + 1, True)
                pe.wait_ge(sem["xe_in"], l * INCS["xe_in"] + PAIRS)
                gate_up(EXPERTS - 2, False)
                scatter(PAIRS - 1)
                hidden_T(EXPERTS - 2, False)
                pe.wait_ge(sem["scattered"], l * INCS["scattered"] + KD * (PAIRS - 1))
                down(EXPERTS - 2, False)
                gate_up(EXPERTS - 1, True)
                hidden_T(EXPERTS - 1, True)
                down(EXPERTS - 1, True)
                mm(psum[0:1, 3584:3586], ident[:, 0:1], ident[:, 0:2], start=True, stop=True).then_inc(sem["ring_free"], 2)
                scatter(PAIRS)
                pe.wait_ge(sem["scattered"], l * INCS["scattered"] + KD * PAIRS)
                mm(psum[0:1, 3584:3586], ident[:, 0:1], ident[:, 0:2], start=True, stop=True).then_inc(sem["layer_done"], 1)
                pe.wait_ge(sem["layer_done"], 4 * (l + 1))

        @block.vector
        def _(dve):
            V = nc.vector
            dve.wait_ge(sem["boot"], 48)
            dve.wait_ge(sem["cond_e"], 1)
            V.tensor_scalar(condE[:, :, :], condE[:, :, :], 1.0, None, ALU.add).then_inc(sem["silu_step"], 1)
            dve.wait_ge(sem["silu_step"], 1)
            V.reciprocal(condE[:, :, :], condE[:, :, :]).then_inc(sem["silu_step"], 1)
            dve.wait_ge(sem["silu_step"], 2)
            V.tensor_tensor(silu[:, :, :], condT[:, :, :], condE[:, :, :], ALU.mult).then_inc(sem["silu"], 1)
            with dve.Fori(0, LAYERS) as l:

                count = dict.fromkeys(INCS, 0)

                def v(ins):
                    count["vec_step"] += 1
                    ins.then_inc(sem["vec_step"], 1)
                    dve.wait_ge(sem["vec_step"], l * INCS["vec_step"] + count["vec_step"])

                def out(name, ins):
                    count[name] += 1
                    ins.then_inc(sem[name], 1)
                    dve.wait_ge(sem[name], l * INCS[name] + count[name])

                dve.wait_ge(sem["par_in"], l * INCS["par_in"] + 16)
                v(V.tensor_tensor(mu_c, PV("mu0", 0, 9), PV("mu1", 0, 9), ALU.add))
                v(V.tensor_scalar(mu_c, mu_c, -1.0, 1.0, ALU.mult, ALU.add))
                v(V.tensor_scalar(one_ka, PV("k_a", 0, 2), -1.0, 1.0, ALU.mult, ALU.add))
                v(V.tensor_scalar(two_ka, one_ka, 2.0, None, ALU.mult))
                v(V.tensor_scalar(naq8, PV("na_q"), 0.125, None, ALU.mult))
                v(V.tensor_scalar(swq8, PV("sw_q"), 0.125, None, ALU.mult))
                v(V.tensor_scalar(neg_sink, PV("sink", 0, 6), -1.0, None, ALU.mult))
                def modulation(q, src):
                    v(V.tensor_tensor(mod[:, q:q + 16, :].rearrange("p (j i) c -> p j i c", j=4),
                                      src.rearrange("p (i j r) -> p j i r", i=4, j=4)[:, :, :, 0:2],
                                      PV("ada_b", q, 16).rearrange("p (j i) -> p j i", j=4).unsqueeze(3).to_broadcast([P, 4, 4, 2]), ALU.add))

                def gain(g, name, q):
                    v(V.scalar_tensor_tensor(g[:, :, :], mod[:, q:q + 8, :], 1.0, PV(name, 0, 8).unsqueeze(2).to_broadcast([P, 8, 2]),
                                             ALU.add, ALU.mult))

                def norm(first):
                    dve.wait_ge(sem["rst_s"], l * INCS["rst_s"] + first + 1)
                    for k in range(KD):
                        V.tensor_tensor(hT[:, k, :], xT[:, k, :], rst, ALU.mult).then_inc(sem["h_part"], 1)

                for rows in (*ada_rows, yT[:, :, :]):
                    v(V.memset(rows, 0.0))
                norm(0)
                dve.wait_ge(sem["ada"], l * INCS["ada"] + 2)
                modulation(0, bank(5))
                gain(gain1, "g1", 8)
                V.tensor_copy(small[:, 62:63], ident[:, 0:1]).then_inc(sem["gain1"], 1)
                v(V.memset(state[:, 1:4:2, :, :], 0.0))

                def shift(q):
                    dve.wait_ge(sem["shift_a"], l * INCS["shift_a"] + q + 1)
                    c = RW_CHUNKS[q]
                    dst = rw_chunk(c)
                    u = bank(2 * (q % 2), 2)
                    for n, (lo, hi) in enumerate(SEGMENTS):
                        v(V.scalar_tensor_tensor(dst[:, lo + 1:hi], u[:, lo:hi - 1], PV("mu0", c), dst[:, lo + 1:hi], ALU.mult, ALU.add))
                        ins = V.scalar_tensor_tensor(dst[:, lo:hi - 1], u[:, lo + 1:hi], PV("mu1", c), dst[:, lo:hi - 1], ALU.mult, ALU.add)
                        (out if n else lambda _, i: v(i))("shifted", ins)

                for q in range(5):
                    shift(q)
                for p in range(2):
                    out("rw_kk", V.tensor_scalar(kkT[:, p, :], kT[:, p, :], PV("k_k", p), None, ALU.mult))
                for q in range(5, 8):
                    shift(q)
                dve.wait_ge(sem["rw_le"], l * INCS["rw_le"] + 8)
                v(V.tensor_scalar(ldT[:, :, :, :], ldT[:, :, :, :], DECAY, None, ALU.mult))
                dve.wait_ge(sem["kk_mm"], l * INCS["kk_mm"] + 2)
                for p in range(2):
                    out("rw_kk_m", V.tensor_scalar(scr[:, p, :], bank(4 + 2 * p, 2)[:, 0:TOK], 1e-24, None, ALU.max))
                shift(8)
                dve.wait_ge(sem["rw_kk_s"], l * INCS["rw_kk_s"] + 2)
                v(V.scalar_tensor_tensor(kkT[:, :, :], kkT[:, :, :], 2.0 ** 10, scr[:, :, :], ALU.mult, ALU.mult))
                dve.wait_ge(sem["lora_mm"], l * INCS["lora_mm"] + 10)
                for b, n, step in RW_ORDER:
                    g, s = UNIT[b], RW_STATE[b][n]
                    T = slice(RW_TILE[b][n] * P, (RW_TILE[b][n] + 1) * P)
                    ends = lambda n: (g.e12[:, n % 2, b, :].unsqueeze(2).to_broadcast([P, 2, HD]), g.e12[:, n % 2, 1 - b, :].unsqueeze(2).to_broadcast([P, 2, HD]))

                    def incoming(n):
                        out(f"rw_s0{b}", V.tensor_tensor(g.S0[:, :, :], state[:, RW_STATE[b][n], :, :], ends(n)[0], ALU.mult))

                    if step == "sums":
                        if (b, n) == (1, 0):
                            for p in range(2):
                                v(V.tensor_copy(gT[:, p, :], bank(4 + 2 * p, 2)[:, 0:TOK]))
                        for p in range(2):
                            v(V.tensor_tensor_scan(Wc[:, p, :], ones, ldT[:, b, p, T], 0.0, ALU.mult, ALU.add))
                        v(V.tensor_tensor(Wm[:, :, :], Wc[:, :, :], Wc[:, :, 63:64].to_broadcast([P, 2, P]), ALU.subtract))
                        out(f"rw_sums{b}", V.tensor_tensor(Ec[:, :, :], Wm[:, :, :], ldT[:, b, :, T], ALU.subtract))
                    elif step == "products":
                        for p in range(2):
                            v(V.tensor_scalar(g.BK[:, 1, p, :], aT[:, b, p, T], PV("k_a", p), one_ka[:, p:p + 1], ALU.mult, ALU.add))
                        v(V.tensor_tensor(g.BK[:, 1, :, :], g.BK[:, 1, :, :], kT[:, :, T], ALU.mult))
                        v(V.tensor_tensor(g.BK[:, 0, :, :], kkT[:, :, T], aT[:, b, :, T], ALU.mult))
                    elif step == "factors":
                        dve.wait_ge(sem[f"rw_exp{b}"], l * INCS[f"rw_exp{b}"] + n + 1)
                        v(V.scalar_tensor_tensor(g.AR[:, n % 2, :, 0, :], kkT[:, :, T], -1.0, eA[:, :, :], ALU.mult, ALU.mult))
                        v(V.tensor_tensor(g.AR[:, n % 2, :, 1, :], rT[:, :, T], eR[:, :, :], ALU.mult))
                        v(V.tensor_tensor(g.BK[:, 0, :, :], g.BK[:, 0, :, :], eB[:, :, :], ALU.mult))
                        out(f"rw_in{b}", V.tensor_tensor(g.BK[:, 1, :, :], g.BK[:, 1, :, :], eB[:, :, :], ALU.mult))
                        if n == 0:
                            dve.wait_ge(sem["state_in"], l * INCS["state_in"] + 16)
                            incoming(0)
                    elif step == "scores":
                        for h in range(4):
                            dve.wait_ge(sem[f"rw_sc{b}"], l * INCS[f"rw_sc{b}"] + 4 * n + h + 1)
                            out(f"rw_masked{b}", V.tensor_tensor(g.SC[:, h, :], g.bank(2 + h % 2), scmask[:, b, :], ALU.mult))
                        v(V.tensor_tensor(g.DD[:, :, 1, :], g.SC[:, :, 0:P], lv[:, b, 0, :].unsqueeze(1).to_broadcast([P, 4, P]), ALU.mult))
                        out(f"rw_dt{b}", V.tensor_tensor(g.DD[:, :, 1, :], g.DD[:, :, 1, :], ident.unsqueeze(1).to_broadcast([P, 4, P]), ALU.add))
                    elif step == "first":
                        dve.wait_ge(sem[f"rw_d0{b}"], l * INCS[f"rw_d0{b}"] + n + 1)
                        out(f"rw_dd{b}", V.tensor_copy(g.DD[:, :, 0, :], g.bank(0).rearrange("p (h t) -> p h t", h=4)))
                    elif step[0] == "Z":
                        dve.wait_ge(sem[f"rw_z{b}"], l * INCS[f"rw_z{b}"] + LEVELS * n + step[1] + 1)
                        z = g.bank(1, 2).rearrange("p (h n) -> p h n", h=4)
                        flat = g.DD[:, :, :, :].rearrange("p h a t -> p h (a t)")
                        part = slice(0 if step[1] < LEVELS - 1 else P, 2 * P)
                        out(f"rw_dd{b}", V.tensor_tensor(flat[:, :, part], flat[:, :, part], z[:, :, part], ALU.add))
                    elif step == "out":
                        dve.wait_ge(sem[f"rw_os{b}"], l * INCS[f"rw_os{b}"] + n + 1)
                        v(V.tensor_tensor(yT[:, :, T], yT[:, :, T], g.bank(0)[:, 0:256].rearrange("p (a t) -> p a t", a=2), ALU.add))
                        v(V.tensor_tensor(Stmp[:, :, :], g.S0[:, :, :], g.bank(3)[:, 256:256 + P].rearrange("p (a t) -> p a t", a=2), ALU.add))
                        out(f"rw_state{b}", V.tensor_tensor(state[:, s, :, :], Stmp[:, :, :], ends(n)[1], ALU.mult))
                        if n + 1 < NT:
                            incoming(n + 1)
                V.tensor_copy(small[:, 60:61], ident[:, 0:1]).then_inc(sem["rw_y_all"], 1)
                for p in range(2):
                    dve.wait_ge(sem["rw_fm"], l * INCS["rw_fm"] + p + 1)
                    out("rw_yc2", V.scalar_tensor_tensor(yT[:, p, :], bank(4 + 2 * p, 2)[:, 0:TOK], -1.0 / HD, yT[:, p, :], ALU.mult, ALU.add))
                dve.wait_ge(sem["ada"], l * INCS["ada"] + 3)
                for i in range(2):
                    modulation(2 * ADA_FIRST + 16 * i, bank(i))
                gain(gain2, "g2", 32)

                def values_in(first, end):
                    for q in range(first, end):
                        j, i = divmod(q, NT)
                        dve.wait_ge(sem["v_mm"], l * INCS["v_mm"] + q + 1)
                        V.tensor_copy(vtok[:, i, PIECE * j:PIECE * (j + 1)], bank(2 + q % 2)[:, 0:PIECE]).then_inc(sem["v_done"], 1)

                values_in(0, 2)
                v(V.tensor_tensor(aT[:, 0, :, :], aT[:, 0, :, :], aT[:, 1, :, :], ALU.add))
                for p in range(2):
                    v(V.tensor_scalar(aT[:, 0, p, :], aT[:, 0, p, :], PV("k_a", p), two_ka[:, p:p + 1], ALU.mult, ALU.add))
                v(V.tensor_tensor(kT[:, :, :], kT[:, :, :], aT[:, 0, :, :], ALU.mult))
                v(V.tensor_tensor(kT[:, :, :], kT[:, :, :], rT[:, :, :], ALU.mult))
                v(V.tensor_scalar(kT[:, 0, :], kT[:, 0, :], PV("r_k", 0), None, ALU.mult))
                out("rw_bonus", V.tensor_scalar(kT[:, 1, :], kT[:, 1, :], PV("r_k", 1), None, ALU.mult))
                values_in(2, 4)
                dve.wait_ge(sem["rw_fs"], l * INCS["rw_fs"] + 2)
                v(V.tensor_tensor(yT[:, :, :], yT[:, :, :], scr[:, :, :], ALU.mult))
                for p in range(2):
                    v(V.tensor_scalar(yT[:, p, :], yT[:, p, :], PV("ln_g", p), PV("ln_b", p), ALU.mult, ALU.add))
                for p in range(2):
                    dve.wait_ge(sem["rw_fm"], l * INCS["rw_fm"] + 5 + p)
                    v(V.tensor_tensor(vT[:, p, :], vT[:, p, :], bank(4 * p, 2)[:, 0:TOK], ALU.mult))
                v(V.tensor_tensor(yT[:, :, :], yT[:, :, :], vT[:, :, :], ALU.add))
                out("rw_final", V.tensor_tensor(mixT[:, 3:5, :], yT[:, :, :], gT[:, :, :], ALU.mult))
                values_in(4, 2 * NT)
                for c in range(10):
                    x = bank(2 * (c % 3), 2)
                    r = nrm[:, c % 2, :]
                    dve.wait_ge(sem["nsr"], l * INCS["nsr"] + c + 1)
                    g = naq8 if c < 3 else PV("na_k") if c < 6 else swq8 if c < 9 else PV("sw_k")
                    if c < 3:
                        v(V.tensor_scalar(r, r, g, None, ALU.mult))
                        for j in range(4):
                            view = lambda t: t[:, 0:LAT].rearrange("p (r j c) -> p r j c", r=8, j=4)[:, :, j, :]
                            v(V.tensor_tensor(qa[:, c, P * j:P * j + P].rearrange("p (r c) -> p r c", r=8)[:, :, :],
                                              view(x), view(r), ALU.mult))
                        out("qk_used", V.tensor_tensor(qa[:, c, LAT:TOK], x[:, LAT:TOK], r[:, LAT:TOK], ALU.mult))
                    else:
                        dst = ka[:, c - 3, :] if c < 6 else qc[:, c - 6, :] if c < 9 else kc
                        out("qk_used", V.scalar_tensor_tensor(dst, x[:, 0:TOK], g, r, ALU.mult, ALU.mult))
                        if c < 6 or c == 9:
                            out("k_ctx", V.tensor_copy(small[:, 61:62], ident[:, 0:1]))
                for i in range(4):
                    dst = kc if i == 3 else qc[:, i, :]
                    dve.wait_ge(sem["rope_mm"], l * INCS["rope_mm"] + i + 1)
                    v(V.tensor_tensor(swap, bank(i), C("sin"), ALU.mult))
                    v(V.tensor_tensor(dst[:, 0:LAT], dst[:, 0:LAT], C("cos"), ALU.mult))
                    out("roped", V.tensor_tensor(dst[:, 0:LAT], dst[:, 0:LAT], swap, ALU.add))
                dve.wait_ge(sem["bias_zero"], l * INCS["bias_zero"] + 2)

                def negated(n):
                    kind, h, j = ATT[n]
                    w = width(ATT[n])
                    dve.wait_ge(sem["att_s"], l * INCS["att_s"] + n + 1)
                    if kind == "na":
                        dve.wait_ge(sem["att_bias"], l * INCS["att_bias"] + n + 1)
                        add = bias[:, n % 2, :]
                    elif kind == "sw":
                        add = C("swmask")[:, P:] if j == 0 else C("swmask")
                    else:
                        add = C("swmask")[:, P:2 * P]
                    if kind in ("sw", "csw"):
                        V.tensor_copy(Ssb[:, n % 2, w:w + 1], neg_sink[:, h:h + 1])
                    else:
                        V.tensor_copy(stats[:, n % 4, 3:4], ident[:, 0:1])
                    V.tensor_tensor_reduce(Ssb[:, n % 2, 0:w], bank(n % 2)[:, 0:w], add[:, 0:w], -1.0,
                                           neg_sink[:, h:h + 1] if kind in ("sw", "csw") else -NEG, ALU.add, ALU.min,
                                           stats[:, n % 4, 0:1]).then_inc(sem["att_m"], 1)

                def inverse_sum(n):
                    dve.wait_ge(sem["att_p"], l * INCS["att_p"] + n + 1)
                    V.reciprocal(stats[:, n % 4, 2:3], stats[:, n % 4, 1:2]).then_inc(sem["att_r"], 1)

                def merged(n):
                    kind, h, j = ATT[n]
                    hb = HD * (h % 2)
                    dve.wait_ge(sem["att_o"], l * INCS["att_o"] + n + 1)
                    src = bank(4 + n % 2)[hb:hb + HD, 0:P]
                    chunk = h // 2 + (0 if kind in ("na", "cna") else 5)
                    if kind == "na":
                        dst = mixT[hb:hb + HD, chunk, 0:LAT].rearrange("p (r j c) -> p r j c", r=8, j=4)[:, :, j, :]
                        src = src.rearrange("p (r c) -> p r c", r=8)
                    elif kind == "sw":
                        dst = mixT[hb:hb + HD, chunk, P * j:P * j + P]
                    else:
                        dst = mixT[hb:hb + HD, chunk, LAT:TOK]
                    V.tensor_copy(dst, src).then_inc(sem["att_oc"], 1)

                for n in range(len(ATT) + 3):
                    if n < len(ATT):
                        negated(n)
                    if 1 <= n <= len(ATT):
                        inverse_sum(n - 1)
                    if n >= 3:
                        merged(n - 3)
                for c in range(KD):
                    dve.wait_ge(sem["out_mm"], l * INCS["out_mm"] + c + 1)
                    for cond, (lo, hi) in enumerate(SEGMENTS):
                        V.scalar_tensor_tensor(xT[:, c, lo:hi], bank(2 * (c % 2), 2)[:, lo:hi], mod[:, 16 + c, cond:cond + 1],
                                                                  xT[:, c, lo:hi], ALU.mult, ALU.add).then_inc(sem["out_done"], 1)
                dve.wait_ge(sem["out_done"], l * INCS["out_done"] + 2 * KD)
                norm(1)
                dve.wait_ge(sem["router_mm"], l * INCS["router_mm"] + 1)
                r = bank(2)[:, 0:NT * EXPERTS].rearrange("p (i e) -> p i e", i=NT)
                v(V.tensor_reduce(amx[:, :, 0:1], r, AX, ALU.max))
                out("r_sub", V.tensor_tensor(aff[:, :, :], r, amx[:, :, 0:1].to_broadcast([P, NT, EXPERTS]), ALU.subtract))
                dve.wait_ge(sem["r_exp"], l * INCS["r_exp"] + 1)
                v(V.tensor_reduce(amx[:, :, 1:2], aff[:, :, :], AX, ALU.add))
                v(V.reciprocal(amx[:, :, 0:1], amx[:, :, 1:2]))
                v(V.memset(aff_sp[:, :, :], -1.0))
                v(V.tensor_tensor(aff_sp[:, 0:4, 0:EXPERTS], aff[:, 0:4, :], amx[:, 0:4, 0:1].to_broadcast([P, 4, EXPERTS]), ALU.mult))
                out("aff_sp", V.tensor_tensor(aff_sp[:, 0, EXPERTS:32], aff[:, 4, :], amx[:, 4, 0:1].to_broadcast([P, EXPERTS]), ALU.mult))
                dve.wait_ge(sem["aff_tp"], l * INCS["aff_tp"] + 1)
                v(V.tensor_copy(affT[0:32, :], bank(3)[0:32, :]))
                for i in range(LCAP // 8):
                    t8, i8 = vals[0:32, 8 * i:8 * i + 8], idx_u[0:32, 8 * i:8 * i + 8].bitcast(U32)
                    for find in (lambda: V.max(t8, affT[0:32, :]), lambda: V.max_index(i8, t8, affT[0:32, :]),
                                 lambda: V.match_replace(affT[0:32, :], t8, affT[0:32, :], -2.0)):
                        V.tensor_copy(dummy[:, 3:4], ident[:, 0:1])
                        v(find())
                v(V.memset(tops_ctx[0:32, :, :], 0.0))
                for half in range(2):
                    v(V.tensor_copy(tops[0:32, 0, LCAP * half:LCAP * (half + 1)], idx_u[0:32, :].bitcast(U32)))
                    v(V.tensor_copy(tops[0:32, 1, LCAP * half:LCAP * (half + 1)], vals[0:32, :]))
                for half in range(2):
                    v(V.tensor_scalar(tops_ctx[0:32, 0, 32 * half:32 * half + CCAP], tops[0:32, 0, 0:CCAP], float(LAT), None, ALU.add))
                    out("idx_top", V.tensor_copy(tops_ctx[0:32, 1, 32 * half:32 * half + CCAP], vals[0:32, 0:CCAP]))
                dve.wait_ge(sem["slot_tp"], l * INCS["slot_tp"] + 1)
                st = bank(3)[:, 0:64].rearrange("p (a r) -> p a r", a=2)
                sc = bank(3)[:, 64:128].rearrange("p (a r) -> p a r", a=2)
                for a, (lat, ctx_) in enumerate(((id_lat, id_ctx), (gate_lat, gate_ctx))):
                    v(V.tensor_copy(lat[0:LCAP, :], st[0:LCAP, a, 0:EXPERTS:2]))
                    v(V.tensor_copy(lat[LCAP:P, :], st[LCAP:P, a, 1:EXPERTS:2]))
                    v(V.tensor_copy(ctx_[0:32, :], sc[0:32, a, EXPERTS:2 * EXPERTS:2]))
                    v(V.tensor_copy(ctx_[32:48, :], sc[32:48, a, EXPERTS + 1:2 * EXPERTS:2]))
                v(V.memset(ye_ctx[0:48, :], 0.0))
                out("xe_zero", V.memset(xe1[:, :, :], 0.0))
                dve.wait_ge(sem["idx_in"], l * INCS["idx_in"] + 32)

                def select(n, first=False):
                    if not first:
                        dve.wait_ge(sem["gather"], l * INCS["gather"] + n)
                    for t in range(4):
                        V.tensor_scalar(sel_lat[:, t, :], idx_lat[:, n, :], C("tokid")[:, t:t + 1], None, ALU.is_equal)
                    V.tensor_scalar(sel_ctx, idx_ctx[:, n, :], C("tokid")[:, 0:1], None, ALU.is_equal).then_inc(sem["sel"], 1)

                def select_T(n):
                    V.tensor_scalar(selT_lat, C("iota")[:, 0:LAT], id_lat[:, bass.ds(n, 1)],
                                    gate_lat[:, bass.ds(n, 1)], ALU.is_equal, ALU.mult)
                    V.tensor_scalar(selT_ctx[0:48, :], C("iota")[0:48, LAT:TOK], id_ctx[0:48, bass.ds(n, 1)],
                                    gate_ctx[0:48, bass.ds(n, 1)], ALU.is_equal, ALU.mult).then_inc(sem["selT"], 1)

                def hidden(e, odd):
                    m = P if odd else CAP
                    dve.wait_ge(sem["m_silu"], l * INCS["m_silu"] + e + 1)
                    V.tensor_tensor(he[0:m, :], sg[0:m, :], bank(2, 2)[0:m, :], ALU.mult).then_inc(sem["he"], 1)

                def accumulate(n):
                    for k in range(KD):
                        dve.wait_ge(sem["scatter"], l * INCS["scatter"] + KD * n - KD + k + 1)
                        b = (6, 4)[k % 2]
                        V.scalar_tensor_tensor(xT[:, k, 0:LAT], bank(b), mod[:, 40 + k, 0:1], xT[:, k, 0:LAT], ALU.mult, ALU.add)
                        V.scalar_tensor_tensor(xT[:, k, LAT:TOK], bank(b + 1)[:, 0:CTX], mod[:, 40 + k, 1:2], xT[:, k, LAT:TOK],
                                               ALU.mult, ALU.add).then_inc(sem["scattered"], 1)
                    dve.wait_ge(sem["scattered"], l * INCS["scattered"] + KD * n)

                select(0, True)
                select_T(0)
                hidden(0, False)
                select(1)
                hidden(1, True)
                with dve.Fori(1, PAIRS - 1) as i:
                    hidden(2 * i, False)
                    accumulate(i)
                    select_T(i)
                    select(i + 1)
                    hidden(2 * i + 1, True)
                hidden(EXPERTS - 2, False)
                accumulate(PAIRS - 1)
                select_T(PAIRS - 1)
                hidden(EXPERTS - 1, True)
                accumulate(PAIRS)
                assert count["vec_step"] == INCS["vec_step"], count["vec_step"]
                V.memset(dummy[:, 2:3], 0.0).then_inc(sem["layer_done"], 1)
                dve.wait_ge(sem["layer_done"], 4 * (l + 1))



def _layout(x):
    c = np.ascontiguousarray
    L = LAYERS

    def chunks(a):
        return a.reshape(L, -1, P).transpose(0, 2, 1)

    tokens = np.concatenate([x["x_sample"][0], x["x_prompt"][0]], 0)
    out = {"cst": _constants(), "xT": c(tokens.reshape(TOK, KD, P).transpose(2, 1, 0))}
    out["cond"] = c(np.stack([x["c"][0], x["c_ctx"]], 0).reshape(2, KD, P).transpose(2, 1, 0))
    par = np.zeros((L, P, PAR_N), np.float32)

    def put(name, a):
        lo, hi = PAR[name]
        par[:, :, lo:hi] = a.reshape(L, P, hi - lo)

    put("ada_b", chunks(x["ada_b"]))
    put("g1", chunks(x["norm1_g"]))
    put("g2", chunks(x["norm2_g"]))
    for name, key in (("na_q", "na_q_norm"), ("na_k", "na_k_norm"), ("sw_q", "swa_q_norm"), ("sw_k", "swa_k_norm")):
        put(name, np.concatenate([x[key], x[key]], 1))
    put("mu0", chunks(x["rw_mu"][:, 0]))
    put("mu1", chunks(x["rw_mu"][:, 1]))
    put("w0", chunks(x["rw_w0"].reshape(L, 512)))
    put("a0", chunks(x["rw_a0"].reshape(L, 512)))
    for name, key in (("k_k", "rw_k_k"), ("k_a", "rw_k_a"), ("r_k", "rw_r_k"), ("ln_g", "rw_ln_g"), ("ln_b", "rw_ln_b")):
        put(name, chunks(x[key].reshape(L, 256)))
    put("sink", np.broadcast_to(x["swa_sink"][:, None, :], (L, P, 6)))
    put("w2", x["rw_w2"].reshape(L, P, 256))
    put("a2", x["rw_a2"].reshape(L, P, 256))
    put("lg2", x["rw_g2"])
    put("router", x["w_router"].reshape(L, KD, P, EXPERTS).transpose(0, 2, 1, 3))
    out["par"] = par
    w = x["w_in"]
    q_order = [h for i in range(3) for h in (i, i + 3)]
    qc = w[:, :, 2304:2688].reshape(L, D, 6, HD)[:, :, q_order].reshape(L, D, 384)
    def pieces(a, n):
        return c(a.reshape(L, KD, P, n, PIECE).transpose(0, 3, 2, 1, 4))

    w_in = np.concatenate([w[:, :, 0:768], qc, w[:, :, 2688:2816], w[:, :, 768:1152], w[:, :, 2816:2944],
                           w[:, :, 1152:2304].reshape(L, D, RWC, P)[:, :, list(RW_CHUNKS)].reshape(L, D, RWC * P),
                           np.zeros((L, D, P), np.float32)], 2)
    out["w_in"] = pieces(w_in, W_IN_PIECES)
    out["ada_w"], out["w_out"] = pieces(x["ada_w"], ADA_PIECES), pieces(x["w_out"], OUT_PIECES)
    out["w_gate"], out["w_up"], out["w_down"] = c(x["w_gate"]), c(x["w_up"]), c(x["w_down"])
    table = np.zeros((L, 6, 16, 64), np.float32)
    table[:, :, 0:15, 16:47] = x["na_rpb"]
    out["rpb"] = c(table.reshape(L, 6, 1024)[:, :, ::-1])
    heads = np.concatenate([x["cache_na_k"][0], x["cache_swa_k"][0]], 1)
    out["kcache"] = c(heads.reshape(L, 4, 2, P, HD).transpose(0, 2, 4, 1, 3).reshape(L, P, 4, P))
    heads = np.concatenate([x["cache_na_v"][0], x["cache_swa_v"][0]], 1)
    out["vcache"] = c(heads.transpose(0, 2, 1, 3).reshape(L, P, 512))
    s = x["state_rwkv"][0].reshape(L, 2, 2, 2, HD, HD)
    out["state"] = c(s.transpose(0, 3, 5, 1, 2, 4).reshape(L, P, 2, 2, HD))
    return out


_OUTS = {"y": (P, KD, TOK), "nk": (LAYERS, P, 4, P), "nv": (LAYERS, P, 512), "ns": (LAYERS, P, 2, 2, HD),
         "vscr": (LAT, 384), "tops": (32, P)}


def _returned(r):
    L = LAYERS
    y = r["out_y"].transpose(2, 1, 0).reshape(TOK, D)
    k = r["out_nk"].reshape(L, 2, HD, 4, P).transpose(0, 3, 1, 4, 2).reshape(1, L, 8, P, HD)
    v = r["out_nv"].reshape(L, P, 8, HD).transpose(0, 2, 1, 3)[None]
    s = r["out_ns"].reshape(L, 2, HD, 2, 2, HD).transpose(0, 3, 4, 1, 5, 2).reshape(1, L, 2, 4, HD, HD)
    c = np.ascontiguousarray
    return c(y[None, LAT:]), c(y[None, :LAT]), c(k[:, :, 0:6]), c(v[:, :, 0:6]), c(k[:, :, 6:8]), c(v[:, :, 6:8]), c(s)


def kernel(**inputs):
    import concourse.bacc as bacc
    from concourse.bass_utils import run_bass_kernel_spmd as run
    arrays = _layout({k: np.asarray(v) for k, v in inputs.items()})
    nc = bacc.Bacc("TRN2", target_bir_lowering=False, num_devices=1)
    nc.disable_value_cache = True
    io = {n: nc.dram_tensor(f"in_{n}", a.shape, F32, kind="ExternalInput").ap() for n, a in arrays.items()}
    io.update({n: nc.dram_tensor(f"out_{n}", shape, F32, kind="ExternalOutput").ap() for n, shape in _OUTS.items()})
    program(nc, io)
    r = run(nc, [{f"in_{k}": v for k, v in arrays.items()}], core_ids=[0])
    return _returned(r.results[0])
```
